# Optimizing a Trainium2 kernel written in Bass

```python
import jax, jax.numpy as jnp
from jax import lax
import numpy as np

D_MODEL = 2048
BATCH = 1
SEQ = 256
DEPTH = 1

CHUNK = 64
N_MEM = 256
FOX_HEADS = 16
FOX_HEAD_DIM = 128
FOX_WIDTH = FOX_HEADS * FOX_HEAD_DIM
CONV_WIDTH = 2048
CONV_TAPS = 3
MEM_HEADS = 4
MEM_HEAD_DIM = 128
MEM_WIDTH = MEM_HEADS * MEM_HEAD_DIM
D_FF = 5632
Q_BLOCK = 128
N_BRANCH = 2
EPS = 1e-6
FORGET_BIAS_INIT = 3.0
W_IN_COLS = 3 * FOX_WIDTH + FOX_HEADS + 3 * CONV_WIDTH + N_BRANCH * D_MODEL

kernel_name = "hybrid_fox_shortconv_macaron_sandwich"

def rmsnorm(x, g):
    xf = x.astype(jnp.float32)
    xf = xf * lax.rsqrt(jnp.mean(xf * xf, axis=-1, keepdims=True) + EPS)
    return (xf * g.astype(jnp.float32)).astype(x.dtype)

def swiglu(u, w13, w2):
    gate, up = jnp.split(u @ w13, 2, axis=-1)
    return (jax.nn.silu(gate) * up) @ w2

def forgetting_attention(q, k, v, log_f):
    b, s, h, dh = q.shape
    nb = s // Q_BLOCK
    scale = dh ** -0.5
    c = jnp.cumsum(log_f, axis=1).transpose(0, 2, 1)
    kh = k.transpose(0, 2, 1, 3)
    vh = v.transpose(0, 2, 1, 3)
    q_blocks = q.transpose(0, 2, 1, 3).reshape(b, h, nb, Q_BLOCK, dh).transpose(2, 0, 1, 3, 4)
    cq_blocks = c.reshape(b, h, nb, Q_BLOCK).transpose(2, 0, 1, 3)
    kpos = jnp.arange(s)

    def one_block(args):
        qb, cqb, i = args
        qpos = i * Q_BLOCK + jnp.arange(Q_BLOCK)
        logits = jnp.einsum('bhqd,bhkd->bhqk', qb, kh,
                            preferred_element_type=jnp.float32) * scale
        logits = logits + (cqb[..., :, None] - c[:, :, None, :])
        logits = jnp.where(kpos[None, :] <= qpos[:, None], logits, -jnp.inf)
        p = jax.nn.softmax(logits, axis=-1)
        return jnp.einsum('bhqk,bhkd->bhqd', p.astype(vh.dtype), vh)

    out = lax.map(one_block, (q_blocks, cq_blocks, jnp.arange(nb)))
    return out.transpose(1, 0, 3, 2, 4).reshape(b, s, h * dh)

def short_conv(z, w, bias):
    s = z.shape[1]
    zp = jnp.pad(z, ((0, 0), (CONV_TAPS - 1, 0), (0, 0)))
    y = bias
    for tap in range(CONV_TAPS):
        y = y + w[tap] * zp[:, tap:tap + s]
    return y

def memory_attention(u, mem_n, w_mq, w_mkv, w_mo):
    b, s, _ = u.shape
    m = mem_n.shape[1]
    q = (u @ w_mq).reshape(b, s, MEM_HEADS, MEM_HEAD_DIM)
    k, v = jnp.split(mem_n @ w_mkv, 2, axis=-1)
    k = k.reshape(b, m, MEM_HEADS, MEM_HEAD_DIM)
    v = v.reshape(b, m, MEM_HEADS, MEM_HEAD_DIM)
    logits = jnp.einsum('bshd,bmhd->bhsm', q, k,
                        preferred_element_type=jnp.float32) * (MEM_HEAD_DIM ** -0.5)
    p = jax.nn.softmax(logits, axis=-1)
    o = jnp.einsum('bhsm,bmhd->bshd', p.astype(v.dtype), v).reshape(b, s, MEM_WIDTH)
    return o @ w_mo

def setup_inputs(seed: int = 0) -> dict:
    key = jax.random.key(seed)
    ks = jax.random.split(key, 32)
    f32 = jnp.float32

    def w(k, shape, fan_in):
        return jax.random.normal(k, shape, f32) * (fan_in ** -0.5)

    def gain(k, shape):
        return 1.0 + 0.05 * jax.random.normal(k, shape, f32)

    L, D = DEPTH, D_MODEL
    return {
        "x": jax.random.normal(ks[0], (BATCH, SEQ, D), f32),
        "mem": jax.random.normal(ks[1], (BATCH, N_MEM, D), f32),
        "ffn1_pre_g": gain(ks[2], (L, D)),
        "ffn1_w13": w(ks[3], (L, D, 2 * D_FF), D),
        "ffn1_w2": w(ks[4], (L, D_FF, D), D_FF),
        "ffn1_post_g": gain(ks[5], (L, D)),
        "mix_pre_g": gain(ks[6], (L, D)),
        "w_in": w(ks[7], (L, D, W_IN_COLS), D),
        "forget_bias": FORGET_BIAS_INIT + 0.1 * jax.random.normal(ks[8], (L, FOX_HEADS), f32),
        "gate_bias": 0.02 * jax.random.normal(ks[9], (L, N_BRANCH, D), f32),
        "conv_w": w(ks[10], (L, CONV_TAPS, CONV_WIDTH), CONV_TAPS),
        "conv_b": 0.02 * jax.random.normal(ks[11], (L, CONV_WIDTH), f32),
        "w_out": w(ks[12], (L, D, D), D),
        "mix_post_g": gain(ks[13], (L, D)),
        "mem_q_pre_g": gain(ks[14], (L, D)),
        "mem_kv_g": gain(ks[15], (L, D)),
        "w_mq": w(ks[16], (L, D, MEM_WIDTH), D),
        "w_mkv": w(ks[17], (L, D, 2 * MEM_WIDTH), D),
        "w_mo": w(ks[18], (L, MEM_WIDTH, D), MEM_WIDTH),
        "mem_post_g": gain(ks[19], (L, D)),
        "ffn2_pre_g": gain(ks[20], (L, D)),
        "ffn2_w13": w(ks[21], (L, D, 2 * D_FF), D),
        "ffn2_w2": w(ks[22], (L, D_FF, D), D_FF),
        "ffn2_post_g": gain(ks[23], (L, D)),
    }

def reference(x, mem, ffn1_pre_g, ffn1_w13, ffn1_w2, ffn1_post_g, mix_pre_g, w_in,
              forget_bias, gate_bias, conv_w, conv_b, w_out, mix_post_g, mem_q_pre_g,
              mem_kv_g, w_mq, w_mkv, w_mo, mem_post_g, ffn2_pre_g, ffn2_w13, ffn2_w2,
              ffn2_post_g):
    b, s, _ = x.shape
    split_at = list(np.cumsum([FOX_WIDTH, FOX_WIDTH, FOX_WIDTH, FOX_HEADS,
                               CONV_WIDTH, CONV_WIDTH, CONV_WIDTH, D_MODEL]))
    h = x
    for l in range(DEPTH):
        f = swiglu(rmsnorm(h, ffn1_pre_g[l]), ffn1_w13[l], ffn1_w2[l])
        h = h + 0.5 * rmsnorm(f, ffn1_post_g[l])

        u = rmsnorm(h, mix_pre_g[l])
        p = u @ w_in[l]
        q, k, v, f_logit, cx, cb, cc, ga, gb = jnp.split(p, split_at, axis=-1)
        log_f = jax.nn.log_sigmoid((f_logit + forget_bias[l]).astype(jnp.float32))
        y_attn = forgetting_attention(q.reshape(b, s, FOX_HEADS, FOX_HEAD_DIM),
                                      k.reshape(b, s, FOX_HEADS, FOX_HEAD_DIM),
                                      v.reshape(b, s, FOX_HEADS, FOX_HEAD_DIM), log_f)
        y_conv = cb * short_conv(cc * cx, conv_w[l], conv_b[l])
        merged = (jax.nn.sigmoid(ga + gate_bias[l, 0]) * y_attn
                  + jax.nn.sigmoid(gb + gate_bias[l, 1]) * y_conv)
        h = h + rmsnorm(merged @ w_out[l], mix_post_g[l])

        m_out = memory_attention(rmsnorm(h, mem_q_pre_g[l]), rmsnorm(mem, mem_kv_g[l]),
                                 w_mq[l], w_mkv[l], w_mo[l])
        h = h + rmsnorm(m_out, mem_post_g[l])

        f = swiglu(rmsnorm(h, ffn2_pre_g[l]), ffn2_w13[l], ffn2_w2[l])
        h = h + 0.5 * rmsnorm(f, ffn2_post_g[l])
    return h


_drawn_inputs = setup_inputs


def setup_inputs(seed=0):
    import zlib

    import numpy as np

    out = dict(_drawn_inputs(seed))
    spreads = {}
    factors = {'forget_bias': 42.408,
     'gate_bias': 8.0,
     'conv_b': 4.39,
     'ffn2_pre_g': 2.999,
     'ffn2_post_g': 4.321}
    for name, (base, spread) in spreads.items():
        noise = np.random.default_rng([zlib.crc32(name.encode()), seed]).standard_normal(out[name].shape)
        drawn = base * np.exp(spread * noise) if base else spread * noise
        out[name] = __import__('jax').numpy.asarray(drawn.astype(out[name].dtype))
    for name, factor in factors.items():
        out[name] = (out[name] * factor).astype(out[name].dtype)
    return out
```

```python
from contextlib import ExitStack

import concourse.bass as bass
from concourse import mybir


P = 128
T = 256
D = 2048
KD = D // P
DFF = 5632
KF = DFF // P
H = 16
MH = 4
SCALE = float(P) ** -0.5
EPS = 1e-6
NEG = -1e30

UK = 2
GT = 4
UW = UK * GT * P
RING = 4

F32 = mybir.dt.float32
F32R = mybir.dt.float32r
ALU = mybir.AluOpType
ACT = mybir.ActivationFunctionType
AX_X = mybir.AxisListType.X

G1 = DFF // 256
U1 = KD // UK
G2 = D // (GT * P)
U2 = KF // UK
PAIRS = H // 2
UM = 4 * U1
UO = MH // UK

F1A, F1A_G = 0, 0
F1B, F1B_G = F1A + G1 * U1, F1A_G + G1
MIX, MIX_G = F1B + G2 * U2, F1B_G + G2
MIX1, MIX1_G = MIX + UM + 2, MIX_G + 5
WO, WO_G = MIX1 + (PAIRS - 1) * UM, MIX1_G + (PAIRS - 1) * 4
MKV, MKV_G = WO + G2 * U1, WO_G + G2
MQ, MQ_G = MKV + 2 * U1, MKV_G + 2
MO, MO_G = MQ + U1, MQ_G + 1
F2A, F2A_G = MO + G2 * UO, MO_G + G2
F2B, F2B_G = F2A + G1 * U1, F2A_G + G1



def group_ends():
    ends, n = [], 0
    sizes = ([U1] * G1 + [U2] * G2 + [U1, U1, 2, U1, U1] + [U1] * 4 * (PAIRS - 1) + [U1] * G2
             + [U1] * 3 + [UO] * G2 + [U1] * G1 + [U2] * G2)
    for size in sizes:
        n += size
        ends.append(n)
    return ends


ENDS = group_ends()

N_F1, N_F1OUT, N_MIX, N_MIXOUT, N_MQ, N_MOUT, N_F2, N_F2OUT = range(8)
HP = KD // 2


def added(norm, kp):
    return norm * HP - norm // 2 * 2 + kp


(C_F1PRE, C_F1POST, C_MIXPRE, C_MIXPOST, C_MQPRE, C_MKV, C_MPOST, C_F2PRE,
 C_F2POST, C_GB, _C1, C_CW, _C2, _C3, C_CB) = range(0, 15 * KD, KD)
NPAR = 15 * KD
PAR_ROWS = (P, NPAR - P)

B_NORM, B_S, B_PT, B_Y = 4, 5, 6, 7
B_SCORE = (B_S, B_NORM)


class Chain:

    def __init__(self, eng, sem):
        self.eng, self.sem, self.n, self.loop = eng, sem, 0, None

    def step(self, ins):
        self.n += 1
        ins.then_inc(self.sem, 1)

    def settle(self):
        if self.loop is None:
            self.eng.wait_ge(self.sem, self.n)
        else:
            i, per = self.loop
            self.eng.wait_ge(self.sem, i * per + self.n)

    def enter(self, i, per):
        self.loop, self.start = (i, per), self.n

    def leave(self, times):
        per = self.loop[1]
        assert self.n - self.start == per, (self.sem, self.n - self.start)
        self.n, self.loop = self.start + per * times, None


def build(nc, a, out):
    with ExitStack() as ctx:
        def sem(name):
            return ctx.enter_context(nc.semaphore(name))

        at = [(nc.sbuf_base + 63) // 32 * 32]

        def place(name, shape, dt=F32, offset=None):
            size = 4
            for n in shape[1:]:
                size *= n
            size = (size + 31) // 32 * 32
            if offset is None:
                offset, at[0] = at[0], at[0] + size
            return nc.alloc_sbuf_tensor_at(name, shape, dt, offset=offset)

        h = place("h", [P, KD, T])
        xs_at = at[0]
        xs = place("xs", [P, KD, 2, T], F32R)
        f = place("f", [P, KD, T], offset=xs_at + KD * T * 4)
        raw = place("raw", [P, RING, UW])
        w_hi = place("w_hi", [P, RING, UW], F32R)
        w_lo = place("w_lo", [P, RING, UW], F32R)
        r_in = place("r_in", [P, T])
        r_out = place("r_out", [P, T])
        ms = place("ms", [P, 2])
        mhalf = place("mhalf", [P, 2])
        rtok = place("rtok", [P, 2])
        diag = place("diag", [P, 2, P])
        ident = place("ident", [P, P])
        tri1 = place("tri1", [P, T])
        ones = tri1[:, P:T]
        mask = place("mask", [P, P])
        par = place("par", [P, NPAR])
        prm = place("prm", [P, KD, 6])
        fbias = place("fbias", [H, 1])
        sq = place("sq", [P, 2, 2 * T])
        sqsum = place("sqsum", [P, 2 * T])
        gt = place("gt", [P, 2, T])
        up = place("up", [P, 2, T])
        arena = at[0]

        g = place("g", [P, KF, 2, T], F32R, arena)
        xr = place("xr", [P, 2, D], F32, arena)
        prow = place("prow", [P, 2, P], F32, arena + 2 * D * 4)
        mrg = place("mrg", [P, KD, 2, T], F32R, arena)
        at[0] = arena + KD * 2 * T * 4
        cross = at[0]
        qk = place("qk", [P, 4, T])
        vc = place("vc", [P, 4, T])
        bc = place("bc", [P, 4, T])
        zp = place("zp", [P, 2, T + 2])
        gat = place("gat", [P, 4, T])
        yc = place("yc", [P, 2, T])
        vtok = place("vtok", [P, 2, 2, P])
        lg = place("lg", [P, 2, 3 * P])
        pt = place("pt", [P, 2, 3 * P])
        ncr = place("ncr", [P, 2, T])
        ncm = place("ncm", [P, 2, 3 * P])
        mg = place("mg", [P, T])
        ctok = place("ctok", [P, 2, H])
        cq = place("cq", [P, 2, 2])
        prp = place("prp", [P, 2, 6])
        st = place("st", [P, 2, 6])
        ftok = place("ftok", [P, 2, H])
        memr_at = arena + KF * 2 * T * 4 - 2 * D * 4
        fz = place("fz", [H, 8, T], F32, memr_at)
        assert at[0] <= memr_at, (at[0], memr_at)
        memr = place("memr", [P, 2, D], F32, memr_at)
        mem = place("mem", [P, KD, 2, T], F32R, cross)
        junk = place("junk", [P, 2, D], F32, cross)
        assert cross + KD * 2 * T * 4 <= memr_at
        at[0] = arena
        kt = place("kt", [P, MH, T])
        vt = place("vt", [P, MH, T])
        qt = place("qt", [P, MH, T])
        mvtok = place("mvtok", [P, MH, 2, P])
        ml = place("ml", [P, MH, 2, T])
        mo = place("mo", [P, MH, T])
        assert at[0] <= cross
        mpt = place("mpt", [P, MH, 2, T], F32, memr_at)
        osp = place("osp", [P, MH, 2, T], F32R, memr_at + MH * 2 * T * 4)
        at[0] = arena + KF * 2 * T * 4
        mst = place("mst", [P, 8])
        mmx = place("mmx", [P, MH, 6])
        ot = place("ot", [P, 8, 512], F32, arena)
        assert at[0] <= nc.sbuf_usable_end, at[0]

        ps = ctx.enter_context(nc.psum_tensor("ps", [P, 8, 512], F32))
        crow = nc.dram_tensor("crow", [1, H, T], F32, kind="Internal").ap()

        x_landed = [sem(f"x_landed{i}") for i in range(4)]
        par_landed = sem("par_landed")
        mem_landed = sem("mem_landed")
        ident_set = sem("ident_set")
        consts_set = sem("consts_set")
        par_t = sem("par_t")
        par_ready = sem("par_ready")
        xt_full = sem("xt_full")
        landed = [sem(f"landed{i}") for i in range(RING)]
        hi_done = sem("hi_done")
        lo_done = sem("lo_done")
        w_used = sem("w_used")
        grp_out = sem("grp_out")
        h_ready = sem("h_ready")
        xhi_ready = sem("xhi_ready")
        x_ready = sem("x_ready")
        t_ready = sem("t_ready")
        sq_ready = sem("sq_ready")
        sq_added = sem("sq_added")
        sum_full = sem("sum_full")
        ms_ready = sem("ms_ready")
        r_ready = sem("r_ready")
        diag_ready = sem("diag_ready")
        r_full = sem("r_full")
        r_set = sem("r_set")
        gate_in = sem("gate_in")
        silu_done = sem("silu_done")
        g_ready = sem("g_ready")
        dve_own = sem("dve_own")
        pool_own = sem("pool_own")
        f_na = sem("f_na")
        f_e = sem("f_e")
        f_y = sem("f_y")
        f_ln = sem("f_ln")
        f_log = sem("f_log")
        f_tok = sem("f_tok")
        f_tokc = sem("f_tokc")
        f_cum = sem("f_cum")
        f_c = sem("f_c")
        crow_stored = sem("crow_stored")
        ncr_landed = sem("ncr_landed")
        prm_set = sem("prm_set")
        cq_set = sem("cq_set")
        ncm_done = sem("ncm_done")
        z_ready = sem("z_ready")
        taps_done = sem("taps_done")
        ycb_done = sem("ycb_done")
        gat_exp = sem("gat_exp")
        sig_ready = sem("sig_ready")
        ymix_ready = sem("ymix_ready")
        vt_full = sem("vt_full")
        vtok_ready = sem("vtok_ready")
        s_full = sem("s_full")
        l_ready = sem("l_ready")
        e_done = sem("e_done")
        p_ready = sem("p_ready")
        pt_full = sem("pt_full")
        pt_ready = sem("pt_ready")
        y_full = sem("y_full")
        y_out = sem("y_out")
        m_ready = sem("m_ready")
        msq_done = sem("msq_done")
        mm_ready = sem("mm_ready")
        mr_ready = sem("mr_ready")
        memn_ready = sem("memn_ready")
        memt_full = sem("memt_full")
        memhi_ready = sem("memhi_ready")
        mem_ready = sem("mem_ready")
        mvt_full = sem("mvt_full")
        mvtok_ready = sem("mvtok_ready")
        ms_full = sem("ms_full")
        mmax_ready = sem("mmax_ready")
        mexp_done = sem("mexp_done")
        mp_ready = sem("mp_ready")
        mpt_full = sem("mpt_full")
        mpt_ready = sem("mpt_ready")
        mo_full = sem("mo_full")
        os_ready = sem("os_ready")
        ot_full = sem("ot_full")
        ot_ready = sem("ot_ready")
        out_stored = sem("out_stored")

        def slot_of(n):
            return n % RING

        def of(n, per=0, i=None):
            return n if i is None else i * per + n

        block = ctx.enter_context(nc.Block())

        @block.sync
        def _(sp):
            xv = a["x"].rearrange("o (b p) (q n) -> p (o b) q n", p=P, q=4)
            for q in range(4):
                sp.dma_start(xr[:, :, q * 512:(q + 1) * 512], xv[:, :, q, :]).then_inc(x_landed[q], 16)

            def load(n0, src, per=0, i=None):
                n = n0
                if n >= RING:
                    sp.wait_ge(lo_done, of(n - RING + 1, per, i))
                s = slot_of(n)
                if len(src.shape) == 4:
                    dst = raw[:, s, :].rearrange("p (k s n) -> p k s n", k=src.shape[1], s=2)
                    halves = [(dst[:, :, b, :], src[:, :, b, :]) for b in range(2)]
                else:
                    dst = raw[:, s, :].rearrange("p (k n) -> p k n", k=src.shape[1])
                    mid = src.shape[1] // 2
                    halves = [(dst[:, :mid, :], src[:, :mid, :]), (dst[:, mid:, :], src[:, mid:, :])]
                for to, frm in halves:
                    sp.dma_start(to, frm).then_inc(landed[s], 16)

            def columns(w, u, c, width=GT * P):
                return w[:, UK * u:UK * u + UK, bass.ds(c, width)]

            def two_columns(w, u, c):
                return w[:, UK * u:UK * u + UK, :, bass.ds(c, 2 * P)]

            def ffn(w13, w2, n13, n2):
                w13 = w13.rearrange("o (k p) (s n) -> p (o k) s n", p=P, s=2)
                w2 = w2.rearrange("o (k p) n -> p (o k) n", p=P)
                for u in range(U1):
                    load(n13 + u, two_columns(w13, u, 0))
                with sp.Fori(0, G1 - 1) as i:
                    for u in range(U1):
                        load(n13 + U1 + u, two_columns(w13, u, i * 256 + 256), U1, i)
                with sp.Fori(0, G2 // 2) as i:
                    for m in range(2):
                        for u in range(U2):
                            load(n2 + m * U2 + u, columns(w2, u, i * 1024 + m * 512), 2 * U2, i)

            ffn(a["ffn1_w13"], a["ffn1_w2"], F1A, F1B)

            w_in = a["w_in"].rearrange("o (k p) n -> p (o k) n", p=P)
            cx = 3 * D + H
            kinds = [(0, D), (2 * D, cx - 2 * D), (cx + D, D), (cx + 3 * D, D)]
            views = [w_in[:, :, c:c + 2 * step].rearrange("p k (s n) -> p k s n", s=2) for c, step in kinds]
            for j in range(UM):
                if j == 2 * U1:
                    for u in range(2):
                        load(MIX + 2 * U1 + u, w_in[:, 8 * u:8 * u + 8, 3 * D:3 * D + P])
                load(MIX + j + (2 if j >= 2 * U1 else 0), two_columns(views[j // U1], j % U1, 0))
            with sp.Fori(0, PAIRS - 1) as i:
                for j in range(UM):
                    load(MIX1 + j, two_columns(views[j // U1], j % U1, i * 256 + 256), UM, i)

            sp.wait_ge(w_used, MIX1)
            sp.dma_start(memr[:, :, :], a["mem"].rearrange("o (b p) n -> p (o b) n", p=P)).then_inc(mem_landed, 16)

            w_out = a["w_out"].rearrange("o (k p) n -> p (o k) n", p=P)
            w_mkv = a["w_mkv"].rearrange("o (k p) n -> p (o k) n", p=P)
            w_mq = a["w_mq"].rearrange("o (k p) n -> p (o k) n", p=P)
            w_mo = a["w_mo"].rearrange("o (k p) n -> p (o k) n", p=P)
            with sp.Fori(0, G2) as i:
                for u in range(U1):
                    load(WO + u, columns(w_out, u, i * 512), U1, i)
            with sp.Fori(0, 2) as i:
                for u in range(U1):
                    load(MKV + u, columns(w_mkv, u, i * 512), U1, i)
            for u in range(U1):
                load(MQ + u, columns(w_mq, u, 0))
            for u in range(G2 * UO):
                load(MO + u, columns(w_mo, u % UO, u // UO * 512))

            ffn(a["ffn2_w13"], a["ffn2_w2"], F2A, F2B)
            sp.wait_ge(out_stored, 8 * 16)

        @block.scalar
        def _(act):
            rows = [(n, "o (k p) -> (o k) p") for n in (
                "ffn1_pre_g", "ffn1_post_g", "mix_pre_g", "mix_post_g", "mem_q_pre_g", "mem_kv_g",
                "mem_post_g", "ffn2_pre_g", "ffn2_post_g")]
            rows += [("gate_bias", "o b (k p) -> (o b k) p"), ("conv_w", "o b (k p) -> (o b k) p"),
                     ("conv_b", "o (k p) -> (o k) p")]
            r = 0
            for name, how in rows:
                src = a[name].rearrange(how, p=P)
                n = src.shape[0]
                act.dma_start(prow[r % P:r % P + n, r // P, :], src).then_inc(par_landed, 16)
                r += n
            act.dma_start(fbias[:, :], a["forget_bias"].rearrange("o h -> h o")).then_inc(par_landed, 16)

            def unit(n0, per=0, i=None):
                s = slot_of(n0)
                act.wait_ge(landed[s], of(32 * (n0 // RING + 1), 32 * (per // RING), i))
                if n0 >= RING:
                    act.wait_ge(w_used, of(n0 - RING + 1, per, i))
                nc.scalar.copy(w_hi[:, s, :], raw[:, s, :]).then_inc(hi_done, 1)

            def units(n0, count):
                loops = count // RING
                if loops > 1:
                    with act.Fori(0, loops) as i:
                        for j in range(RING):
                            unit(n0 + j, RING, i)
                else:
                    loops = 0
                for j in range(loops * RING, count):
                    unit(n0 + j)

            def square_pair(norm, kp, src):
                c = norm * HP + kp
                if kp >= 2:
                    act.wait_ge(sq_added, added(norm, kp - 1))
                elif norm > 0:
                    act.wait_ge(sum_full, norm)
                nc.scalar.activation(sq[:, c % 2, :], src.rearrange("p k t -> p (k t)"), ACT.Square).then_inc(sq_ready, 1)

            def input_pair(base, norm, gain, kp):
                act.wait_ge(h_ready, base + kp + 1)
                for k in (2 * kp, 2 * kp + 1):
                    ins = nc.scalar.activation(xs[:, k, 0, :], h[:, k, :], ACT.Copy, scale=par[:, gain + k:gain + k + 1])
                ins.then_inc(xhi_ready, 1)
                square_pair(norm, kp, h[:, 2 * kp:2 * kp + 2, :])

            def input_and_units(base, norm, gain, n0):
                for kp in range(HP):
                    if kp >= RING:
                        unit(n0 + kp)
                    input_pair(base, norm, gain, kp)

            def branch_out(norm, grp, m):
                act.wait_ge(grp_out, grp + 1)
                for c in range(2):
                    square_pair(norm, 2 * m + c, f[:, 4 * m + 2 * c:4 * m + 2 * c + 2, :])

            def silu(ffn, grp0, per=0, i=None):
                n = ffn * G1 + grp0
                act.wait_ge(gate_in, of(n + 1, per, i))
                nc.scalar.activation(gt[:, :, :], gt[:, :, :], ACT.Silu).then_inc(silu_done, 1)

            def ffn(k, base, norm, gain, n13, n2, grp2):
                input_and_units(base, norm, gain, n13)
                for grp in range(1, 2):
                    for u in range(U1):
                        unit(n13 + U1 * grp + u)
                        if u == RING - 1:
                            silu(k, grp - 1)
                with act.Fori(0, G1 - 2) as i:
                    for u in range(U1):
                        unit(n13 + 2 * U1 + u, U1, i)
                        if u == RING - 1:
                            silu(k, 1, 1, i)
                for u in range(RING):
                    unit(n2 + u)
                silu(k, G1 - 1)
                for m in range(G2):
                    units(n2 + m * U2 + RING, U2 if m < G2 - 1 else U2 - RING)
                    if m < G2 - 1:
                        branch_out(norm + 1, grp2 + m, m)

            units(0, RING)
            act.wait_ge(par_ready, 1)
            ffn(0, 0, N_F1, C_F1PRE, F1A, F1B, F1B_G)

            for u in range(RING):
                unit(MIX + u)
            branch_out(N_F1OUT, MIX_G - 1, G2 - 1)

            def pair_starts(p):
                act.wait_ge(ncm_done, p + 1)
                nc.scalar.copy(cq[:, :, :], ctok[:, :, bass.ds(p * 2, 2)]).then_inc(cq_set, 1)
                act.dma_start(ncr[:, :, :], crow[:, bass.ds(p * 2, 2), :].broadcast_to([P, 2, T])).then_inc(ncr_landed, 16)

            def gates(p):
                act.wait_ge(grp_out, p * 4 + MIX1_G)
                act.wait_ge(prm_set, p + 1)
                for t in range(4):
                    ins = nc.scalar.activation(gat[:, t, :], gat[:, t, :], ACT.Exp,
                                               bias=prp[:, t % 2, 4 + t // 2:5 + t // 2], scale=-1.0)
                ins.then_inc(gat_exp, 1)

            def head_exp(p, hd):
                act.wait_ge(l_ready, p * 2 + hd + 1)
                nc.scalar.activation(lg[:, hd, 0:P], lg[:, hd, 0:P], ACT.Exp,
                                     bias=st[:, hd, 0:1], accum_out=st[:, hd, 2:3])
                nc.scalar.activation(lg[:, hd, P:3 * P], lg[:, hd, P:3 * P], ACT.Exp,
                                     bias=st[:, hd, 1:2], accum_out=st[:, hd, 3:4]).then_inc(e_done, 1)

            def pair_params(i):
                if not isinstance(i, int) or i > 0:
                    act.wait_ge(taps_done, i)
                nc.scalar.copy(prp[:, :, :], prm[:, bass.ds(i * 2, 2), :]).then_inc(prm_set, 1)

            input_and_units(HP, N_MIX, C_MIXPRE, MIX)
            for j in range(U1, UM + 2):
                unit(MIX + j)
                if j == 22:
                    act.wait_ge(f_na, 1)
                    nc.scalar.activation(fz[:, 2, :], fz[:, 1, :], ACT.Exp).then_inc(f_e, 1)
                if j == 24:
                    act.wait_ge(f_y, 1)
                    nc.scalar.activation(fz[:, 4, :], fz[:, 3, :], ACT.Ln).then_inc(f_ln, 1)
                if j == 31:
                    act.wait_ge(f_c, 1)
                    act.dma_start(crow.rearrange("o h t -> (o h) t"), fz[:, 7, :]).then_inc(crow_stored, 16)
                if j == 22:
                    pair_params(0)

            def pair_body(i):
                for j in range(UM):
                    unit(MIX1 + j, UM, i)
                    if j == 0:
                        pair_starts(i)
                    if j == 4:
                        gates(i)
                    if j == 7:
                        head_exp(i, 0)
                    if j == 10:
                        head_exp(i, 1)
                    if j == 20:
                        pair_params(i + 1)

            act.wait_ge(crow_stored, 16)
            with act.Fori(0, PAIRS - 1) as i:
                pair_body(i)

            for j in range(G2 * U1):
                unit(WO + j)
                if j == 0:
                    pair_starts(PAIRS - 1)
                if j == 3:
                    gates(PAIRS - 1)
                if j == 4:
                    head_exp(PAIRS - 1, 0)
                if j == 5:
                    head_exp(PAIRS - 1, 1)
                if j == 12:
                    act.wait_ge(m_ready, H + 1)
                    act.wait_ge(mem_landed, 16)
                    for b in range(2):
                        nc.scalar.activation(junk[:, b, :], memr[:, b, :], ACT.Square,
                                             accum_out=mst[:, b:b + 1]).then_inc(msq_done, 1)
                for kp in range(HP):
                    if j == min(18 + 2 * kp, 31):
                        act.wait_ge(memt_full, kp + 1)
                        for t in range(2):
                            k = 2 * kp + t
                            ins = nc.scalar.activation(mem[:, k, 0, :], ps[:, 5 + kp % 2, t * T:(t + 1) * T], ACT.Copy,
                                                       scale=par[:, C_MKV + k:C_MKV + k + 1])
                        ins.then_inc(memhi_ready, 1)
                if j in (11, 19, 27):
                    branch_out(N_MIXOUT, WO_G + (j - 11) // 8, (j - 11) // 8)

            for j in range(RING):
                unit(MKV + j)
            branch_out(N_MIXOUT, MKV_G - 1, G2 - 1)
            input_and_units(2 * HP, N_MQ, C_MQPRE, MKV)
            for j in range(U1, 2 * U1):
                unit(MKV + j)
            for j in range(U1):
                unit(MQ + j)
            for j in range(RING):
                unit(MO + j)
            for hd in range(MH):
                act.wait_ge(mmax_ready, hd + 1)
                for b in range(2):
                    ins = nc.scalar.activation(ml[:, hd, b, :], ps[:, 4 + hd, b * T:(b + 1) * T], ACT.Exp,
                                               bias=mmx[:, hd, b:b + 1], scale=SCALE,
                                               accum_out=mmx[:, hd, 2 + b:3 + b])
                ins.then_inc(mexp_done, 1)
            for j in range(RING, G2 * UO):
                unit(MO + j)
                if j % 2 == 1:
                    branch_out(N_MOUT, MO_G + (j - 5) // 2, (j - 5) // 2)
            for j in range(RING):
                unit(F2A + j)
                if j % 2 == 1:
                    branch_out(N_MOUT, MO_G + 2 + j // 2, 2 + j // 2)
            ffn(1, 3 * HP, N_F2, C_F2PRE, F2A, F2B, F2B_G)
            branch_out(N_F2OUT, F2B_G + G2 - 1, G2 - 1)

            for c in range(8):
                act.wait_ge(ot_full, c + 1)
                nc.scalar.copy(ot[:, c, :], ps[:, c, :]).then_inc(ot_ready, 1)
                act.wait_ge(ot_ready, c + 1)
                b, q = c % 2, c // 2
                act.dma_start(out[0, b * P:(b + 1) * P, q * 512:(q + 1) * 512], ot[:, c, :]).then_inc(out_stored, 16)

        @block.vector
        def _(dve):
            own = Chain(dve, dve_own)

            def tile_tokens(r, n):
                return r[:, :].rearrange("p (o t) -> p o t", o=1).broadcast_to([P, n, T])

            def banks(grp, b=0, n=2):
                first = grp % 2 * 2 + b
                return ps[:, first:first + n, :].rearrange("p b (m t) -> p (b m) t", t=T)

            def unit(n0, per=0, i=None):
                s = slot_of(n0)
                dve.wait_ge(hi_done, of(n0 + 1, per, i))
                nc.vector.tensor_tensor(w_lo[:, s, :], raw[:, s, :], w_hi[:, s, :].bitcast(F32),
                                        ALU.subtract).then_inc(lo_done, 1)

            def units(n0, count):
                loops = count // RING
                if loops > 1:
                    with dve.Fori(0, loops) as i:
                        for j in range(RING):
                            unit(n0 + j, RING, i)
                else:
                    loops = 0
                for j in range(loops * RING, count):
                    unit(n0 + j)

            def group_done(grp, per=0, i=None):
                dve.wait_ge(w_used, of(ENDS[grp], per * U1, i))

            def mean(norm, weight=1.0):
                dve.wait_ge(sum_full, norm + 1)
                nc.vector.tensor_scalar(ms[:, :], ps[:, B_NORM, 0:2], 1.0 / (D * weight * weight),
                                        EPS / (weight * weight), ALU.mult, ALU.add).then_inc(ms_ready, 1)

            def spread(norm):
                dve.wait_ge(r_ready, norm + 1)
                for b in range(2):
                    ins = nc.vector.tensor_scalar(diag[:, b, :], ident[:, :], rtok[:, b:b + 1], None, ALU.mult)
                ins.then_inc(diag_ready, 1)
                dve.wait_ge(r_full, norm + 1)
                nc.vector.tensor_copy((r_out if norm % 2 else r_in)[:, :], ps[:, B_NORM, T:2 * T]).then_inc(r_set, 1)
                dve.wait_ge(r_set, norm + 1)

            def input_lo(base, gain, kp):
                dve.wait_ge(xhi_ready, base + kp + 1)
                for k in (2 * kp, 2 * kp + 1):
                    ins = nc.vector.scalar_tensor_tensor(
                        out=xs[:, k, 1, :], in0=h[:, k, :], scalar=par[:, gain + k:gain + k + 1],
                        in1=xs[:, k, 0, :].bitcast(F32), op0=ALU.mult, op1=ALU.subtract)
                ins.then_inc(x_ready, 1)

            def input_and_units(base, gain, n0, update):
                update(0)
                for kp in range(HP):
                    if kp + 1 < HP:
                        update(kp + 1)
                    if kp >= RING:
                        unit(n0 + kp)
                    input_lo(base, gain, kp)

            def branch_tiles(grp, m):
                group_done(grp)
                nc.vector.tensor_copy(f[:, 4 * m:4 * m + 4, :], banks(grp)).then_inc(grp_out, 1)

            def branch_norm(gain, kp):
                for k in (2 * kp, 2 * kp + 1):
                    ins = nc.vector.scalar_tensor_tensor(
                        out=f[:, k, :], in0=f[:, k, :], scalar=par[:, gain + k:gain + k + 1],
                        in1=r_out[:, :], op0=ALU.mult, op1=ALU.mult)
                ins.then_inc(t_ready, 1)

            def branch_scale(norm, grp, weight=1.0):
                mean(norm, weight)
                dve.wait_ge(grp_out, grp)
                spread(norm)

            def gate_up_out(k, grp, par_grp, per=0, i=None):
                group_done(grp, per, i)
                nc.vector.tensor_tensor(gt[:, :, :], banks(par_grp, 0, 1), tile_tokens(r_in, 2), ALU.mult).then_inc(gate_in, 1)
                nc.vector.tensor_tensor(up[:, :, :], banks(par_grp, 1, 1), tile_tokens(r_in, 2), ALU.mult).then_inc(grp_out, 1)

            def gate_times_up(k, grp, n, per=0, i=None):
                dve.wait_ge(silu_done, of(k * G1 + n + 1, per, i))
                dve.wait_ge(grp_out, of(grp + 1, per, i))
                own.step(nc.vector.tensor_tensor(up[:, :, :], gt[:, :, :], up[:, :, :], ALU.mult))
                own.settle()
                where = bass.ds(2 * n if i is None else i * (2 * per) + 2 * n, 2)
                own.step(nc.vector.tensor_copy(g[:, where, 0, :], up[:, :, :]))
                own.settle()
                nc.vector.tensor_tensor(g[:, where, 1, :], up[:, :, :], g[:, where, 0, :].bitcast(F32),
                                        ALU.subtract).then_inc(g_ready, 1)

            def ffn(k, base, norm, gain, n13, grp13, n2, grp2, update):
                input_and_units(base, gain, n13, update)
                for j in range(U1, 2 * U1):
                    unit(n13 + j)
                    if j == U1 + 3:
                        mean(norm)
                        spread(norm)
                        gate_up_out(k, grp13, grp13)
                    if j == U1 + 4:
                        gate_times_up(k, grp13, 0)
                with dve.Fori(0, (G1 - 2) // 2) as i:
                    own.enter(i, 4)
                    for j in range(2 * U1):
                        unit(n13 + 2 * U1 + j, 2 * U1, i)
                        b = 1 + j // U1
                        if j % U1 == 3:
                            gate_up_out(k, grp13 + b, grp13 + b, 2, i)
                        if j % U1 == 4:
                            gate_times_up(k, grp13 + b, b, 2, i)
                own.leave((G1 - 2) // 2)
                for j in range(RING):
                    unit(n2 + j)
                gate_up_out(k, grp2 - 1, grp2 - 1)
                gate_times_up(k, grp2 - 1, G1 - 1)
                for m in range(G2):
                    units(n2 + m * U2 + RING, U2 if m < G2 - 1 else U2 - RING)
                    if m < G2 - 1:
                        branch_tiles(grp2 + m, m)

            nc.vector.memset(tri1[:, :], 1.0).then_inc(consts_set, 1)
            nc.vector.memset(mhalf[:, :], -0.5).then_inc(consts_set, 1)
            dve.sem_inc(ncm_done, 1)
            dve.sem_inc(m_ready, 1)
            dve.wait_ge(par_t, 1)
            nc.vector.tensor_copy(par[:, 0:P], ps[:, 0, 0:P])
            own.step(nc.vector.tensor_copy(par[:, P:NPAR], ps[:, 1, 0:NPAR - P]))
            own.settle()
            nc.vector.tensor_copy(prm[:, :, 0:4].rearrange("p k f -> p f k"),
                                  par[:, C_CW:NPAR].rearrange("p (f k) -> p f k", f=4))
            nc.vector.tensor_scalar(prm[:, :, 4:6].rearrange("p k f -> p f k"),
                                    par[:, C_GB:C_CW].rearrange("p (f k) -> p f k", f=2),
                                    -1.0, None, ALU.mult).then_inc(par_ready, 1)
            for j in range(RING):
                unit(F1A + j)

            def x_pair(kp):
                dve.wait_ge(xt_full, kp + 1)
                nc.vector.tensor_copy(h[:, 2 * kp:2 * kp + 2, :].rearrange("p k t -> p (k t)"),
                                      ps[:, 4 + kp % 4, :]).then_inc(h_ready, 1)

            ffn(0, 0, N_F1, C_F1PRE, F1A, F1A_G, F1B, F1B_G, x_pair)

            for j in range(RING):
                unit(MIX + j)
            branch_tiles(MIX_G - 1, G2 - 1)
            branch_scale(N_F1OUT, MIX_G, 0.5)
            input_and_units(HP, C_MIXPRE, MIX, lambda kp: branch_norm(C_F1POST, kp))

            def pair_qk(p, grp, par_grp, per=0, i=None):
                group_done(grp, per, i)
                nc.vector.tensor_tensor(qk[:, :, :], banks(par_grp), tile_tokens(r_in, 4), ALU.mult).then_inc(grp_out, 1)

            def pair_vc(p, grp, par_grp, per=0, i=None):
                group_done(grp, per, i)
                nc.vector.tensor_tensor(vc[:, :, :], banks(par_grp), tile_tokens(r_in, 4), ALU.mult).then_inc(grp_out, 1)

            def pair_vtok(p):
                dve.wait_ge(vt_full, p + 1)
                nc.vector.tensor_copy(vtok[:, :, :, :].rearrange("p a b d -> p (a b d)"), ps[:, B_Y, :]).then_inc(vtok_ready, 1)

            def pair_bc(p, grp, par_grp, per=0, i=None):
                group_done(grp, per, i)
                if i is not None:
                    dve.wait_ge(ycb_done, p)
                nc.vector.tensor_tensor(bc[:, :, :], banks(par_grp), tile_tokens(r_in, 4), ALU.mult).then_inc(grp_out, 1)

            def pair_taps(p):
                dve.wait_ge(z_ready, p + 1)
                dve.wait_ge(prm_set, p + 1)
                for t in range(2):
                    ins = nc.vector.tensor_scalar(yc[:, t, :], zp[:, t, 0:T], prp[:, t, 0:1], prp[:, t, 3:4], ALU.mult, ALU.add)
                own.step(ins)
                own.settle()
                for tap in (1, 2):
                    for t in range(2):
                        ins = nc.vector.scalar_tensor_tensor(out=yc[:, t, :], in0=zp[:, t, tap:tap + T], scalar=prp[:, t, tap:tap + 1],
                                                             in1=yc[:, t, :], op0=ALU.mult, op1=ALU.add)
                    if tap == 1:
                        own.step(ins)
                        own.settle()
                ins.then_inc(taps_done, 1)

            def pair_gates(p, grp, par_grp, per=0, i=None):
                group_done(grp, per, i)
                nc.vector.tensor_tensor(gat[:, :, :], banks(par_grp), tile_tokens(r_in, 4), ALU.mult)                    .then_inc(grp_out, 1)

            def pair_sigmoid(p):
                dve.wait_ge(gat_exp, p + 1)
                own.step(nc.vector.tensor_scalar(gat[:, :, :], gat[:, :, :], 1.0, None, ALU.add))
                own.settle()
                nc.vector.reciprocal(gat[:, :, :], gat[:, :, :]).then_inc(sig_ready, 1)

            def pair_decay(p):
                dve.wait_ge(ncr_landed, p * 16 + 16)
                dve.wait_ge(cq_set, p + 1)
                for hd in range(2):
                    nc.vector.scalar_tensor_tensor(out=ncm[:, hd, 0:P], in0=ncr[:, hd, 0:P], scalar=cq[:, 0, hd:hd + 1],
                                                   in1=mask[:, :], op0=ALU.add, op1=ALU.add)
                    nc.vector.tensor_scalar(ncm[:, hd, P:2 * P], ncr[:, hd, 0:P], cq[:, 1, hd:hd + 1], None, ALU.add)
                    ins = nc.vector.scalar_tensor_tensor(out=ncm[:, hd, 2 * P:3 * P], in0=ncr[:, hd, P:T], scalar=cq[:, 1, hd:hd + 1],
                                                         in1=mask[:, :], op0=ALU.add, op1=ALU.add)
                ins.then_inc(ncm_done, 1)

            def head_logits(p, hd):
                dve.wait_ge(s_full, p * 2 + hd + 1)
                dve.wait_ge(ncm_done, p + 2)
                own.step(nc.vector.scalar_tensor_tensor(out=lg[:, hd, :], in0=ps[:, B_SCORE[hd], 0:3 * P], scalar=SCALE,
                                                        in1=ncm[:, hd, :], op0=ALU.mult, op1=ALU.add))
                own.settle()
                nc.vector.reduce_max(st[:, hd, 0:1], lg[:, hd, 0:P], AX_X)
                own.step(nc.vector.reduce_max(st[:, hd, 1:2], lg[:, hd, P:3 * P], AX_X))
                own.settle()
                nc.vector.tensor_scalar(st[:, hd, 0:2], st[:, hd, 0:2], -1.0, None, ALU.mult).then_inc(l_ready, 1)

            def head_probs(p, hd):
                dve.wait_ge(e_done, p * 2 + hd + 1)
                own.step(nc.vector.reciprocal(st[:, hd, 4:6], st[:, hd, 2:4]))
                own.settle()
                nc.vector.tensor_scalar(lg[:, hd, 0:P], lg[:, hd, 0:P], st[:, hd, 4:5], None, ALU.mult)
                nc.vector.tensor_scalar(lg[:, hd, P:3 * P], lg[:, hd, P:3 * P], st[:, hd, 5:6], None, ALU.mult).then_inc(p_ready, 1)

            def head_pt(p, hd):
                dve.wait_ge(pt_full, p * 2 + hd + 1)
                nc.vector.tensor_copy(pt[:, hd, :], ps[:, B_PT, 0:3 * P]).then_inc(pt_ready, 1)

            def head_merge(p, hd):
                dve.wait_ge(y_full, p * 2 + hd + 1)
                dve.wait_ge(sig_ready, p + 1)
                dve.wait_ge(m_ready, p * 2 + hd + 1)
                nc.vector.tensor_tensor(mg[:, :], ps[:, B_Y, 0:T], gat[:, hd, :], ALU.mult).then_inc(y_out, 1)
                dve.wait_ge(ymix_ready, p + 1)
                dve.wait_ge(y_out, p * 2 + hd + 1)
                own.step(nc.vector.tensor_tensor(mg[:, :], mg[:, :], yc[:, hd, :], ALU.add))
                own.settle()
                k = bass.ds(p * 2 + hd, 1)
                mgt = mg[:, :].rearrange("p (o t) -> p o t", o=1)
                own.step(nc.vector.tensor_copy(mrg[:, k, 0, :], mgt))
                own.settle()
                nc.vector.tensor_tensor(mrg[:, k, 1, :], mgt, mrg[:, k, 0, :].bitcast(F32), ALU.subtract).then_inc(m_ready, 1)

            for j in range(U1, UM + 2):
                unit(MIX + j)
                if j == 11:
                    mean(N_MIX)
                    spread(N_MIX)
                    pair_qk(0, MIX_G, MIX_G)
                if j == 21:
                    group_done(MIX_G + 2)
                    own.step(nc.vector.tensor_tensor(fz[:, 0, :], ps[0:H, (MIX_G + 2) % 2 * 2, 0:T], r_in[0:H, :], ALU.mult))
                    own.settle()
                    dve.wait_ge(par_landed, 13 * 16)
                    own.step(nc.vector.tensor_scalar(fz[:, 0, :], fz[:, 0, :], fbias[:, 0:1], None, ALU.add))
                    own.settle()
                    own.step(nc.vector.tensor_scalar(fz[:, 1, :], fz[:, 0, :], -1.0, None, ALU.mult))
                    own.settle()
                    nc.vector.tensor_tensor(fz[:, 1, :], fz[:, 0, :], fz[:, 1, :], ALU.min).then_inc(f_na, 1)
                    nc.vector.tensor_scalar(fz[:, 5, :], fz[:, 0, :], 0.0, None, ALU.min).then_inc(grp_out, 1)
                if j == 23:
                    dve.wait_ge(f_e, 1)
                    nc.vector.tensor_scalar(fz[:, 3, :], fz[:, 2, :], 1.0, None, ALU.add).then_inc(f_y, 1)
                    dve.wait_ge(f_y, 1)
                    nc.vector.scalar_tensor_tensor(out=fz[:, 6, :], in0=fz[:, 3, :], scalar=-1.0, in1=fz[:, 2, :],
                                                   op0=ALU.add, op1=ALU.subtract)
                    own.step(nc.vector.reciprocal(fz[:, 7, :], fz[:, 3, :]))
                    own.settle()
                if j == 25:
                    dve.wait_ge(f_ln, 1)
                    own.step(nc.vector.tensor_tensor(fz[:, 6, :], fz[:, 6, :], fz[:, 7, :], ALU.mult))
                    own.step(nc.vector.tensor_tensor(fz[:, 5, :], fz[:, 5, :], fz[:, 4, :], ALU.subtract))
                    own.settle()
                    nc.vector.tensor_tensor(fz[:, 5, :], fz[:, 5, :], fz[:, 6, :], ALU.add).then_inc(f_log, 1)
                if j == 27:
                    dve.wait_ge(f_tok, 1)
                    nc.vector.tensor_copy(ftok[:, :, :], ps[:, B_S, 0:2 * H].rearrange("p (b h) -> p b h", h=H)).then_inc(f_tokc, 1)
                if j == 19:
                    pair_vc(0, MIX_G + 1, MIX_G + 1)
                if j == 29:
                    dve.wait_ge(f_cum, 1)
                    nc.vector.tensor_copy(ctok[:, :, :], ps[:, B_PT, 0:2 * H].rearrange("p (b h) -> p b h", h=H))
                    nc.vector.tensor_scalar(fz[:, 7, :], ps[0:H, B_PT, T:2 * T], -1.0, None, ALU.mult).then_inc(f_c, 1)
                if j == 23:
                    pair_vtok(0)
                if j == 29:
                    pair_bc(0, MIX_G + 3, MIX_G + 3)
                if j == 31:
                    pair_taps(0)
            dve.wait_ge(taps_done, 1)

            with dve.Fori(0, PAIRS - 1) as i:
                own.enter(i, 13)
                for j in range(UM):
                    unit(MIX1 + j, UM, i)
                    if j == 3:
                        pair_gates(i, MIX1_G - 1, MIX1_G - 1, 4, i)
                    if j == 4:
                        pair_decay(i)
                    if j == 5:
                        pair_sigmoid(i)
                    if j == 6:
                        head_logits(i, 0)
                    if j == 8:
                        head_probs(i, 0)
                    if j == 9:
                        head_logits(i, 1)
                    if j == 11:
                        head_pt(i, 0)
                        pair_qk(i + 1, MIX1_G, MIX1_G, 4, i)
                    if j == 12:
                        head_probs(i, 1)
                    if j == 14:
                        head_merge(i, 0)
                    if j == 15:
                        head_pt(i, 1)
                    if j == 18:
                        head_merge(i, 1)
                    if j == 19:
                        pair_vc(i + 1, MIX1_G + 1, MIX1_G + 1, 4, i)
                    if j == 23:
                        pair_vtok(i + 1)
                    if j == 27:
                        pair_bc(i + 1, MIX1_G + 2, MIX1_G + 2, 4, i)
                    if j == 29:
                        pair_taps(i + 1)
            own.leave(PAIRS - 1)

            last = PAIRS - 1
            for j in range(G2 * U1):
                unit(WO + j)
                if j == 3:
                    pair_gates(last, WO_G - 1, WO_G - 1)
                    pair_decay(last)
                if j == 4:
                    head_logits(last, 0)
                    head_logits(last, 1)
                    pair_sigmoid(last)
                if j == 5:
                    head_probs(last, 0)
                if j == 6:
                    head_probs(last, 1)
                if j == 7:
                    head_pt(last, 0)
                if j == 8:
                    head_pt(last, 1)
                if j == 9:
                    head_merge(last, 0)
                if j == 10:
                    head_merge(last, 1)
                if j == 13:
                    dve.wait_ge(msq_done, 2)
                    nc.vector.tensor_scalar(mst[:, 2:4], mst[:, 0:2], 1.0 / D, EPS, ALU.mult, ALU.add).then_inc(mm_ready, 1)
                if j == 14:
                    dve.wait_ge(mr_ready, 1)
                    for b in range(2):
                        nc.vector.tensor_scalar(memr[:, b, :], memr[:, b, :], mst[:, 4 + b:5 + b], None, ALU.mult).then_inc(memn_ready, 1)
                for kp in range(HP):
                    if j == min(18 + 2 * kp, 31):
                        dve.wait_ge(memhi_ready, kp + 1)
                        for t in range(2):
                            k = 2 * kp + t
                            ins = nc.vector.scalar_tensor_tensor(
                                out=mem[:, k, 1, :], in0=ps[:, 5 + kp % 2, t * T:(t + 1) * T], scalar=par[:, C_MKV + k:C_MKV + k + 1],
                                in1=mem[:, k, 0, :].bitcast(F32), op0=ALU.mult, op1=ALU.subtract)
                        ins.then_inc(mem_ready, 1)
                if j in (11, 19, 27):
                    branch_tiles(WO_G + (j - 11) // 8, (j - 11) // 8)

            for j in range(RING):
                unit(MKV + j)
            branch_tiles(MKV_G - 1, G2 - 1)
            branch_scale(N_MIXOUT, MKV_G)
            input_and_units(2 * HP, C_MQPRE, MKV, lambda kp: branch_norm(C_MIXPOST, kp))
            for j in range(U1, 2 * U1):
                unit(MKV + j)
                if j == 11:
                    group_done(MKV_G)
                    nc.vector.tensor_copy(kt[:, :, :], banks(MKV_G)).then_inc(grp_out, 1)
                if j == 15:
                    mean(N_MQ)
                    spread(N_MQ)
            for j in range(U1):
                unit(MQ + j)
                if j == 3:
                    group_done(MKV_G + 1)
                    nc.vector.tensor_copy(vt[:, :, :], banks(MKV_G + 1)).then_inc(grp_out, 1)
                if j == 7:
                    dve.wait_ge(mvt_full, 1)
                    nc.vector.tensor_copy(mvtok[:, :, :, :].rearrange("p m b d -> p (m b d)"),
                                          ps[:, 5:7, :].rearrange("p b n -> p (b n)")).then_inc(mvtok_ready, 1)
            for j in range(RING):
                unit(MO + j)
            group_done(MQ_G)
            nc.vector.tensor_tensor(qt[:, :, :], banks(MQ_G), tile_tokens(r_in, MH), ALU.mult).then_inc(grp_out, 1)
            for hd in range(MH):
                dve.wait_ge(ms_full, hd + 1)
                own.step(nc.vector.reduce_max(mmx[:, hd, 0:2], ps[:, 4 + hd, :].rearrange("p (b k) -> p b k", b=2), AX_X))
                own.settle()
                nc.vector.tensor_scalar(mmx[:, hd, 0:2], mmx[:, hd, 0:2], -SCALE, None, ALU.mult).then_inc(mmax_ready, 1)
            for hd in range(MH):
                dve.wait_ge(mexp_done, hd + 1)
                own.step(nc.vector.reciprocal(mmx[:, hd, 4:6], mmx[:, hd, 2:4]))
                own.settle()
                for b in range(2):
                    ins = nc.vector.tensor_scalar(ml[:, hd, b, :], ml[:, hd, b, :], mmx[:, hd, 4 + b:5 + b], None, ALU.mult)
                ins.then_inc(mp_ready, 1)
            for hd in range(MH):
                dve.wait_ge(mpt_full, hd + 1)
                nc.vector.tensor_copy(mpt[:, hd, :, :].rearrange("p b t -> p (b t)"), ps[:, hd, :]).then_inc(mpt_ready, 1)
            for hd in range(MH):
                dve.wait_ge(mo_full, hd + 1)
                own.step(nc.vector.tensor_copy(mo[:, hd, :], ps[:, 4 + hd, 0:T]))
                own.settle()
                own.step(nc.vector.tensor_copy(osp[:, hd, 0, :], mo[:, hd, :]))
                own.settle()
                nc.vector.tensor_tensor(osp[:, hd, 1, :], mo[:, hd, :], osp[:, hd, 0, :].bitcast(F32), ALU.subtract).then_inc(os_ready, 1)
            for j in range(RING, G2 * UO):
                unit(MO + j)
                if j % 2 == 1:
                    branch_tiles(MO_G + (j - 5) // 2, (j - 5) // 2)
            for j in range(RING):
                unit(F2A + j)
                if j % 2 == 1:
                    branch_tiles(MO_G + 2 + j // 2, 2 + j // 2)
            branch_scale(N_MOUT, F2A_G)
            ffn(1, 3 * HP, N_F2, C_F2PRE, F2A, F2A_G, F2B, F2B_G, lambda kp: branch_norm(C_MPOST, kp))
            branch_tiles(F2B_G + G2 - 1, G2 - 1)
            branch_scale(N_F2OUT, F2B_G + G2, 0.5)
            for kp in range(HP):
                branch_norm(C_F2POST, kp)

        @block.gpsimd
        def _(pool):
            own = Chain(pool, pool_own)
            own.step(nc.gpsimd.memset(ident[:, :], 0.0))
            own.step(nc.gpsimd.memset(mask[:, :], 0.0))
            own.settle()
            nc.gpsimd.affine_select(out=ident[:, :], in_=ident[:, :], compare_op=ALU.not_equal, fill=1.0, base=0,
                                    pattern=[[-1, P]], channel_multiplier=1).then_inc(ident_set, 1)
            nc.gpsimd.affine_select(out=mask[:, :], in_=mask[:, :], compare_op=ALU.is_ge, fill=NEG, base=0,
                                    pattern=[[-1, P]], channel_multiplier=1)
            pool.wait_ge(consts_set, 2)
            nc.gpsimd.affine_select(out=tri1[:, 0:P], in_=tri1[:, 0:P], compare_op=ALU.is_ge, fill=0.0, base=0,
                                    pattern=[[1, P]], channel_multiplier=-1).then_inc(ident_set, 1)

            def add_squares(norm, kp):
                c = norm * HP + kp
                pool.wait_ge(sq_ready, c + 1)
                if kp == 0:
                    if norm > 0:
                        pool.wait_ge(sum_full, norm)
                    ins = nc.gpsimd.tensor_copy(sqsum[:, :], sq[:, c % 2, :])
                else:
                    pool.wait_ge(sq_added, added(norm, kp))
                    ins = nc.gpsimd.tensor_tensor(sqsum[:, :], sqsum[:, :], sq[:, c % 2, :], ALU.add)
                ins.then_inc(sq_added, 1)

            def inverse_rms(norm):
                pool.wait_ge(ms_ready, norm + 1)
                nc.gpsimd.tensor_tensor(rtok[:, :], ms[:, :], mhalf[:, :], ALU.pow).then_inc(r_ready, 1)

            def update(n, kp):
                pool.wait_ge(t_ready, n * HP + kp + 1)
                nc.gpsimd.tensor_tensor(h[:, 2 * kp:2 * kp + 2, :], h[:, 2 * kp:2 * kp + 2, :],
                                        f[:, 2 * kp:2 * kp + 2, :], ALU.add).then_inc(h_ready, 1)

            def branch_and_input(n, norm):
                for kp in range(HP - 2):
                    add_squares(norm, kp)
                inverse_rms(norm)
                update(n, 0)
                for kp in range(HP):
                    if kp + 1 < HP:
                        update(n, kp + 1)
                    if norm + 1 < 8:
                        add_squares(norm + 1, kp)
                if norm + 1 < 8:
                    inverse_rms(norm + 1)

            for kp in range(HP):
                add_squares(N_F1, kp)
            inverse_rms(N_F1)
            branch_and_input(0, N_F1OUT)

            def pair_conv(p, grp_done):
                grp_done()
                if not isinstance(p, int):
                    pool.wait_ge(taps_done, p)
                nc.gpsimd.tensor_tensor(zp[:, :, 2:T + 2], bc[:, 2:4, :], vc[:, 2:4, :], ALU.mult).then_inc(z_ready, 1)
                pool.wait_ge(taps_done, p + 1)
                nc.gpsimd.tensor_tensor(yc[:, :, :], yc[:, :, :], bc[:, 0:2, :], ALU.mult).then_inc(ycb_done, 1)

            def pair_conv_gate(p):
                pool.wait_ge(sig_ready, p + 1)
                pool.wait_ge(ycb_done, p + 1)
                nc.gpsimd.tensor_tensor(yc[:, :, :], yc[:, :, :], gat[:, 2:4, :], ALU.mult).then_inc(ymix_ready, 1)

            own.step(nc.gpsimd.memset(zp[:, :, 0:2], 0.0))
            own.settle()
            pair_conv(0, lambda: pool.wait_ge(grp_out, MIX_G + 4))
            with pool.Fori(0, PAIRS - 1) as i:
                pair_conv_gate(i)
                pair_conv(i + 1, lambda: pool.wait_ge(grp_out, i * 4 + MIX1_G + 3))
            pair_conv_gate(PAIRS - 1)

            pool.wait_ge(mm_ready, 1)
            nc.gpsimd.tensor_tensor(mst[:, 4:6], mst[:, 2:4], mhalf[:, 0:2], ALU.pow).then_inc(mr_ready, 1)
            branch_and_input(1, N_MIXOUT)
            branch_and_input(2, N_MOUT)
            branch_and_input(3, N_F2OUT)

        @block.tensor
        def _(pe):
            def product(n0, grp, x, k0, first=False, last=False, ready=None, per=0, i=None, grp_per=0):
                s = slot_of(n0)
                pe.wait_ge(lo_done, of(n0 + 1, per, i))
                if ready is not None:
                    pe.wait_ge(*ready)
                if first and grp >= 2:
                    pe.wait_ge(grp_out, of(grp - 1, grp_per, i))
                for kk in range(UK):
                    for m in range(GT):
                        c = (kk * GT + m) * P
                        o = ps[:, grp % 2 * 2 + m // 2, m % 2 * T:m % 2 * T + T]
                        hi, lo = w_hi[:, s, c:c + P], w_lo[:, s, c:c + P]
                        nc.tensor.matmul(o, hi, x[:, k0 + kk, 0, :], start=first and kk == 0 and m % 2 == 0,
                                         stop=False, skip_group_check=True)
                        nc.tensor.matmul(o, hi, x[:, k0 + kk, 1, :], start=False, stop=False, skip_group_check=True)
                        ins = nc.tensor.matmul(o, lo, x[:, k0 + kk, 0, :], start=False,
                                               stop=last and kk == UK - 1, skip_group_check=True)
                return ins

            def unit(n0, grp, x, k0, units=U1, ready=None, per=0, i=None, grp_per=0):
                last = k0 == UK * (units - 1)
                ins = product(n0, grp, x, k0, k0 == 0, last, ready, per, i, grp_per)
                ins.then_inc(w_used, 1)

            def sums(norm):
                parts = [sqsum]
                if norm % 2:
                    pe.wait_ge(sq_ready, (norm + 1) * HP)
                    parts = [sqsum, sq[:, 0, :], sq[:, 1, :]]
                pe.wait_ge(sq_added, added(norm, HP - 2 if norm % 2 else HP))
                if norm > 0:
                    pe.wait_ge(r_set, norm)
                for b in range(2):
                    for n, part in enumerate(parts):
                        for t in range(2):
                            c = t * T + b * P
                            ins = nc.tensor.matmul(ps[:, B_NORM, b:b + 1], part[:, c:c + P], ones[:, 0:1],
                                                   start=n + t == 0, stop=n == len(parts) - 1 and t == 1)
                ins.then_inc(sum_full, 1)

            def spread(norm):
                pe.wait_ge(diag_ready, norm + 1)
                for b in range(2):
                    ins = nc.tensor.matmul(ps[:, B_NORM, T + b * P:T + (b + 1) * P], ones, diag[:, b, :],
                                           start=True, stop=True)
                ins.then_inc(r_full, 1)

            def ffn(k, base, norm, n13, grp13, n2, grp2):
                for b in range(2):
                    for u in range(U1):
                        unit(n13 + b * U1 + u, grp13 + b, xs, UK * u, ready=(x_ready, base + u + 1) if b == 0 else None)
                        if b == 1 and u == 0:
                            sums(norm)
                        if b == 1 and u == 1:
                            spread(norm)
                with pe.Fori(0, (G1 - 2) // 2) as i:
                    for b in range(2):
                        for u in range(U1):
                            unit(n13 + (2 + b) * U1 + u, grp13 + 2 + b, xs, UK * u, per=2 * U1, i=i, grp_per=2)
                with pe.Fori(0, G2 // 2) as i:
                    for b in range(2):
                        for u in range(U2):
                            unit(n2 + b * U2 + u, grp2 + b, g, UK * u, U2, (g_ready, k * G1 + u + 1) if b == 0 else None,
                                 2 * U2, i, 2)
                sums(norm + 1)
                spread(norm + 1)

            pe.wait_ge(ident_set, 2)
            pe.wait_ge(par_landed, 13 * 16)
            nc.tensor.transpose(ps[:, 0, 0:P], prow[:, 0, :], ident[:, :])
            nc.tensor.transpose(ps[:, 1, 0:NPAR - P], prow[0:NPAR - P, 1, :], ident[0:NPAR - P, 0:NPAR - P]).then_inc(par_t, 1)
            for kp in range(HP):
                if kp % 2 == 0:
                    pe.wait_ge(x_landed[kp // 2], 16)
                if kp >= 4:
                    pe.wait_ge(h_ready, kp - 3)
                for t in range(2):
                    for b in range(2):
                        k = 2 * kp + t
                        ins = nc.tensor.transpose(ps[:, 4 + kp % 4, (t * 2 + b) * P:(t * 2 + b + 1) * P],
                                                  xr[:, b, k * P:(k + 1) * P], ident[:, :])
                ins.then_inc(xt_full, 1)
            pe.wait_ge(par_ready, 1)
            ffn(0, 0, N_F1, F1A, F1A_G, F1B, F1B_G)

            def head_scores(p, hd):
                q, k = qk[:, hd, :], qk[:, 2 + hd, :]
                bank = B_SCORE[hd]
                nc.tensor.matmul(ps[:, bank, 0:P], q[:, 0:P], k[:, 0:P], start=True, stop=True)
                nc.tensor.matmul(ps[:, bank, P:3 * P], q[:, P:T], k, start=True, stop=True).then_inc(s_full, 1)

            def head_transpose(p, hd):
                pe.wait_ge(p_ready, p * 2 + hd + 1)
                if hd == 1:
                    pe.wait_ge(pt_ready, p * 2 + 1)
                for b in range(3):
                    ins = nc.tensor.transpose(ps[:, B_PT, b * P:(b + 1) * P], lg[:, hd, b * P:(b + 1) * P], ident[:, :])
                ins.then_inc(pt_full, 1)

            def head_values(p, hd):
                pe.wait_ge(pt_ready, p * 2 + hd + 1)
                if hd == 0:
                    pe.wait_ge(vtok_ready, p + 1)
                else:
                    pe.wait_ge(y_out, p * 2 + 1)
                nc.tensor.matmul(ps[:, B_Y, 0:T], vtok[:, hd, 0, :], pt[:, hd, 0:2 * P], start=True, stop=False, skip_group_check=True)
                nc.tensor.matmul(ps[:, B_Y, P:T], vtok[:, hd, 1, :], pt[:, hd, 2 * P:3 * P], start=False, stop=True,
                                 skip_group_check=True).then_inc(y_full, 1)

            def pair_values(p, grp_done):
                grp_done()
                for hd in range(2):
                    for b in range(2):
                        ins = nc.tensor.transpose(ps[:, B_Y, (hd * 2 + b) * P:(hd * 2 + b + 1) * P],
                                                  vc[:, hd, b * P:(b + 1) * P], ident[:, :])
                ins.then_inc(vt_full, 1)

            for j in range(UM + 2):
                if j < U1:
                    unit(MIX + j, MIX_G, xs, UK * j, ready=(x_ready, HP + j + 1))
                elif 2 * U1 <= j < 2 * U1 + 2:
                    fu, s = j - 2 * U1, slot_of(MIX + j)
                    pe.wait_ge(lo_done, MIX + j + 1)
                    if fu == 0:
                        pe.wait_ge(grp_out, MIX_G + 1)
                    o = ps[:, (MIX_G + 2) % 2 * 2, 0:T]
                    for kk in range(8):
                        k = fu * 8 + kk
                        hi, lo = w_hi[:, s, kk * P:(kk + 1) * P], w_lo[:, s, kk * P:(kk + 1) * P]
                        nc.tensor.matmul(o, hi, xs[:, k, 0, :], start=k == 0, stop=False, skip_group_check=True)
                        nc.tensor.matmul(o, hi, xs[:, k, 1, :], start=False, stop=False, skip_group_check=True)
                        ins = nc.tensor.matmul(o, lo, xs[:, k, 0, :], start=False, stop=k == KD - 1, skip_group_check=True)
                    ins.then_inc(w_used, 1)
                else:
                    b = j // U1 if j < 2 * U1 else (j - 2) // U1 + 1
                    unit(MIX + j, MIX_G + b, xs, UK * ((j if b < 2 else j - 2) % U1))
                if j == 8:
                    sums(N_MIX)
                if j == 9:
                    spread(N_MIX)
                if j == 23:
                    pe.wait_ge(f_log, 1)
                    for b in range(2):
                        ins = nc.tensor.matmul(ps[:, B_S, b * H:(b + 1) * H], fz[:, 5, b * P:(b + 1) * P],
                                               ident[0:H, 0:H], start=True, stop=True)
                    ins.then_inc(f_tok, 1)
                if j == 25:
                    pe.wait_ge(f_tokc, 1)
                    nc.tensor.matmul(ps[:, B_PT, 0:H], tri1[:, 0:P], ftok[:, 0, :], start=True, stop=True)
                    nc.tensor.matmul(ps[:, B_PT, H:2 * H], ones, ftok[:, 0, :], start=True, stop=False)
                    nc.tensor.matmul(ps[:, B_PT, H:2 * H], tri1[:, 0:P], ftok[:, 1, :], start=False, stop=True)
                    nc.tensor.matmul(ps[0:H, B_PT, T:2 * T], ftok[:, 0, :], tri1[:, :], start=True, stop=False, skip_group_check=True)
                    nc.tensor.matmul(ps[0:H, B_PT, T + P:2 * T], ftok[:, 1, :], tri1[:, 0:P], start=False, stop=True,
                                     skip_group_check=True).then_inc(f_cum, 1)
                if j == 19:
                    pair_values(0, lambda: pe.wait_ge(grp_out, MIX_G + 2))

            with pe.Fori(0, PAIRS - 1) as i:
                for j in range(UM):
                    unit(MIX1 + j, MIX1_G + j // U1, xs, UK * (j % U1), per=UM, i=i, grp_per=4)
                    if j == 1:
                        head_scores(i, 0)
                    if j == 3:
                        head_scores(i, 1)
                    if j == 6:
                        head_transpose(i, 0)
                    if j == 9:
                        head_values(i, 0)
                    if j == 10:
                        head_transpose(i, 1)
                    if j == 13:
                        head_values(i, 1)
                    if j == 19:
                        pe.wait_ge(y_out, i * 2 + 2)
                        pair_values(i + 1, lambda: pe.wait_ge(grp_out, i * 4 + MIX1_G + 2))

            last = PAIRS - 1
            for j in range(G2 * U1):
                u = j % U1
                unit(WO + j, WO_G + j // U1, mrg, UK * u, ready=(m_ready, 2 * u + 3) if j < U1 else None)
                if j == 0:
                    head_scores(last, 0)
                    head_scores(last, 1)
                if j == 2:
                    head_transpose(last, 0)
                if j == 4:
                    head_transpose(last, 1)
                    head_values(last, 0)
                if j == 6:
                    head_values(last, 1)
                for kp in range(HP):
                    if j == 13 + 2 * kp:
                        pe.wait_ge(memn_ready, 2)
                        if kp >= 2:
                            pe.wait_ge(mem_ready, kp - 1)
                        for t in range(2):
                            for b in range(2):
                                k = 2 * kp + t
                                ins = nc.tensor.transpose(ps[:, 5 + kp % 2, (t * 2 + b) * P:(t * 2 + b + 1) * P],
                                                          memr[:, b, k * P:(k + 1) * P], ident[:, :])
                        ins.then_inc(memt_full, 1)

            for j in range(2 * U1):
                u = j % U1
                unit(MKV + j, MKV_G + j // U1, mem, UK * u, ready=(mem_ready, u + 1) if j < U1 else None)
                if j == 1:
                    sums(N_MIXOUT)
                if j == 2:
                    spread(N_MIXOUT)
                if j == 12:
                    sums(N_MQ)
                if j == 13:
                    spread(N_MQ)
            for u in range(U1):
                unit(MQ + u, MQ_G, xs, UK * u, ready=(x_ready, 2 * HP + u + 1))
                if u == 3:
                    pe.wait_ge(grp_out, MKV_G + 2)
                    for hd in range(MH):
                        for b in range(2):
                            c = (hd % 2 * 2 + b) * P
                            ins = nc.tensor.transpose(ps[:, 5 + hd // 2, c:c + P], vt[:, hd, b * P:(b + 1) * P], ident[:, :])
                    ins.then_inc(mvt_full, 1)
            pe.wait_ge(mvtok_ready, 1)
            pe.wait_ge(grp_out, MQ_G + 1)
            for hd in range(MH):
                for b in range(2):
                    ins = nc.tensor.matmul(ps[:, 4 + hd, b * T:(b + 1) * T], qt[:, hd, b * P:(b + 1) * P], kt[:, hd, :],
                                           start=True, stop=True)
                ins.then_inc(ms_full, 1)
            for hd in range(MH):
                pe.wait_ge(mp_ready, hd + 1)
                for kb in range(2):
                    for b in range(2):
                        ins = nc.tensor.transpose(ps[:, hd, (kb * 2 + b) * P:(kb * 2 + b + 1) * P],
                                                  ml[:, hd, b, kb * P:(kb + 1) * P], ident[:, :])
                ins.then_inc(mpt_full, 1)
            for hd in range(MH):
                pe.wait_ge(mpt_ready, hd + 1)
                for kb in range(2):
                    ins = nc.tensor.matmul(ps[:, 4 + hd, 0:T], mvtok[:, hd, kb, :], mpt[:, hd, kb, :], start=kb == 0, stop=kb == 1)
                ins.then_inc(mo_full, 1)
            for j in range(G2 * UO):
                u = j % UO
                unit(MO + j, MO_G + j // UO, osp, UK * u, UO, (os_ready, 2 * u + 2) if j < UO else None)
            sums(N_MOUT)
            spread(N_MOUT)

            ffn(1, 3 * HP, N_F2, F2A, F2A_G, F2B, F2B_G)

            for c in range(8):
                b, q = c % 2, c // 2
                pe.wait_ge(h_ready, 4 * HP + 2 * q + 2)
                for t in range(4):
                    ins = nc.tensor.transpose(ps[:, c, t * P:(t + 1) * P], h[:, 4 * q + t, b * P:(b + 1) * P], ident[:, :])
                ins.then_inc(ot_full, 1)


_INS = ["x", "mem", "ffn1_pre_g", "ffn1_w13", "ffn1_w2", "ffn1_post_g", "mix_pre_g", "w_in", "forget_bias",
        "gate_bias", "conv_w", "conv_b", "w_out", "mix_post_g", "mem_q_pre_g", "mem_kv_g", "w_mq", "w_mkv",
        "w_mo", "mem_post_g", "ffn2_pre_g", "ffn2_w13", "ffn2_w2", "ffn2_post_g"]


def kernel(**inputs):
    import numpy as np
    import concourse.bacc as bacc
    from concourse.bass_utils import run_bass_kernel_spmd

    nc = bacc.Bacc("TRN2", target_bir_lowering=False, num_devices=1)
    arrays, aps = {}, {}
    for name in _INS:
        arrays[f"in_{name}"] = np.ascontiguousarray(inputs[name])
        aps[name] = nc.dram_tensor(f"in_{name}", arrays[f"in_{name}"].shape, F32, kind="ExternalInput").ap()
    out = nc.dram_tensor("out", (1, T, D), F32, kind="ExternalOutput").ap()
    build(nc, aps, out)
    return run_bass_kernel_spmd(nc, [arrays], core_ids=[0]).results[0]["out"]
```

```python
from contextlib import ExitStack

import concourse.bass as bass
from concourse import mybir


P = 128
T = 256
D = 2048
KD = D // P
DFF = 5632
KF = DFF // P
H = 16
MH = 4
SCALE = float(P) ** -0.5
EPS = 1e-6
NEG = -1e30

UK = 2
GT = 4
UW = UK * GT * P
RING = 4

F32 = mybir.dt.float32
F32R = mybir.dt.float32r
ALU = mybir.AluOpType
ACT = mybir.ActivationFunctionType
AX_X = mybir.AxisListType.X

G1 = DFF // 256
U1 = KD // UK
G2 = D // (GT * P)
U2 = KF // UK
PAIRS = H // 2
UM = 4 * U1
UO = MH // UK

F1A, F1A_G = 0, 0
F1B, F1B_G = F1A + G1 * U1, F1A_G + G1
MIX, MIX_G = F1B + G2 * U2, F1B_G + G2
MIX1, MIX1_G = MIX + UM + 2, MIX_G + 5
WO, WO_G = MIX1 + (PAIRS - 1) * UM, MIX1_G + (PAIRS - 1) * 4
MK, MK_G = WO + G2 * U1, WO_G + G2
MQ, MQ_G = MK + U1, MK_G + 1
MV, MV_G = MQ + U1, MQ_G + 1
MO, MO_G = MV + U1, MV_G + 1
F2A, F2A_G = MO + G2 * UO, MO_G + G2
F2B, F2B_G = F2A + G1 * U1, F2A_G + G1

WO_ORDER = ([(m, u) for m in range(2) for u in range(U1 - 1)] + [(m, U1 - 1) for m in range(2)]
            + [(m, u) for m in range(2, G2) for u in range(U1)])
SIGMOIDS = (5, 7, 8, 10)
MEM_T = (18, 19, 20, 22, 24, 25, 26, 27)
MEM_SPLIT = (22, 23, 24, 26, 28, 29, 30, 31)


def group_ends():
    ends, n = [], 0
    sizes = ([U1] * G1 + [U2] * G2 + [U1, U1, 2, U1, U1] + [U1] * 4 * (PAIRS - 1)
             + [2 * U1 - 1, 1] + [U1] * (G2 - 2) + [U1] * 3 + [UO] * G2 + [U1] * G1 + [U2] * G2)
    for size in sizes:
        n += size
        ends.append(n)
    return ends


ENDS = group_ends()

OUT_BANKS = (5, 6, 7, 0, 1, 4, 2, 3)
assert (F2B_G + G2 - 1) % 2 == 1

N_F1, N_F1OUT, N_MIX, N_MIXOUT, N_MQ, N_MOUT, N_F2, N_F2OUT = range(8)
HP = KD // 2


def added(norm, kp):
    return norm * HP - norm // 2 * 2 + kp


(C_F1PRE, C_F1POST, C_MIXPRE, C_MIXPOST, C_MQPRE, C_MKV, C_MPOST, C_F2PRE,
 C_F2POST, C_GB, _C1, C_CW, _C2, _C3, C_CB) = range(0, 15 * KD, KD)
NPAR = 15 * KD
PAR_ROWS = (P, NPAR - P)

B_NORM, B_S, B_PT, B_Y = 4, 5, 6, 7
B_SCORE = (B_S, B_NORM)


class Chain:

    def __init__(self, eng, sem):
        self.eng, self.sem, self.n, self.loop = eng, sem, 0, None

    def step(self, ins):
        self.n += 1
        ins.then_inc(self.sem, 1)

    def settle(self):
        if self.loop is None:
            self.eng.wait_ge(self.sem, self.n)
        else:
            i, per = self.loop
            self.eng.wait_ge(self.sem, i * per + self.n)

    def enter(self, i, per):
        self.loop, self.start = (i, per), self.n

    def leave(self, times):
        per = self.loop[1]
        assert self.n - self.start == per, (self.sem, self.n - self.start)
        self.n, self.loop = self.start + per * times, None


def build(nc, a, out):
    with ExitStack() as ctx:
        def sem(name):
            return ctx.enter_context(nc.semaphore(name))

        at = [(nc.sbuf_base + 63) // 32 * 32]

        def place(name, shape, dt=F32, offset=None):
            size = 4
            for n in shape[1:]:
                size *= n
            size = (size + 31) // 32 * 32
            if offset is None:
                offset, at[0] = at[0], at[0] + size
            return nc.alloc_sbuf_tensor_at(name, shape, dt, offset=offset)

        h = place("h", [P, KD, T])
        xs_at = at[0]
        xs = place("xs", [P, KD, 2, T], F32R)
        f = place("f", [P, KD, T], offset=xs_at + KD * T * 4)
        raw = place("raw", [P, RING, UW])
        w_hi = place("w_hi", [P, RING, UW], F32R)
        w_lo = place("w_lo", [P, RING, UW], F32R)
        r_in = place("r_in", [P, T])
        r_out = place("r_out", [P, T])
        ms = place("ms", [P, 2])
        mhalf = place("mhalf", [P, 2])
        rtok = place("rtok", [P, 2])
        diag = place("diag", [P, 2, P])
        ident = place("ident", [P, P])
        tri1 = place("tri1", [P, T])
        ones = tri1[:, P:T]
        mask = place("mask", [P, P])
        par = place("par", [P, NPAR])
        prm = place("prm", [P, KD, 6])
        fbias = place("fbias", [H, 1])
        sq = place("sq", [P, 2, 2 * T])
        sqsum = place("sqsum", [P, 2 * T])
        gt = place("gt", [P, 2, T])
        up = place("up", [P, 2, T])
        arena = at[0]

        g = place("g", [P, KF, 2, T], F32R, arena)
        xr = place("xr", [P, 2, D], F32, arena)
        prow = place("prow", [P, 2, P], F32, arena + 2 * D * 4)
        mrg = place("mrg", [P, KD, 2, T], F32R, arena)
        at[0] = arena + KD * 2 * T * 4
        cross = at[0]
        qk = place("qk", [P, 4, T])
        vc = place("vc", [P, 4, T])
        bc = place("bc", [P, 4, T])
        zp = place("zp", [P, 2, T + 2])
        gat = place("gat", [P, 4, T])
        yc = place("yc", [P, 2, T])
        vtok = place("vtok", [P, 2, 2, P])
        lg = place("lg", [P, 2, 3 * P])
        pt = place("pt", [P, 2, 3 * P])
        ncr = place("ncr", [P, 2, T])
        ncm = place("ncm", [P, 2, 3 * P])
        mg = place("mg", [P, T])
        ctok = place("ctok", [P, 2, H])
        cq = place("cq", [P, 2, 2])
        prp = place("prp", [P, 2, 6])
        st = place("st", [P, 2, 6])
        ftok = place("ftok", [P, 2, H])
        memr_at = arena + KF * 2 * T * 4 - 2 * D * 4
        fz = place("fz", [H, 8, T], F32, memr_at)
        assert at[0] <= memr_at, (at[0], memr_at)
        memr = place("memr", [P, 2, D], F32, memr_at)
        mem = place("mem", [P, KD, 2, T], F32R, cross)
        junk = place("junk", [P, 2, D], F32, cross)
        assert cross + KD * 2 * T * 4 <= memr_at
        at[0] = arena
        kt = place("kt", [P, MH, T])
        qt = place("qt", [P, MH, T])
        mvtok = place("mvtok", [P, MH, 2, P])
        ml = place("ml", [P, MH, 2, T])
        assert at[0] <= cross
        mpt = place("mpt", [P, MH, 2, T], F32, memr_at)
        osp = place("osp", [P, MH, 2, T], F32R, memr_at + MH * 2 * T * 4)
        at[0] = arena + KF * 2 * T * 4
        mst = place("mst", [P, 8])
        mmx = place("mmx", [P, MH, 6])
        ht = place("ht", [P, 8, 512], F32, xs_at)
        ot = place("ot", [P, 8, 512], F32, arena)
        assert at[0] <= nc.sbuf_usable_end, at[0]

        ps = ctx.enter_context(nc.psum_tensor("ps", [P, 8, 512], F32))
        crow = nc.dram_tensor("crow", [1, H, T], F32, kind="Internal").ap()

        x_landed = [sem(f"x_landed{i}") for i in range(4)]
        par_landed = sem("par_landed")
        mem_landed = sem("mem_landed")
        ident_set = sem("ident_set")
        consts_set = sem("consts_set")
        par_t = sem("par_t")
        par_ready = sem("par_ready")
        xt_full = sem("xt_full")
        landed = [sem(f"landed{i}") for i in range(RING)]
        hi_done = sem("hi_done")
        lo_done = sem("lo_done")
        w_used = sem("w_used")
        grp_out = sem("grp_out")
        h_ready = sem("h_ready")
        xhi_ready = sem("xhi_ready")
        x_ready = sem("x_ready")
        x0_ready = sem("x0_ready")
        t_ready = sem("t_ready")
        sq_ready = sem("sq_ready")
        sq_added = sem("sq_added")
        sq_folded = sem("sq_folded")
        sum_full = sem("sum_full")
        ms_ready = sem("ms_ready")
        r_ready = sem("r_ready")
        diag_ready = sem("diag_ready")
        r_full = sem("r_full")
        r_set = sem("r_set")
        gate_in = sem("gate_in")
        silu_done = sem("silu_done")
        g_ready = sem("g_ready")
        dve_own = sem("dve_own")
        pool_own = sem("pool_own")
        f_na = sem("f_na")
        f_e = sem("f_e")
        f_y = sem("f_y")
        f_ln = sem("f_ln")
        f_log = sem("f_log")
        f_tok = sem("f_tok")
        f_tokc = sem("f_tokc")
        f_cum = sem("f_cum")
        f_c = sem("f_c")
        crow_stored = sem("crow_stored")
        ncr_landed = sem("ncr_landed")
        prm_set = sem("prm_set")
        cq_set = sem("cq_set")
        ncm_done = sem("ncm_done")
        z_ready = sem("z_ready")
        taps_done = sem("taps_done")
        ycb_done = sem("ycb_done")
        gat_exp = sem("gat_exp")
        sig_ready = sem("sig_ready")
        ymix_ready = sem("ymix_ready")
        vt_full = sem("vt_full")
        vtok_ready = sem("vtok_ready")
        s_full = sem("s_full")
        l_ready = sem("l_ready")
        e_done = sem("e_done")
        p_ready = sem("p_ready")
        pt_full = sem("pt_full")
        pt_ready = sem("pt_ready")
        y_full = sem("y_full")
        y_out = sem("y_out")
        m_ready = sem("m_ready")
        msq_done = sem("msq_done")
        mm_ready = sem("mm_ready")
        mr_ready = sem("mr_ready")
        memn_ready = sem("memn_ready")
        memt_full = sem("memt_full")
        memhi_ready = sem("memhi_ready")
        mem_ready = sem("mem_ready")
        ms_full = sem("ms_full")
        mmax_ready = sem("mmax_ready")
        mexp_done = sem("mexp_done")
        mp_ready = sem("mp_ready")
        mpt_full = sem("mpt_full")
        mpt_ready = sem("mpt_ready")
        mo_full = sem("mo_full")
        oshi_ready = sem("oshi_ready")
        os_ready = sem("os_ready")
        ht_full = sem("ht_full")
        ht_ready = sem("ht_ready")
        ot_full = sem("ot_full")
        ot_ready = sem("ot_ready")
        out_stored = sem("out_stored")

        def slot_of(n):
            return n % RING

        def of(n, per=0, i=None):
            return n if i is None else i * per + n

        def out_chunk(c):
            b, q = c % 2, c // 2
            return out[0, b * P:(b + 1) * P, q * 512:(q + 1) * 512]

        block = ctx.enter_context(nc.Block())

        @block.sync
        def _(sp):
            xv = a["x"].rearrange("o (b p) (q n) -> p (o b) q n", p=P, q=4)
            for q in range(4):
                sp.dma_start(xr[:, :, q * 512:(q + 1) * 512], xv[:, :, q, :]).then_inc(x_landed[q], 16)

            def load(n0, src, per=0, i=None):
                n = n0
                if n >= RING:
                    sp.wait_ge(lo_done, of(n - RING + 1, per, i))
                s = slot_of(n)
                if len(src.shape) == 4:
                    dst = raw[:, s, :].rearrange("p (k s n) -> p k s n", k=src.shape[1], s=2)
                    halves = [(dst[:, :, b, :], src[:, :, b, :]) for b in range(2)]
                else:
                    dst = raw[:, s, :].rearrange("p (k n) -> p k n", k=src.shape[1])
                    mid = src.shape[1] // 2
                    halves = [(dst[:, :mid, :], src[:, :mid, :]), (dst[:, mid:, :], src[:, mid:, :])]
                for to, frm in halves:
                    sp.dma_start(to, frm).then_inc(landed[s], 16)

            def columns(w, u, c, width=GT * P):
                return w[:, UK * u:UK * u + UK, bass.ds(c, width)]

            def two_columns(w, u, c):
                return w[:, UK * u:UK * u + UK, :, bass.ds(c, 2 * P)]

            def ffn(w13, w2, n13, n2):
                w13 = w13.rearrange("o (k p) (s n) -> p (o k) s n", p=P, s=2)
                w2 = w2.rearrange("o (k p) n -> p (o k) n", p=P)
                for u in range(U1):
                    load(n13 + u, two_columns(w13, u, 0))
                with sp.Fori(0, G1 - 1) as i:
                    for u in range(U1):
                        load(n13 + U1 + u, two_columns(w13, u, i * 256 + 256), U1, i)
                with sp.Fori(0, G2 // 2) as i:
                    for m in range(2):
                        for u in range(U2):
                            load(n2 + m * U2 + u, columns(w2, u, i * 1024 + m * 512), 2 * U2, i)

            ffn(a["ffn1_w13"], a["ffn1_w2"], F1A, F1B)

            w_in = a["w_in"].rearrange("o (k p) n -> p (o k) n", p=P)
            cx = 3 * D + H
            kinds = [(0, D), (2 * D, cx - 2 * D), (cx + D, D), (cx + 3 * D, D)]
            views = [w_in[:, :, c:c + 2 * step].rearrange("p k (s n) -> p k s n", s=2) for c, step in kinds]
            for j in range(UM):
                if j == 2 * U1:
                    for u in range(2):
                        load(MIX + 2 * U1 + u, w_in[:, 8 * u:8 * u + 8, 3 * D:3 * D + P])
                load(MIX + j + (2 if j >= 2 * U1 else 0), two_columns(views[j // U1], j % U1, 0))
            with sp.Fori(0, PAIRS - 1) as i:
                for j in range(UM):
                    load(MIX1 + j, two_columns(views[j // U1], j % U1, i * 256 + 256), UM, i)

            sp.wait_ge(w_used, MIX1)
            sp.dma_start(memr[:, :, :], a["mem"].rearrange("o (b p) n -> p (o b) n", p=P)).then_inc(mem_landed, 16)

            w_out = a["w_out"].rearrange("o (k p) n -> p (o k) n", p=P)
            w_mkv = a["w_mkv"].rearrange("o (k p) n -> p (o k) n", p=P)
            w_mq = a["w_mq"].rearrange("o (k p) n -> p (o k) n", p=P)
            w_mo = a["w_mo"].rearrange("o (k p) n -> p (o k) n", p=P)
            for j, (m, u) in enumerate(WO_ORDER):
                load(WO + j, columns(w_out, u, m * 512))
            for n0, w, c in ((MK, w_mkv, 0), (MQ, w_mq, 0), (MV, w_mkv, 512)):
                for u in range(U1):
                    load(n0 + u, columns(w, u, c))
            for u in range(G2 * UO):
                load(MO + u, columns(w_mo, u % UO, u // UO * 512))

            ffn(a["ffn2_w13"], a["ffn2_w2"], F2A, F2B)
            for c in range(0, 8, 2):
                sp.wait_ge(ot_ready, c + 1)
                sp.dma_start(out_chunk(c), ot[:, c, :]).then_inc(out_stored, 16)
            sp.wait_ge(out_stored, 8 * 16)

        @block.scalar
        def _(act):
            rows = [(n, "o (k p) -> (o k) p") for n in (
                "ffn1_pre_g", "ffn1_post_g", "mix_pre_g", "mix_post_g", "mem_q_pre_g", "mem_kv_g",
                "mem_post_g", "ffn2_pre_g", "ffn2_post_g")]
            rows += [("gate_bias", "o b (k p) -> (o b k) p"), ("conv_w", "o b (k p) -> (o b k) p"),
                     ("conv_b", "o (k p) -> (o k) p")]
            r = 0
            for name, how in rows:
                src = a[name].rearrange(how, p=P)
                n = src.shape[0]
                act.dma_start(prow[r % P:r % P + n, r // P, :], src).then_inc(par_landed, 16)
                r += n
            act.dma_start(fbias[:, :], a["forget_bias"].rearrange("o h -> h o")).then_inc(par_landed, 16)

            def unit(n0, per=0, i=None):
                s = slot_of(n0)
                act.wait_ge(landed[s], of(32 * (n0 // RING + 1), 32 * (per // RING), i))
                if n0 >= RING:
                    act.wait_ge(w_used, of(n0 - RING + 1, per, i))
                nc.scalar.copy(w_hi[:, s, :], raw[:, s, :]).then_inc(hi_done, 1)

            def units(n0, count):
                loops = count // RING
                if loops > 1:
                    with act.Fori(0, loops) as i:
                        for j in range(RING):
                            unit(n0 + j, RING, i)
                else:
                    loops = 0
                for j in range(loops * RING, count):
                    unit(n0 + j)

            def square_pair(norm, kp, src):
                c = norm * HP + kp
                if kp >= 2:
                    act.wait_ge(sq_added, added(norm, kp - 1))
                elif norm > 0:
                    act.wait_ge(sum_full, norm)
                nc.scalar.activation(sq[:, c % 2, :], src.rearrange("p k t -> p (k t)"), ACT.Square).then_inc(sq_ready, 1)

            def input_pair(base, norm, gain, kp):
                act.wait_ge(h_ready, base + kp + 1)
                if kp > 0 or norm == N_F1:
                    for k in (2 * kp, 2 * kp + 1):
                        ins = nc.scalar.activation(xs[:, k, 0, :], h[:, k, :], ACT.Copy, scale=par[:, gain + k:gain + k + 1])
                    ins.then_inc(xhi_ready, 1)
                square_pair(norm, kp, h[:, 2 * kp:2 * kp + 2, :])

            def input_and_units(base, norm, gain, n0, kp0=RING):
                for kp in range(HP):
                    if kp >= kp0:
                        unit(n0 + kp - kp0)
                    input_pair(base, norm, gain, kp)

            def branch_out(norm, grp, m):
                act.wait_ge(w_used, ENDS[grp])
                for c in range(2):
                    square_pair(norm, 2 * m + c, ps[:, grp % 2 * 2 + c, :].rearrange("p (k t) -> p k t", t=T))

            def next_and_branch_end(n0, norm, grp):
                unit(n0)
                unit(n0 + 1)
                unit(n0 + 2)
                branch_out(norm, grp, G2 - 1)
                unit(n0 + 3)

            def silu(ffn, grp0, per=0, i=None):
                n = ffn * G1 + grp0
                act.wait_ge(gate_in, of(n + 1, per, i))
                nc.scalar.activation(gt[:, :, :], gt[:, :, :], ACT.Silu).then_inc(silu_done, 1)

            def ffn(k, base, norm, gain, n13, n2, grp2):
                input_and_units(base, norm, gain, n13 + RING)
                for grp in range(1, 2):
                    for u in range(U1):
                        unit(n13 + U1 * grp + u)
                        if u == RING - 1:
                            silu(k, grp - 1)
                with act.Fori(0, G1 - 2) as i:
                    for u in range(U1):
                        unit(n13 + 2 * U1 + u, U1, i)
                        if u == RING - 1:
                            silu(k, 1, 1, i)
                for u in range(RING):
                    if u == RING - 1 and k == 1:
                        for c in range(8):
                            act.wait_ge(ht_full, c + 1)
                            nc.scalar.copy(ht[:, c, :], ps[:, 4 + c % 4, :]).then_inc(ht_ready, 1)
                    unit(n2 + u)
                silu(k, G1 - 1)
                for m in range(G2):
                    units(n2 + m * U2 + RING, U2 if m < G2 - 1 else U2 - RING)
                    if m < G2 - 1:
                        branch_out(norm + 1, grp2 + m, m)

            units(0, RING)
            act.wait_ge(par_ready, 1)
            ffn(0, 0, N_F1, C_F1PRE, F1A, F1B, F1B_G)

            next_and_branch_end(MIX, N_F1OUT, MIX_G - 1)

            def pair_starts(p):
                act.wait_ge(ncm_done, p + 1)
                nc.scalar.copy(cq[:, :, :], ctok[:, :, bass.ds(p * 2, 2)]).then_inc(cq_set, 1)
                act.dma_start(ncr[:, :, :], crow[:, bass.ds(p * 2, 2), :].broadcast_to([P, 2, T])).then_inc(ncr_landed, 16)

            def gates(p):
                act.wait_ge(grp_out, p * 4 + MIX1_G)
                act.wait_ge(prm_set, p + 1)
                for t in range(4):
                    ins = nc.scalar.activation(gat[:, t, :], gat[:, t, :], ACT.Exp,
                                               bias=prp[:, t % 2, 4 + t // 2:5 + t // 2], scale=-1.0)
                ins.then_inc(gat_exp, 1)

            def head_exp(p, hd):
                act.wait_ge(l_ready, p * 2 + hd + 1)
                nc.scalar.activation(lg[:, hd, 0:P], lg[:, hd, 0:P], ACT.Exp,
                                     bias=st[:, hd, 0:1], accum_out=st[:, hd, 2:3])
                nc.scalar.activation(lg[:, hd, P:3 * P], lg[:, hd, P:3 * P], ACT.Exp,
                                     bias=st[:, hd, 1:2], accum_out=st[:, hd, 3:4]).then_inc(e_done, 1)

            def pair_params(i):
                if not isinstance(i, int) or i > 0:
                    act.wait_ge(taps_done, i)
                nc.scalar.copy(prp[:, :, :], prm[:, bass.ds(i * 2, 2), :]).then_inc(prm_set, 1)

            input_and_units(HP, N_MIX, C_MIXPRE, MIX + RING)
            for j in range(U1, UM + 2):
                unit(MIX + j)
                if j == 22:
                    act.wait_ge(f_na, 1)
                    nc.scalar.activation(fz[:, 2, :], fz[:, 1, :], ACT.Exp).then_inc(f_e, 1)
                if j == 24:
                    act.wait_ge(f_y, 1)
                    nc.scalar.activation(fz[:, 4, :], fz[:, 3, :], ACT.Ln).then_inc(f_ln, 1)
                if j == 31:
                    act.wait_ge(f_c, 1)
                    act.dma_start(crow.rearrange("o h t -> (o h) t"), fz[:, 7, :]).then_inc(crow_stored, 16)
                if j == 22:
                    pair_params(0)

            def pair_body(i):
                for j in range(UM):
                    unit(MIX1 + j, UM, i)
                    if j == 0:
                        pair_starts(i)
                    if j == 4:
                        gates(i)
                    if j == 7:
                        head_exp(i, 0)
                    if j == 10:
                        head_exp(i, 1)
                    if j == 20:
                        pair_params(i + 1)

            act.wait_ge(crow_stored, 16)
            with act.Fori(0, PAIRS - 1) as i:
                pair_body(i)

            def memory_hi(j):
                if j in MEM_SPLIT:
                    kp = MEM_SPLIT.index(j)
                    act.wait_ge(memt_full, kp + 1)
                    for t in range(2):
                        k = 2 * kp + t
                        ins = nc.scalar.activation(mem[:, k, 0, :], ps[:, 5 + kp % 2, t * T:(t + 1) * T], ACT.Copy,
                                                   scale=par[:, C_MKV + k:C_MKV + k + 1])
                    ins.then_inc(memhi_ready, 1)

            for j in range(G2 * U1):
                unit(WO + j)
                if j == 0:
                    pair_starts(PAIRS - 1)
                if j == 4:
                    gates(PAIRS - 1)
                if j == 5:
                    head_exp(PAIRS - 1, 0)
                if j == 7:
                    head_exp(PAIRS - 1, 1)
                if j == 14:
                    act.wait_ge(m_ready, H + 1)
                    act.wait_ge(mem_landed, 16)
                    for b in range(2):
                        nc.scalar.activation(junk[:, b, :], memr[:, b, :], ACT.Square,
                                             accum_out=mst[:, b:b + 1]).then_inc(msq_done, 1)
                memory_hi(j)
                for m, after in enumerate((18, 20, 28)):
                    if j == after:
                        branch_out(N_MIXOUT, WO_G + m, m)

            next_and_branch_end(MK, N_MIXOUT, MK_G - 1)
            input_and_units(2 * HP, N_MQ, C_MQPRE, MK + RING, 0)
            for j in range(RING, U1):
                unit(MQ + j)

            def memory_exp(hd):
                act.wait_ge(mmax_ready, hd + 1)
                for b in range(2):
                    ins = nc.scalar.activation(ml[:, hd, b, :], ps[:, 4 + hd, b * T:(b + 1) * T], ACT.Exp,
                                               bias=mmx[:, hd, b:b + 1], scale=SCALE,
                                               accum_out=mmx[:, hd, 2 + b:3 + b])
                ins.then_inc(mexp_done, 1)

            for j in range(U1):
                unit(MV + j)
                if j >= 6:
                    memory_exp(2 * (j - 6))
                    memory_exp(2 * (j - 6) + 1)
            for j in range(RING):
                unit(MO + j)
            for hd in range(MH):
                act.wait_ge(mo_full, hd + 1)
                nc.scalar.copy(osp[:, hd, 0, :], ps[:, 4 + hd, 0:T]).then_inc(oshi_ready, 1)
            for j in range(RING, G2 * UO):
                unit(MO + j)
                if j % 2 == 1:
                    branch_out(N_MOUT, MO_G + (j - 5) // 2, (j - 5) // 2)
            branch_out(N_MOUT, MO_G + 2, 2)
            next_and_branch_end(F2A, N_MOUT, F2A_G - 1)
            ffn(1, 3 * HP, N_F2, C_F2PRE, F2A, F2B, F2B_G)
            branch_out(N_F2OUT, F2B_G + G2 - 1, G2 - 1)

            for c in range(1, 8, 2):
                act.wait_ge(ot_ready, c + 1)
                act.dma_start(out_chunk(c), ot[:, c, :]).then_inc(out_stored, 16)

        @block.vector
        def _(dve):
            own = Chain(dve, dve_own)

            def tile_tokens(r, n):
                return r[:, :].rearrange("p (o t) -> p o t", o=1).broadcast_to([P, n, T])

            def banks(grp, b=0, n=2):
                first = grp % 2 * 2 + b
                return ps[:, first:first + n, :].rearrange("p b (m t) -> p (b m) t", t=T)

            def unit(n0, per=0, i=None):
                s = slot_of(n0)
                dve.wait_ge(hi_done, of(n0 + 1, per, i))
                nc.vector.tensor_tensor(w_lo[:, s, :], raw[:, s, :], w_hi[:, s, :].bitcast(F32),
                                        ALU.subtract).then_inc(lo_done, 1)

            def units(n0, count):
                loops = count // RING
                if loops > 1:
                    with dve.Fori(0, loops) as i:
                        for j in range(RING):
                            unit(n0 + j, RING, i)
                else:
                    loops = 0
                for j in range(loops * RING, count):
                    unit(n0 + j)

            def group_done(grp, per=0, i=None):
                dve.wait_ge(w_used, of(ENDS[grp], per * U1, i))

            def mean(norm, weight=1.0):
                dve.wait_ge(sum_full, norm + 1)
                nc.vector.tensor_scalar(ms[:, :], ps[:, B_NORM, 0:2], 1.0 / (D * weight * weight),
                                        EPS / (weight * weight), ALU.mult, ALU.add).then_inc(ms_ready, 1)

            def spread(norm):
                dve.wait_ge(r_ready, norm + 1)
                for b in range(2):
                    ins = nc.vector.tensor_scalar(diag[:, b, :], ident[:, :], rtok[:, b:b + 1], None, ALU.mult)
                ins.then_inc(diag_ready, 1)
                dve.wait_ge(r_full, norm + 1)
                nc.vector.tensor_copy((r_out if norm % 2 else r_in)[:, :], ps[:, B_NORM, T:2 * T]).then_inc(r_set, 1)
                dve.wait_ge(r_set, norm + 1)

            def input_lo(base, gain, kp):
                dve.wait_ge(xhi_ready, base - base // HP + kp + 1)
                for k in (2 * kp, 2 * kp + 1):
                    ins = nc.vector.scalar_tensor_tensor(
                        out=xs[:, k, 1, :], in0=h[:, k, :], scalar=par[:, gain + k:gain + k + 1],
                        in1=xs[:, k, 0, :].bitcast(F32), op0=ALU.mult, op1=ALU.subtract)
                ins.then_inc(x_ready, 1)

            def branch_tiles(gain, norm, grp, m):
                dve.wait_ge(sq_ready, norm * HP + 2 * m + 2)
                for t in range(4):
                    k = 4 * m + t
                    ins = nc.vector.tensor_scalar(f[:, k, :], banks(grp)[:, t, :], par[:, gain + k:gain + k + 1], None, ALU.mult)
                ins.then_inc(grp_out, 1)

            def branch_norm(kp):
                nc.vector.tensor_tensor(f[:, 2 * kp:2 * kp + 2, :], f[:, 2 * kp:2 * kp + 2, :],
                                        tile_tokens(r_out, 2), ALU.mult).then_inc(t_ready, 1)

            def branch_end(gain, norm, grp, weight=1.0):
                dve.wait_ge(sq_ready, (norm + 1) * HP)
                own.step(nc.vector.tensor_tensor(sq[:, 0, :], sq[:, 0, :], sq[:, 1, :], ALU.add))
                own.settle()
                nc.vector.tensor_tensor(sq[:, 0, 0:T], sq[:, 0, 0:T], sq[:, 0, T:2 * T], ALU.add).then_inc(sq_folded, 1)
                branch_tiles(gain, norm, grp, G2 - 1)
                mean(norm, weight)
                dve.wait_ge(grp_out, grp + 1)

            def first_pair(base, norm, gain):
                for k in range(2):
                    own.step(nc.vector.tensor_tensor(f[:, k, :], f[:, k, :], r_out[:, :], ALU.mult))
                    own.settle()
                    add = nc.vector.tensor_tensor(h[:, k, :], h[:, k, :], f[:, k, :], ALU.add)
                    if k == 0:
                        own.step(add)
                        own.settle()
                    else:
                        add.then_inc(h_ready, 1)
                        dve.wait_ge(h_ready, base + 1)
                    own.step(nc.vector.tensor_scalar(xs[:, k, 0, :], h[:, k, :], par[:, gain + k:gain + k + 1], None, ALU.mult))
                    own.settle()
                    nc.vector.scalar_tensor_tensor(
                        out=xs[:, k, 1, :], in0=h[:, k, :], scalar=par[:, gain + k:gain + k + 1],
                        in1=xs[:, k, 0, :].bitcast(F32), op0=ALU.mult, op1=ALU.subtract).then_inc(x_ready if k else x0_ready, 1)

            def next_input(norm, gain, n0, kp0=RING):
                spread(norm)
                base = (norm + 1) // 2 * HP
                first_pair(base, norm, gain)
                branch_norm(1)
                for kp in range(HP):
                    if 0 < kp < HP - 1:
                        branch_norm(kp + 1)
                    if kp >= kp0:
                        unit(n0 + kp - kp0)
                    if kp > 0:
                        input_lo(base, gain, kp)

            def gate_up_out(k, grp, par_grp, per=0, i=None):
                group_done(grp, per, i)
                nc.vector.tensor_tensor(gt[:, :, :], banks(par_grp, 0, 1), tile_tokens(r_in, 2), ALU.mult).then_inc(gate_in, 1)
                nc.vector.tensor_tensor(up[:, :, :], banks(par_grp, 1, 1), tile_tokens(r_in, 2), ALU.mult).then_inc(grp_out, 1)

            def gate_times_up(k, grp, n, per=0, i=None):
                dve.wait_ge(silu_done, of(k * G1 + n + 1, per, i))
                dve.wait_ge(grp_out, of(grp + 1, per, i))
                own.step(nc.vector.tensor_tensor(up[:, :, :], gt[:, :, :], up[:, :, :], ALU.mult))
                own.settle()
                where = bass.ds(2 * n if i is None else i * (2 * per) + 2 * n, 2)
                own.step(nc.vector.tensor_copy(g[:, where, 0, :], up[:, :, :]))
                own.settle()
                nc.vector.tensor_tensor(g[:, where, 1, :], up[:, :, :], g[:, where, 0, :].bitcast(F32),
                                        ALU.subtract).then_inc(g_ready, 1)

            def ffn(k, norm, post, n13, grp13, n2, grp2):
                for j in range(U1, 2 * U1):
                    unit(n13 + j)
                    if j == U1 + 3:
                        mean(norm)
                        spread(norm)
                        gate_up_out(k, grp13, grp13)
                    if j == U1 + 4:
                        gate_times_up(k, grp13, 0)
                with dve.Fori(0, (G1 - 2) // 2) as i:
                    own.enter(i, 4)
                    for j in range(2 * U1):
                        unit(n13 + 2 * U1 + j, 2 * U1, i)
                        b = 1 + j // U1
                        if j % U1 == 3:
                            gate_up_out(k, grp13 + b, grp13 + b, 2, i)
                        if j % U1 == 4:
                            gate_times_up(k, grp13 + b, b, 2, i)
                own.leave((G1 - 2) // 2)
                for j in range(RING):
                    unit(n2 + j)
                gate_up_out(k, grp2 - 1, grp2 - 1)
                gate_times_up(k, grp2 - 1, G1 - 1)
                for m in range(G2):
                    units(n2 + m * U2 + RING, U2 if m < G2 - 1 else U2 - RING)
                    if m < G2 - 1:
                        branch_tiles(post, norm + 1, grp2 + m, m)

            def next_and_branch_end(n0, gain, norm, grp, weight=1.0):
                unit(n0)
                unit(n0 + 1)
                unit(n0 + 2)
                branch_end(gain, norm, grp, weight)
                unit(n0 + 3)

            nc.vector.memset(tri1[:, :], 1.0).then_inc(consts_set, 1)
            nc.vector.memset(mhalf[:, :], -0.5).then_inc(consts_set, 1)
            dve.sem_inc(ncm_done, 1)
            dve.sem_inc(m_ready, 1)
            dve.wait_ge(par_t, 1)
            nc.vector.tensor_copy(par[:, 0:P], ps[:, 0, 0:P])
            own.step(nc.vector.tensor_copy(par[:, P:NPAR], ps[:, 1, 0:NPAR - P]))
            own.settle()
            nc.vector.tensor_copy(prm[:, :, 0:4].rearrange("p k f -> p f k"),
                                  par[:, C_CW:NPAR].rearrange("p (f k) -> p f k", f=4))
            nc.vector.tensor_scalar(prm[:, :, 4:6].rearrange("p k f -> p f k"),
                                    par[:, C_GB:C_CW].rearrange("p (f k) -> p f k", f=2),
                                    -1.0, None, ALU.mult).then_inc(par_ready, 1)
            for j in range(RING):
                unit(F1A + j)

            def x_pair(kp):
                dve.wait_ge(xt_full, kp + 1)
                nc.vector.tensor_copy(h[:, 2 * kp:2 * kp + 2, :].rearrange("p k t -> p (k t)"),
                                      ps[:, 4 + kp % 4, :]).then_inc(h_ready, 1)

            x_pair(0)
            for kp in range(HP):
                if kp + 1 < HP:
                    x_pair(kp + 1)
                if kp >= RING:
                    unit(F1A + kp)
                input_lo(0, C_F1PRE, kp)
            ffn(0, N_F1, C_F1POST, F1A, F1A_G, F1B, F1B_G)

            next_and_branch_end(MIX, C_F1POST, N_F1OUT, MIX_G - 1, 0.5)
            next_input(N_F1OUT, C_MIXPRE, MIX + RING)

            def pair_qk(p, grp, par_grp, per=0, i=None):
                group_done(grp, per, i)
                nc.vector.tensor_tensor(qk[:, :, :], banks(par_grp), tile_tokens(r_in, 4), ALU.mult).then_inc(grp_out, 1)

            def pair_vc(p, grp, par_grp, per=0, i=None):
                group_done(grp, per, i)
                nc.vector.tensor_tensor(vc[:, :, :], banks(par_grp), tile_tokens(r_in, 4), ALU.mult).then_inc(grp_out, 1)

            def pair_vtok(p):
                dve.wait_ge(vt_full, p + 1)
                nc.vector.tensor_copy(vtok[:, :, :, :].rearrange("p a b d -> p (a b d)"), ps[:, B_Y, :]).then_inc(vtok_ready, 1)

            def pair_bc(p, grp, par_grp, per=0, i=None):
                group_done(grp, per, i)
                if i is not None:
                    dve.wait_ge(ycb_done, p)
                nc.vector.tensor_tensor(bc[:, :, :], banks(par_grp), tile_tokens(r_in, 4), ALU.mult).then_inc(grp_out, 1)

            def pair_taps(p):
                dve.wait_ge(z_ready, p + 1)
                dve.wait_ge(prm_set, p + 1)
                for t in range(2):
                    ins = nc.vector.tensor_scalar(yc[:, t, :], zp[:, t, 0:T], prp[:, t, 0:1], prp[:, t, 3:4], ALU.mult, ALU.add)
                own.step(ins)
                own.settle()
                for tap in (1, 2):
                    for t in range(2):
                        ins = nc.vector.scalar_tensor_tensor(out=yc[:, t, :], in0=zp[:, t, tap:tap + T], scalar=prp[:, t, tap:tap + 1],
                                                             in1=yc[:, t, :], op0=ALU.mult, op1=ALU.add)
                    if tap == 1:
                        own.step(ins)
                        own.settle()
                ins.then_inc(taps_done, 1)

            def pair_gates(p, grp, par_grp, per=0, i=None):
                group_done(grp, per, i)
                nc.vector.tensor_tensor(gat[:, :, :], banks(par_grp), tile_tokens(r_in, 4), ALU.mult)                    .then_inc(grp_out, 1)

            def pair_sigmoid(p, t):
                dve.wait_ge(gat_exp, p + 1)
                own.step(nc.vector.tensor_scalar(gat[:, t, :], gat[:, t, :], 1.0, None, ALU.add))
                own.settle()
                nc.vector.reciprocal(gat[:, t, :], gat[:, t, :]).then_inc(sig_ready, 1)

            def pair_decay(p):
                dve.wait_ge(ncr_landed, p * 16 + 16)
                dve.wait_ge(cq_set, p + 1)
                for hd in range(2):
                    nc.vector.scalar_tensor_tensor(out=ncm[:, hd, 0:P], in0=ncr[:, hd, 0:P], scalar=cq[:, 0, hd:hd + 1],
                                                   in1=mask[:, :], op0=ALU.add, op1=ALU.add)
                    nc.vector.tensor_scalar(ncm[:, hd, P:2 * P], ncr[:, hd, 0:P], cq[:, 1, hd:hd + 1], None, ALU.add)
                    ins = nc.vector.scalar_tensor_tensor(out=ncm[:, hd, 2 * P:3 * P], in0=ncr[:, hd, P:T], scalar=cq[:, 1, hd:hd + 1],
                                                         in1=mask[:, :], op0=ALU.add, op1=ALU.add)
                ins.then_inc(ncm_done, 1)

            def head_logits(p, hd):
                dve.wait_ge(s_full, p * 2 + hd + 1)
                dve.wait_ge(ncm_done, p + 2)
                own.step(nc.vector.scalar_tensor_tensor(out=lg[:, hd, :], in0=ps[:, B_SCORE[hd], 0:3 * P], scalar=SCALE,
                                                        in1=ncm[:, hd, :], op0=ALU.mult, op1=ALU.add))
                own.settle()
                nc.vector.reduce_max(st[:, hd, 0:1], lg[:, hd, 0:P], AX_X)
                own.step(nc.vector.reduce_max(st[:, hd, 1:2], lg[:, hd, P:3 * P], AX_X))
                own.settle()
                nc.vector.tensor_scalar(st[:, hd, 0:2], st[:, hd, 0:2], -1.0, None, ALU.mult).then_inc(l_ready, 1)

            def head_probs(p, hd):
                dve.wait_ge(e_done, p * 2 + hd + 1)
                own.step(nc.vector.reciprocal(st[:, hd, 4:6], st[:, hd, 2:4]))
                own.settle()
                nc.vector.tensor_scalar(lg[:, hd, 0:P], lg[:, hd, 0:P], st[:, hd, 4:5], None, ALU.mult)
                nc.vector.tensor_scalar(lg[:, hd, P:3 * P], lg[:, hd, P:3 * P], st[:, hd, 5:6], None, ALU.mult).then_inc(p_ready, 1)

            def head_pt(p, hd):
                dve.wait_ge(pt_full, p * 2 + hd + 1)
                nc.vector.tensor_copy(pt[:, hd, :], ps[:, B_PT, 0:3 * P]).then_inc(pt_ready, 1)

            def head_merge(p, hd):
                dve.wait_ge(y_full, p * 2 + hd + 1)
                dve.wait_ge(sig_ready, p * 4 + 4)
                dve.wait_ge(m_ready, p * 2 + hd + 1)
                nc.vector.tensor_tensor(mg[:, :], ps[:, B_Y, 0:T], gat[:, hd, :], ALU.mult).then_inc(y_out, 1)
                dve.wait_ge(ymix_ready, p + 1)
                dve.wait_ge(y_out, p * 2 + hd + 1)
                own.step(nc.vector.tensor_tensor(mg[:, :], mg[:, :], yc[:, hd, :], ALU.add))
                own.settle()
                k = bass.ds(p * 2 + hd, 1)
                mgt = mg[:, :].rearrange("p (o t) -> p o t", o=1)
                own.step(nc.vector.tensor_copy(mrg[:, k, 0, :], mgt))
                own.settle()
                nc.vector.tensor_tensor(mrg[:, k, 1, :], mgt, mrg[:, k, 0, :].bitcast(F32), ALU.subtract).then_inc(m_ready, 1)

            for j in range(U1, UM + 2):
                unit(MIX + j)
                if j == 11:
                    mean(N_MIX)
                    spread(N_MIX)
                    pair_qk(0, MIX_G, MIX_G)
                if j == 21:
                    group_done(MIX_G + 2)
                    own.step(nc.vector.tensor_tensor(fz[:, 0, :], ps[0:H, (MIX_G + 2) % 2 * 2, 0:T], r_in[0:H, :], ALU.mult))
                    own.settle()
                    dve.wait_ge(par_landed, 13 * 16)
                    own.step(nc.vector.tensor_scalar(fz[:, 0, :], fz[:, 0, :], fbias[:, 0:1], None, ALU.add))
                    own.settle()
                    own.step(nc.vector.tensor_scalar(fz[:, 1, :], fz[:, 0, :], -1.0, None, ALU.mult))
                    own.settle()
                    nc.vector.tensor_tensor(fz[:, 1, :], fz[:, 0, :], fz[:, 1, :], ALU.min).then_inc(f_na, 1)
                    nc.vector.tensor_scalar(fz[:, 5, :], fz[:, 0, :], 0.0, None, ALU.min).then_inc(grp_out, 1)
                if j == 23:
                    dve.wait_ge(f_e, 1)
                    nc.vector.tensor_scalar(fz[:, 3, :], fz[:, 2, :], 1.0, None, ALU.add).then_inc(f_y, 1)
                    dve.wait_ge(f_y, 1)
                    nc.vector.scalar_tensor_tensor(out=fz[:, 6, :], in0=fz[:, 3, :], scalar=-1.0, in1=fz[:, 2, :],
                                                   op0=ALU.add, op1=ALU.subtract)
                    own.step(nc.vector.reciprocal(fz[:, 7, :], fz[:, 3, :]))
                    own.settle()
                if j == 25:
                    dve.wait_ge(f_ln, 1)
                    own.step(nc.vector.tensor_tensor(fz[:, 6, :], fz[:, 6, :], fz[:, 7, :], ALU.mult))
                    own.step(nc.vector.tensor_tensor(fz[:, 5, :], fz[:, 5, :], fz[:, 4, :], ALU.subtract))
                    own.settle()
                    nc.vector.tensor_tensor(fz[:, 5, :], fz[:, 5, :], fz[:, 6, :], ALU.add).then_inc(f_log, 1)
                if j == 27:
                    dve.wait_ge(f_tok, 1)
                    nc.vector.tensor_copy(ftok[:, :, :], ps[:, B_S, 0:2 * H].rearrange("p (b h) -> p b h", h=H)).then_inc(f_tokc, 1)
                if j == 19:
                    pair_vc(0, MIX_G + 1, MIX_G + 1)
                if j == 29:
                    dve.wait_ge(f_cum, 1)
                    nc.vector.tensor_copy(ctok[:, :, :], ps[:, B_PT, 0:2 * H].rearrange("p (b h) -> p b h", h=H))
                    nc.vector.tensor_scalar(fz[:, 7, :], ps[0:H, B_PT, T:2 * T], -1.0, None, ALU.mult).then_inc(f_c, 1)
                if j == 23:
                    pair_vtok(0)
                if j == 29:
                    pair_bc(0, MIX_G + 3, MIX_G + 3)
                if j == 31:
                    pair_taps(0)
            dve.wait_ge(taps_done, 1)

            with dve.Fori(0, PAIRS - 1) as i:
                own.enter(i, 16)
                for j in range(UM):
                    unit(MIX1 + j, UM, i)
                    if j == 3:
                        pair_gates(i, MIX1_G - 1, MIX1_G - 1, 4, i)
                    if j == 4:
                        pair_decay(i)
                    if j in SIGMOIDS:
                        pair_sigmoid(i, SIGMOIDS.index(j))
                    if j == 6:
                        head_logits(i, 0)
                    if j == 8:
                        head_probs(i, 0)
                    if j == 9:
                        head_logits(i, 1)
                    if j == 11:
                        head_pt(i, 0)
                        pair_qk(i + 1, MIX1_G, MIX1_G, 4, i)
                    if j == 12:
                        head_probs(i, 1)
                    if j == 14:
                        head_merge(i, 0)
                    if j == 15:
                        head_pt(i, 1)
                    if j == 18:
                        head_merge(i, 1)
                    if j == 19:
                        pair_vc(i + 1, MIX1_G + 1, MIX1_G + 1, 4, i)
                    if j == 23:
                        pair_vtok(i + 1)
                    if j == 27:
                        pair_bc(i + 1, MIX1_G + 2, MIX1_G + 2, 4, i)
                    if j == 29:
                        pair_taps(i + 1)
            own.leave(PAIRS - 1)

            def memory_lo(j):
                if j in MEM_SPLIT:
                    kp = MEM_SPLIT.index(j)
                    dve.wait_ge(memhi_ready, kp + 1)
                    for t in range(2):
                        k = 2 * kp + t
                        ins = nc.vector.scalar_tensor_tensor(
                            out=mem[:, k, 1, :], in0=ps[:, 5 + kp % 2, t * T:(t + 1) * T], scalar=par[:, C_MKV + k:C_MKV + k + 1],
                            in1=mem[:, k, 0, :].bitcast(F32), op0=ALU.mult, op1=ALU.subtract)
                    ins.then_inc(mem_ready, 1)

            last = PAIRS - 1
            for j in range(G2 * U1):
                unit(WO + j)
                if j == 3:
                    pair_gates(last, WO_G - 1, WO_G - 1)
                    pair_decay(last)
                if j == 4:
                    head_logits(last, 0)
                if j in SIGMOIDS:
                    pair_sigmoid(last, SIGMOIDS.index(j))
                if j == 6:
                    head_logits(last, 1)
                if j == 7:
                    head_probs(last, 0)
                if j == 8:
                    head_probs(last, 1)
                if j == 9:
                    head_pt(last, 0)
                if j == 11:
                    head_pt(last, 1)
                    head_merge(last, 0)
                if j == 13:
                    head_merge(last, 1)
                if j == 15:
                    dve.wait_ge(msq_done, 2)
                    nc.vector.tensor_scalar(mst[:, 2:4], mst[:, 0:2], 1.0 / D, EPS, ALU.mult, ALU.add).then_inc(mm_ready, 1)
                if j in (16, 18):
                    b = (j - 16) // 2
                    dve.wait_ge(mr_ready, 1)
                    nc.vector.tensor_scalar(memr[:, b, :], memr[:, b, :], mst[:, 4 + b:5 + b], None, ALU.mult).then_inc(memn_ready, 1)
                memory_lo(j)
                for m, after in enumerate((17, 19, 27)):
                    if j == after:
                        branch_tiles(C_MIXPOST, N_MIXOUT, WO_G + m, m)

            next_and_branch_end(MK, C_MIXPOST, N_MIXOUT, MK_G - 1)
            next_input(N_MIXOUT, C_MQPRE, MK + RING, 0)
            group_done(MK_G)
            nc.vector.tensor_copy(kt[:, :, :], banks(MK_G)).then_inc(grp_out, 1)
            for j in range(RING, U1):
                unit(MQ + j)

            def memory_max(hd):
                dve.wait_ge(ms_full, hd + 1)
                own.step(nc.vector.reduce_max(mmx[:, hd, 0:2], ps[:, 4 + hd, :].rearrange("p (b k) -> p b k", b=2), AX_X))
                own.settle()
                nc.vector.tensor_scalar(mmx[:, hd, 0:2], mmx[:, hd, 0:2], -SCALE, None, ALU.mult).then_inc(mmax_ready, 1)

            def memory_probs(hd):
                dve.wait_ge(mexp_done, hd + 1)
                own.step(nc.vector.reciprocal(mmx[:, hd, 4:6], mmx[:, hd, 2:4]))
                own.settle()
                for b in range(2):
                    ins = nc.vector.tensor_scalar(ml[:, hd, b, :], ml[:, hd, b, :], mmx[:, hd, 4 + b:5 + b], None, ALU.mult)
                ins.then_inc(mp_ready, 1)

            def memory_pt(hd):
                dve.wait_ge(mpt_full, hd + 1)
                nc.vector.tensor_copy(mpt[:, hd, :, :].rearrange("p b t -> p (b t)"), ps[:, 4 + hd, :]).then_inc(mpt_ready, 1)

            for j in range(U1 + RING):
                if j == U1 + RING - 1:
                    group_done(MV_G)
                    nc.vector.tensor_copy(mvtok[:, :, :, :].rearrange("p m b d -> p b m d"),
                                          ps[:, MV_G % 2 * 2:MV_G % 2 * 2 + 2, :].rearrange("p b (m d) -> p b m d", d=P)).then_inc(grp_out, 1)
                unit(MV + j)
                if j == 0:
                    mean(N_MQ)
                    spread(N_MQ)
                if j == 3:
                    group_done(MQ_G)
                    nc.vector.tensor_tensor(qt[:, :, :], banks(MQ_G), tile_tokens(r_in, MH), ALU.mult).then_inc(grp_out, 1)
                for step, first in ((memory_max, 5), (memory_probs, 7), (memory_pt, 9)):
                    if first <= j < first + 2:
                        step(2 * (j - first))
                        step(2 * (j - first) + 1)
            for hd in range(MH):
                dve.wait_ge(oshi_ready, hd + 1)
                nc.vector.tensor_tensor(osp[:, hd, 1, :], ps[:, 4 + hd, 0:T], osp[:, hd, 0, :].bitcast(F32), ALU.subtract).then_inc(os_ready, 1)
            for j in range(RING, G2 * UO):
                unit(MO + j)
                if j % 2 == 1:
                    branch_tiles(C_MPOST, N_MOUT, MO_G + (j - 5) // 2, (j - 5) // 2)
            branch_tiles(C_MPOST, N_MOUT, MO_G + 2, 2)
            next_and_branch_end(F2A, C_MPOST, N_MOUT, F2A_G - 1)
            next_input(N_MOUT, C_F2PRE, F2A + RING)
            ffn(1, N_F2, C_F2POST, F2A, F2A_G, F2B, F2B_G)

            branch_end(C_F2POST, N_F2OUT, F2B_G + G2 - 1, 0.5)
            dve.wait_ge(r_ready, N_F2OUT + 1)
            dve.wait_ge(ht_ready, 8)
            for c in range(8):
                dve.wait_ge(ot_full, c + 1)
                nc.vector.scalar_tensor_tensor(out=ot[:, c, :], in0=ps[:, OUT_BANKS[c], :], scalar=rtok[:, c % 2:c % 2 + 1],
                                               in1=ht[:, c, :], op0=ALU.mult, op1=ALU.add).then_inc(ot_ready, 1)

        @block.gpsimd
        def _(pool):
            own = Chain(pool, pool_own)
            own.step(nc.gpsimd.memset(ident[:, :], 0.0))
            own.step(nc.gpsimd.memset(mask[:, :], 0.0))
            own.settle()
            nc.gpsimd.affine_select(out=ident[:, :], in_=ident[:, :], compare_op=ALU.not_equal, fill=1.0, base=0,
                                    pattern=[[-1, P]], channel_multiplier=1).then_inc(ident_set, 1)
            nc.gpsimd.affine_select(out=mask[:, :], in_=mask[:, :], compare_op=ALU.is_ge, fill=NEG, base=0,
                                    pattern=[[-1, P]], channel_multiplier=1)
            pool.wait_ge(consts_set, 2)
            nc.gpsimd.affine_select(out=tri1[:, 0:P], in_=tri1[:, 0:P], compare_op=ALU.is_ge, fill=0.0, base=0,
                                    pattern=[[1, P]], channel_multiplier=-1).then_inc(ident_set, 1)

            def add_squares(norm, kp):
                c = norm * HP + kp
                pool.wait_ge(sq_ready, c + 1)
                if kp == 0:
                    if norm > 0:
                        pool.wait_ge(sum_full, norm)
                    ins = nc.gpsimd.tensor_copy(sqsum[:, :], sq[:, c % 2, :])
                else:
                    pool.wait_ge(sq_added, added(norm, kp))
                    ins = nc.gpsimd.tensor_tensor(sqsum[:, :], sqsum[:, :], sq[:, c % 2, :], ALU.add)
                ins.then_inc(sq_added, 1)

            def inverse_rms(norm):
                pool.wait_ge(ms_ready, norm + 1)
                nc.gpsimd.tensor_tensor(rtok[:, :], ms[:, :], mhalf[:, :], ALU.pow).then_inc(r_ready, 1)

            def update(n, kp):
                pool.wait_ge(t_ready, n * (HP - 1) + kp)
                if kp == 1:
                    pool.wait_ge(h_ready, (n + 1) * HP + 1)
                nc.gpsimd.tensor_tensor(h[:, 2 * kp:2 * kp + 2, :], h[:, 2 * kp:2 * kp + 2, :],
                                        f[:, 2 * kp:2 * kp + 2, :], ALU.add).then_inc(h_ready, 1)

            def branch_and_input(n, norm):
                for kp in range(HP - 2):
                    add_squares(norm, kp)
                inverse_rms(norm)
                if norm < N_F2OUT:
                    for kp in range(HP):
                        if kp + 1 < HP:
                            update(n, kp + 1)
                        add_squares(norm + 1, kp)
                    inverse_rms(norm + 1)

            for kp in range(HP):
                add_squares(N_F1, kp)
            inverse_rms(N_F1)
            branch_and_input(0, N_F1OUT)

            def pair_conv(p, grp_done):
                grp_done()
                if not isinstance(p, int):
                    pool.wait_ge(taps_done, p)
                nc.gpsimd.tensor_tensor(zp[:, :, 2:T + 2], bc[:, 2:4, :], vc[:, 2:4, :], ALU.mult).then_inc(z_ready, 1)
                pool.wait_ge(taps_done, p + 1)
                nc.gpsimd.tensor_tensor(yc[:, :, :], yc[:, :, :], bc[:, 0:2, :], ALU.mult).then_inc(ycb_done, 1)

            def pair_conv_gate(p):
                pool.wait_ge(sig_ready, p * 4 + 4)
                pool.wait_ge(ycb_done, p + 1)
                nc.gpsimd.tensor_tensor(yc[:, :, :], yc[:, :, :], gat[:, 2:4, :], ALU.mult).then_inc(ymix_ready, 1)

            own.step(nc.gpsimd.memset(zp[:, :, 0:2], 0.0))
            own.settle()
            pair_conv(0, lambda: pool.wait_ge(grp_out, MIX_G + 4))
            with pool.Fori(0, PAIRS - 1) as i:
                pair_conv_gate(i)
                pair_conv(i + 1, lambda: pool.wait_ge(grp_out, i * 4 + MIX1_G + 3))
            pair_conv_gate(PAIRS - 1)

            pool.wait_ge(mm_ready, 1)
            nc.gpsimd.tensor_tensor(mst[:, 4:6], mst[:, 2:4], mhalf[:, 0:2], ALU.pow).then_inc(mr_ready, 1)
            branch_and_input(1, N_MIXOUT)
            branch_and_input(2, N_MOUT)
            branch_and_input(3, N_F2OUT)

        @block.tensor
        def _(pe):
            def product(n0, grp, x, k0, first=False, last=False, ready=None, per=0, i=None, grp_per=0, ready0=None):
                s = slot_of(n0)
                pe.wait_ge(lo_done, of(n0 + 1, per, i))
                if ready is not None:
                    pe.wait_ge(*(ready0 or ready))
                if first and grp >= 2:
                    pe.wait_ge(grp_out, of(grp - 1, grp_per, i))
                for kk in range(UK):
                    if kk == 1 and ready0 is not None:
                        pe.wait_ge(*ready)
                    for m in range(GT):
                        c = (kk * GT + m) * P
                        o = ps[:, grp % 2 * 2 + m // 2, m % 2 * T:m % 2 * T + T]
                        hi, lo = w_hi[:, s, c:c + P], w_lo[:, s, c:c + P]
                        nc.tensor.matmul(o, hi, x[:, k0 + kk, 0, :], start=first and kk == 0 and m % 2 == 0,
                                         stop=False, skip_group_check=True)
                        nc.tensor.matmul(o, hi, x[:, k0 + kk, 1, :], start=False, stop=False, skip_group_check=True)
                        ins = nc.tensor.matmul(o, lo, x[:, k0 + kk, 0, :], start=False,
                                               stop=last and kk == UK - 1, skip_group_check=True)
                return ins

            def unit(n0, grp, x, k0, units=U1, ready=None, per=0, i=None, grp_per=0, ready0=None):
                last = k0 == UK * (units - 1)
                ins = product(n0, grp, x, k0, k0 == 0, last, ready, per, i, grp_per, ready0)
                ins.then_inc(w_used, 1)

            def sums(norm):
                pe.wait_ge(sq_added, added(norm, HP))
                if norm > 0:
                    pe.wait_ge(r_set, norm)
                for t in range(2):
                    for b in range(2):
                        c = t * T + b * P
                        ins = nc.tensor.matmul(ps[:, B_NORM, b:b + 1], sqsum[:, c:c + P], ones[:, 0:1],
                                               start=t == 0 and b == 0, stop=t == 1, skip_group_check=True)
                ins.then_inc(sum_full, 1)

            def branch_sums(norm, between=None):
                pe.wait_ge(sq_added, added(norm, HP - 2))
                pe.wait_ge(r_set, norm)
                for t in range(2):
                    for b in range(2):
                        c = t * T + b * P
                        nc.tensor.matmul(ps[:, B_NORM, b:b + 1], sqsum[:, c:c + P], ones[:, 0:1],
                                         start=t == 0 and b == 0, stop=False, skip_group_check=True)
                if between is not None:
                    between()
                pe.wait_ge(sq_folded, (norm + 1) // 2)
                for b in range(2):
                    ins = nc.tensor.matmul(ps[:, B_NORM, b:b + 1], sq[:, 0, b * P:(b + 1) * P], ones[:, 0:1],
                                           start=False, stop=True, skip_group_check=True)
                ins.then_inc(sum_full, 1)

            def spread(norm):
                pe.wait_ge(diag_ready, norm + 1)
                for b in range(2):
                    ins = nc.tensor.matmul(ps[:, B_NORM, T + b * P:T + (b + 1) * P], ones, diag[:, b, :],
                                           start=True, stop=True)
                ins.then_inc(r_full, 1)

            def transpose_chunk(src, c, bank, done):
                b, q = c % 2, c // 2
                for t in range(4):
                    ins = nc.tensor.transpose(ps[:, bank, t * P:(t + 1) * P], src[:, 4 * q + t, b * P:(b + 1) * P], ident[:, :])
                ins.then_inc(done, 1)

            def ffn(k, base, norm, n13, grp13, n2, grp2):
                for b in range(2):
                    for u in range(U1):
                        unit(n13 + b * U1 + u, grp13 + b, xs, UK * u, ready=(x_ready, base + u + 1) if b == 0 else None,
                             ready0=(x0_ready, 3) if k == 1 and b + u == 0 else None)
                        if b == 1 and u == 0:
                            sums(norm)
                        if b == 1 and u == 1:
                            spread(norm)
                with pe.Fori(0, (G1 - 2) // 2) as i:
                    for b in range(2):
                        for u in range(U1):
                            unit(n13 + (2 + b) * U1 + u, grp13 + 2 + b, xs, UK * u, per=2 * U1, i=i, grp_per=2)
                if k == 1:
                    for c in range(8):
                        if c >= 4:
                            pe.wait_ge(ht_ready, c - 3)
                        transpose_chunk(h, c, 4 + c % 4, ht_full)
                with pe.Fori(0, G2 // 2) as i:
                    for b in range(2):
                        for u in range(U2):
                            unit(n2 + b * U2 + u, grp2 + b, g, UK * u, U2, (g_ready, k * G1 + u + 1) if b == 0 else None,
                                 2 * U2, i, 2)

            pe.wait_ge(ident_set, 2)
            pe.wait_ge(par_landed, 13 * 16)
            nc.tensor.transpose(ps[:, 0, 0:P], prow[:, 0, :], ident[:, :])
            nc.tensor.transpose(ps[:, 1, 0:NPAR - P], prow[0:NPAR - P, 1, :], ident[0:NPAR - P, 0:NPAR - P]).then_inc(par_t, 1)
            for kp in range(HP):
                if kp % 2 == 0:
                    pe.wait_ge(x_landed[kp // 2], 16)
                if kp >= 4:
                    pe.wait_ge(h_ready, kp - 3)
                for t in range(2):
                    for b in range(2):
                        k = 2 * kp + t
                        ins = nc.tensor.transpose(ps[:, 4 + kp % 4, (t * 2 + b) * P:(t * 2 + b + 1) * P],
                                                  xr[:, b, k * P:(k + 1) * P], ident[:, :])
                ins.then_inc(xt_full, 1)
            pe.wait_ge(par_ready, 1)
            ffn(0, 0, N_F1, F1A, F1A_G, F1B, F1B_G)
            branch_sums(N_F1OUT)
            spread(N_F1OUT)

            def head_scores(p, hd):
                q, k = qk[:, hd, :], qk[:, 2 + hd, :]
                bank = B_SCORE[hd]
                nc.tensor.matmul(ps[:, bank, 0:P], q[:, 0:P], k[:, 0:P], start=True, stop=True)
                nc.tensor.matmul(ps[:, bank, P:3 * P], q[:, P:T], k, start=True, stop=True).then_inc(s_full, 1)

            def head_transpose(p, hd):
                pe.wait_ge(p_ready, p * 2 + hd + 1)
                if hd == 1:
                    pe.wait_ge(pt_ready, p * 2 + 1)
                for b in range(3):
                    ins = nc.tensor.transpose(ps[:, B_PT, b * P:(b + 1) * P], lg[:, hd, b * P:(b + 1) * P], ident[:, :])
                ins.then_inc(pt_full, 1)

            def head_values(p, hd):
                pe.wait_ge(pt_ready, p * 2 + hd + 1)
                if hd == 0:
                    pe.wait_ge(vtok_ready, p + 1)
                else:
                    pe.wait_ge(y_out, p * 2 + 1)
                nc.tensor.matmul(ps[:, B_Y, 0:T], vtok[:, hd, 0, :], pt[:, hd, 0:2 * P], start=True, stop=False, skip_group_check=True)
                nc.tensor.matmul(ps[:, B_Y, P:T], vtok[:, hd, 1, :], pt[:, hd, 2 * P:3 * P], start=False, stop=True,
                                 skip_group_check=True).then_inc(y_full, 1)

            def pair_values(p, grp_done):
                grp_done()
                for hd in range(2):
                    for b in range(2):
                        ins = nc.tensor.transpose(ps[:, B_Y, (hd * 2 + b) * P:(hd * 2 + b + 1) * P],
                                                  vc[:, hd, b * P:(b + 1) * P], ident[:, :])
                ins.then_inc(vt_full, 1)

            for j in range(UM + 2):
                if j < U1:
                    unit(MIX + j, MIX_G, xs, UK * j, ready=(x_ready, HP + j + 1), ready0=(x0_ready, 1) if j == 0 else None)
                elif 2 * U1 <= j < 2 * U1 + 2:
                    fu, s = j - 2 * U1, slot_of(MIX + j)
                    pe.wait_ge(lo_done, MIX + j + 1)
                    if fu == 0:
                        pe.wait_ge(grp_out, MIX_G + 1)
                    o = ps[:, (MIX_G + 2) % 2 * 2, 0:T]
                    for kk in range(8):
                        k = fu * 8 + kk
                        hi, lo = w_hi[:, s, kk * P:(kk + 1) * P], w_lo[:, s, kk * P:(kk + 1) * P]
                        nc.tensor.matmul(o, hi, xs[:, k, 0, :], start=k == 0, stop=False, skip_group_check=True)
                        nc.tensor.matmul(o, hi, xs[:, k, 1, :], start=False, stop=False, skip_group_check=True)
                        ins = nc.tensor.matmul(o, lo, xs[:, k, 0, :], start=False, stop=k == KD - 1, skip_group_check=True)
                    ins.then_inc(w_used, 1)
                else:
                    b = j // U1 if j < 2 * U1 else (j - 2) // U1 + 1
                    unit(MIX + j, MIX_G + b, xs, UK * ((j if b < 2 else j - 2) % U1))
                if j == 8:
                    sums(N_MIX)
                if j == 9:
                    spread(N_MIX)
                if j == 23:
                    pe.wait_ge(f_log, 1)
                    for b in range(2):
                        ins = nc.tensor.matmul(ps[:, B_S, b * H:(b + 1) * H], fz[:, 5, b * P:(b + 1) * P],
                                               ident[0:H, 0:H], start=True, stop=True)
                    ins.then_inc(f_tok, 1)
                if j == 25:
                    pe.wait_ge(f_tokc, 1)
                    nc.tensor.matmul(ps[:, B_PT, 0:H], tri1[:, 0:P], ftok[:, 0, :], start=True, stop=True)
                    nc.tensor.matmul(ps[:, B_PT, H:2 * H], ones, ftok[:, 0, :], start=True, stop=False)
                    nc.tensor.matmul(ps[:, B_PT, H:2 * H], tri1[:, 0:P], ftok[:, 1, :], start=False, stop=True)
                    nc.tensor.matmul(ps[0:H, B_PT, T:2 * T], ftok[:, 0, :], tri1[:, :], start=True, stop=False, skip_group_check=True)
                    nc.tensor.matmul(ps[0:H, B_PT, T + P:2 * T], ftok[:, 1, :], tri1[:, 0:P], start=False, stop=True,
                                     skip_group_check=True).then_inc(f_cum, 1)
                if j == 19:
                    pair_values(0, lambda: pe.wait_ge(grp_out, MIX_G + 2))

            with pe.Fori(0, PAIRS - 1) as i:
                for j in range(UM):
                    unit(MIX1 + j, MIX1_G + j // U1, xs, UK * (j % U1), per=UM, i=i, grp_per=4)
                    if j == 1:
                        head_scores(i, 0)
                    if j == 3:
                        head_scores(i, 1)
                    if j == 6:
                        head_transpose(i, 0)
                    if j == 9:
                        head_values(i, 0)
                    if j == 10:
                        head_transpose(i, 1)
                    if j == 13:
                        head_values(i, 1)
                    if j == 19:
                        pe.wait_ge(y_out, i * 2 + 2)
                        pair_values(i + 1, lambda: pe.wait_ge(grp_out, i * 4 + MIX1_G + 2))

            last = PAIRS - 1
            for j, (m, u) in enumerate(WO_ORDER):
                unit(WO + j, WO_G + m, mrg, UK * u, ready=(m_ready, 2 * u + 3) if m == 0 else None)
                if j == 0:
                    head_scores(last, 0)
                    head_scores(last, 1)
                if j == 5:
                    head_transpose(last, 0)
                if j == 7:
                    head_values(last, 0)
                    head_transpose(last, 1)
                if j == 9:
                    head_values(last, 1)
                if j in MEM_T:
                    kp = MEM_T.index(j)
                    pe.wait_ge(memn_ready, 2)
                    if kp >= 2:
                        pe.wait_ge(mem_ready, kp - 1)
                    for t in range(2):
                        for b in range(2):
                            k = 2 * kp + t
                            ins = nc.tensor.transpose(ps[:, 5 + kp % 2, (t * 2 + b) * P:(t * 2 + b + 1) * P],
                                                      memr[:, b, k * P:(k + 1) * P], ident[:, :])
                    ins.then_inc(memt_full, 1)

            for u in range(U1):
                unit(MK + u, MK_G, mem, UK * u, ready=(mem_ready, u + 1))
                if u == 1:
                    branch_sums(N_MIXOUT)
                if u == 2:
                    spread(N_MIXOUT)
            for u in range(U1):
                unit(MQ + u, MQ_G, xs, UK * u, ready=(x_ready, 2 * HP + u + 1))
                if u == 4:
                    sums(N_MQ)
                if u == 5:
                    spread(N_MQ)

            def memory_transpose(hd):
                pe.wait_ge(mp_ready, hd + 1)
                for kb in range(2):
                    for b in range(2):
                        ins = nc.tensor.transpose(ps[:, 4 + hd, (kb * 2 + b) * P:(kb * 2 + b + 1) * P],
                                                  ml[:, hd, b, kb * P:(kb + 1) * P], ident[:, :])
                ins.then_inc(mpt_full, 1)

            def memory_values(hd):
                pe.wait_ge(mpt_ready, hd + 1)
                for kb in range(2):
                    ins = nc.tensor.matmul(ps[:, 4 + hd, 0:T], mvtok[:, hd, kb, :], mpt[:, hd, kb, :], start=kb == 0, stop=kb == 1)
                ins.then_inc(mo_full, 1)

            for u in range(U1):
                s = slot_of(MV + u)
                pe.wait_ge(lo_done, MV + u + 1)
                if u == 0:
                    pe.wait_ge(grp_out, MV_G - 1)
                for kk in range(UK):
                    k = UK * u + kk
                    hi, lo = (w[:, s, kk * 512:(kk + 1) * 512] for w in (w_hi, w_lo))
                    for b in range(2):
                        o = ps[:, MV_G % 2 * 2 + b, :]
                        m_hi, m_lo = (mem[:, k, part, b * P:(b + 1) * P] for part in range(2))
                        nc.tensor.matmul(o, m_hi, hi, start=k == 0, stop=False)
                        nc.tensor.matmul(o, m_hi, lo, start=False, stop=False)
                        ins = nc.tensor.matmul(o, m_lo, hi, start=False, stop=k == KD - 1)
                ins.then_inc(w_used, 1)
                if u == 1:
                    pe.wait_ge(grp_out, MQ_G + 1)
                    for hd in range(MH):
                        for b in range(2):
                            ins = nc.tensor.matmul(ps[:, 4 + hd, b * T:(b + 1) * T], qt[:, hd, b * P:(b + 1) * P], kt[:, hd, :],
                                                   start=True, stop=True)
                        ins.then_inc(ms_full, 1)
                if u in (5, 6):
                    memory_transpose(2 * (u - 5))
                    memory_transpose(2 * (u - 5) + 1)
            pe.wait_ge(grp_out, MV_G + 1)
            for j in range(G2 * UO):
                u = j % UO
                if j < UO:
                    memory_values(2 * j)
                    memory_values(2 * j + 1)
                unit(MO + j, MO_G + j // UO, osp, UK * u, UO, (os_ready, 2 * u + 2) if j < UO else None)
            branch_sums(N_MOUT)
            spread(N_MOUT)

            ffn(1, 3 * HP, N_F2, F2A, F2A_G, F2B, F2B_G)

            def out_block(c):
                transpose_chunk(f, c, OUT_BANKS[c], ot_full)

            pe.wait_ge(grp_out, F2B_G + G2 - 1)
            branch_sums(N_F2OUT, lambda: out_block(0))
            for c in range(1, 5):
                out_block(c)
            pe.wait_ge(ms_ready, N_F2OUT + 1)
            out_block(5)
            pe.wait_ge(grp_out, F2B_G + G2)
            out_block(6)
            out_block(7)


_INS = ["x", "mem", "ffn1_pre_g", "ffn1_w13", "ffn1_w2", "ffn1_post_g", "mix_pre_g", "w_in", "forget_bias",
        "gate_bias", "conv_w", "conv_b", "w_out", "mix_post_g", "mem_q_pre_g", "mem_kv_g", "w_mq", "w_mkv",
        "w_mo", "mem_post_g", "ffn2_pre_g", "ffn2_w13", "ffn2_w2", "ffn2_post_g"]


def kernel(**inputs):
    import numpy as np
    import concourse.bacc as bacc
    from concourse.bass_utils import run_bass_kernel_spmd

    nc = bacc.Bacc("TRN2", target_bir_lowering=False, num_devices=1)
    arrays, aps = {}, {}
    for name in _INS:
        arrays[f"in_{name}"] = np.ascontiguousarray(inputs[name])
        aps[name] = nc.dram_tensor(f"in_{name}", arrays[f"in_{name}"].shape, F32, kind="ExternalInput").ap()
    out = nc.dram_tensor("out", (1, T, D), F32, kind="ExternalOutput").ap()
    build(nc, aps, out)
    return run_bass_kernel_spmd(nc, [arrays], core_ids=[0]).results[0]["out"]
```

```python
from contextlib import ExitStack

import concourse.bass as bass
from concourse import mybir


P = 128
T = 256
D = 2048
KD = D // P
DFF = 5632
KF = DFF // P
H = 16
MH = 4
SCALE = float(P) ** -0.5
EPS = 1e-6
NEG = -1e30

UK = 2
GT = 4
UW = UK * GT * P
RING = 4

F32 = mybir.dt.float32
F32R = mybir.dt.float32r
ALU = mybir.AluOpType
ACT = mybir.ActivationFunctionType
AX_X = mybir.AxisListType.X

G1 = DFF // 256
U1 = KD // UK
G2 = D // (GT * P)
U2 = KF // UK
PAIRS = H // 2
UM = 4 * U1
UO = MH // UK

F1A, F1A_G = 0, 0
F1B, F1B_G = F1A + G1 * U1, F1A_G + G1
MIX, MIX_G = F1B + G2 * U2, F1B_G + G2
MIX1, MIX1_G = MIX + UM + 2, MIX_G + 5
WO, WO_G = MIX1 + (PAIRS - 1) * UM, MIX1_G + (PAIRS - 1) * 4
MK, MK_G = WO + G2 * U1, WO_G + G2
MQ, MQ_G = MK + U1, MK_G + 1
MV, MV_G = MQ + U1, MQ_G + 1
MO, MO_G = MV + U1, MV_G + 1
F2A, F2A_G = MO + G2 * UO, MO_G + G2
F2B, F2B_G = F2A + G1 * U1, F2A_G + G1

WO_ORDER = ([(m, u) for m in range(2) for u in range(U1 - 1)] + [(m, U1 - 1) for m in range(2)]
            + [(m, u) for m in range(2, G2) for u in range(U1)])
X_AHEAD = (0, 1, 3, 4)
SIGMOIDS = (5, 7, 8, 10)
MEM_T = (18, 19, 20, 22, 24, 25, 26, 27)
MEM_SPLIT = (22, 23, 24, 26, 28, 29, 30, 31)


def group_ends():
    ends, n = [], 0
    sizes = ([U1] * G1 + [U2] * G2 + [U1, U1, 2, U1, U1] + [U1] * 4 * (PAIRS - 1)
             + [2 * U1 - 1, 1] + [U1] * (G2 - 2) + [U1] * 3 + [UO] * G2 + [U1] * G1 + [U2] * G2)
    for size in sizes:
        n += size
        ends.append(n)
    return ends


ENDS = group_ends()

OUT_BANKS = (5, 6, 7, 0, 1, 4, 2, 3)
assert (F2B_G + G2 - 1) % 2 == 1

N_F1, N_F1OUT, N_MIX, N_MIXOUT, N_MQ, N_MOUT, N_F2, N_F2OUT = range(8)
HP = KD // 2


def added(norm, kp):
    return norm * (HP - 1) - norm // 2 * 2 + kp - 1


WIDE = G1 - 2 + G2 // 2

(C_F1PRE, C_F1POST, C_MIXPRE, C_MIXPOST, C_MQPRE, C_MKV, C_MPOST, C_F2PRE,
 C_F2POST, C_GB, _C1, C_CW, _C2, _C3, C_CB) = range(0, 15 * KD, KD)
NPAR = 15 * KD

B_NORM, B_S, B_PT, B_Y = 4, 5, 6, 7
B_SCORE = (B_S, B_NORM)


class Chain:

    def __init__(self, eng, sem):
        self.eng, self.sem, self.n, self.loop = eng, sem, 0, None

    def step(self, ins):
        self.n += 1
        ins.then_inc(self.sem, 1)

    def settle(self):
        if self.loop is None:
            self.eng.wait_ge(self.sem, self.n)
        else:
            i, per = self.loop
            self.eng.wait_ge(self.sem, i * per + self.n)

    def enter(self, i, per):
        self.loop, self.start = (i, per), self.n

    def leave(self, times):
        per = self.loop[1]
        assert self.n - self.start == per, (self.sem, self.n - self.start)
        self.n, self.loop = self.start + per * times, None


def build(nc, a, out):
    with ExitStack() as ctx:
        def sem(name):
            return ctx.enter_context(nc.semaphore(name))

        at = [(nc.sbuf_base + 63) // 32 * 32]

        def place(name, shape, dt=F32, offset=None):
            size = 4
            for n in shape[1:]:
                size *= n
            size = (size + 31) // 32 * 32
            if offset is None:
                offset, at[0] = at[0], at[0] + size
            return nc.alloc_sbuf_tensor_at(name, shape, dt, offset=offset)

        h = place("h", [P, KD, T])
        xs_at = at[0]
        xs = place("xs", [P, KD, 2, T], F32R)
        f = place("f", [P, KD, T], offset=xs_at + KD * T * 4)
        raw = place("raw", [P, RING, UW])
        w_hi = place("w_hi", [P, RING, UW], F32R)
        w_lo = place("w_lo", [P, RING, UW], F32R)
        r_in = place("r_in", [P, T])
        r_out = place("r_out", [P, T])
        ms = place("ms", [P, 2])
        mhalf = place("mhalf", [P, 2])
        rtok = place("rtok", [P, 2])
        diag = place("diag", [P, 2, P])
        ident = place("ident", [P, P])
        tri1 = place("tri1", [P, T])
        ones = tri1[:, P:T]
        mask = place("mask", [P, P])
        par = place("par", [P, NPAR])
        prm = place("prm", [P, KD, 6])
        fbias = place("fbias", [H, 1])
        sq = place("sq", [P, 2, 2 * T])
        sqsum = place("sqsum", [P, 2 * T])
        gt = place("gt", [P, 2, T])
        up = place("up", [P, 2, T])
        half = place("half", [P, GT, T])
        arena = at[0]

        g = place("g", [P, KF, 2, T], F32R, arena)
        xr = place("xr", [P, 2, D], F32, arena)
        prow = place("prow", [P, 2, P], F32, arena + 2 * D * 4)
        mrg = place("mrg", [P, KD, 2, T], F32R, arena)
        at[0] = arena + KD * 2 * T * 4
        cross = at[0]
        qk = place("qk", [P, 4, T])
        vc = place("vc", [P, 4, T])
        bc = place("bc", [P, 4, T])
        zp = place("zp", [P, 2, T + 2])
        gat = place("gat", [P, 4, T])
        yc = place("yc", [P, 2, T])
        vtok = place("vtok", [P, 2, 2, P])
        lg = place("lg", [P, 2, 3 * P])
        pt = place("pt", [P, 2, 3 * P])
        ncr = place("ncr", [P, 2, T])
        ncm = place("ncm", [P, 2, 3 * P])
        mg = place("mg", [P, T])
        ctok = place("ctok", [P, 2, H])
        cq = place("cq", [P, 2, 2])
        prp = place("prp", [P, 2, 6])
        st = place("st", [P, 2, 6])
        ftok = place("ftok", [P, 2, H])
        memr_at = arena + KF * 2 * T * 4 - 2 * D * 4
        fz = place("fz", [H, 8, T], F32, memr_at)
        assert at[0] <= memr_at, (at[0], memr_at)
        memr = place("memr", [P, 2, D], F32, memr_at)
        mem = place("mem", [P, KD, 2, T], F32R, cross)
        junk = place("junk", [P, 2, D], F32, cross)
        assert cross + KD * 2 * T * 4 <= memr_at
        at[0] = arena
        kt = place("kt", [P, MH, T])
        qt = place("qt", [P, MH, T])
        mvtok = place("mvtok", [P, MH, 2, P])
        ml = place("ml", [P, MH, 2, T])
        assert at[0] <= cross
        mpt = place("mpt", [P, MH, 2, T], F32, memr_at)
        osp = place("osp", [P, MH, 2, T], F32R, memr_at + MH * 2 * T * 4)
        at[0] = arena + KF * 2 * T * 4
        mst = place("mst", [P, 8])
        mmx = place("mmx", [P, MH, 6])
        ht = place("ht", [P, 8, 512], F32, xs_at)
        ot = place("ot", [P, 8, 512], F32, arena)
        assert at[0] <= nc.sbuf_usable_end, at[0]

        ps = ctx.enter_context(nc.psum_tensor("ps", [P, 8, 512], F32))
        crow = nc.dram_tensor("crow", [1, H, T], F32, kind="Internal").ap()

        x_landed = [sem(f"x_landed{i}") for i in range(4)]
        gain_landed = sem("gain_landed")
        par_landed = sem("par_landed")
        mem_landed = sem("mem_landed")
        ident_set = sem("ident_set")
        consts_set = sem("consts_set")
        gain_t = sem("gain_t")
        gain_ready = sem("gain_ready")
        par_t = sem("par_t")
        par_ready = sem("par_ready")
        xt_full = sem("xt_full")
        landed = [sem(f"landed{i}") for i in range(RING)]
        hi_done = sem("hi_done")
        lo_done = sem("lo_done")
        w_used = sem("w_used")
        grp_out = sem("grp_out")
        h_ready = sem("h_ready")
        xhi_ready = sem("xhi_ready")
        x_ready = sem("x_ready")
        x0_ready = sem("x0_ready")
        t_ready = sem("t_ready")
        sq_ready = sem("sq_ready")
        sq_added = sem("sq_added")
        sq_folded = sem("sq_folded")
        sum_full = sem("sum_full")
        ms_ready = sem("ms_ready")
        r_ready = sem("r_ready")
        diag_ready = sem("diag_ready")
        r_full = sem("r_full")
        r_set = sem("r_set")
        half_ready = sem("half_ready")
        gate_in = sem("gate_in")
        silu_done = sem("silu_done")
        g_ready = sem("g_ready")
        dve_own = sem("dve_own")
        pool_own = sem("pool_own")
        f_na = sem("f_na")
        f_e = sem("f_e")
        f_y = sem("f_y")
        f_ln = sem("f_ln")
        f_log = sem("f_log")
        f_tok = sem("f_tok")
        f_tokc = sem("f_tokc")
        f_cum = sem("f_cum")
        f_c = sem("f_c")
        crow_stored = sem("crow_stored")
        ncr_landed = sem("ncr_landed")
        prm_set = sem("prm_set")
        cq_set = sem("cq_set")
        ncm_done = sem("ncm_done")
        z_ready = sem("z_ready")
        taps_done = sem("taps_done")
        ycb_done = sem("ycb_done")
        gat_exp = sem("gat_exp")
        sig_ready = sem("sig_ready")
        ymix_ready = sem("ymix_ready")
        vt_full = sem("vt_full")
        vtok_ready = sem("vtok_ready")
        s_full = sem("s_full")
        l_ready = sem("l_ready")
        e_done = sem("e_done")
        p_ready = sem("p_ready")
        pt_full = sem("pt_full")
        pt_ready = sem("pt_ready")
        y_full = sem("y_full")
        y_out = sem("y_out")
        m_ready = sem("m_ready")
        msq_done = sem("msq_done")
        mm_ready = sem("mm_ready")
        mr_ready = sem("mr_ready")
        memn_ready = sem("memn_ready")
        memt_full = sem("memt_full")
        memhi_ready = sem("memhi_ready")
        mem_ready = sem("mem_ready")
        ms_full = sem("ms_full")
        mmax_ready = sem("mmax_ready")
        mexp_done = sem("mexp_done")
        mp_ready = sem("mp_ready")
        mpt_full = sem("mpt_full")
        mpt_ready = sem("mpt_ready")
        mo_full = sem("mo_full")
        oshi_ready = sem("oshi_ready")
        os_ready = sem("os_ready")
        mv_out = sem("mv_out")
        ht_full = sem("ht_full")
        ht_ready = sem("ht_ready")
        ot_full = sem("ot_full")
        ot_ready = sem("ot_ready")
        out_stored = sem("out_stored")

        def slot_of(n):
            return n % RING

        def of(n, per=0, i=None):
            return n if i is None else i * per + n

        def out_chunk(c):
            b, q = c % 2, c // 2
            return out[0, b * P:(b + 1) * P, q * 512:(q + 1) * 512]

        def memory_block(b):
            return ps[:, MV_G % 2 * 2 + b, :].rearrange("p (m d) -> p m d", d=P)

        def wide_banks(grp):
            first = (grp + 1) % 2 * 4
            return ps[:, first:first + 4, :]

        block = ctx.enter_context(nc.Block())

        @block.sync
        def _(sp):
            xv = a["x"].rearrange("o (b p) (q n) -> p (o b) q n", p=P, q=4)

            def load_x(q):
                sp.dma_start(xr[:, :, q * 512:(q + 1) * 512], xv[:, :, q, :]).then_inc(x_landed[q], 16)

            def load(n0, src, per=0, i=None):
                n = n0
                if n >= RING:
                    sp.wait_ge(lo_done, of(n - RING + 1, per, i))
                s = slot_of(n)
                if len(src.shape) == 4:
                    dst = raw[:, s, :].rearrange("p (k s n) -> p k s n", k=src.shape[1], s=2)
                    halves = [(dst[:, :, b, :], src[:, :, b, :]) for b in range(2)]
                else:
                    dst = raw[:, s, :].rearrange("p (k n) -> p k n", k=src.shape[1])
                    mid = src.shape[1] // 2
                    halves = [(dst[:, :mid, :], src[:, :mid, :]), (dst[:, mid:, :], src[:, mid:, :])]
                for to, frm in halves:
                    sp.dma_start(to, frm).then_inc(landed[s], 16)

            def columns(w, u, c, width=GT * P):
                return w[:, UK * u:UK * u + UK, bass.ds(c, width)]

            def two_columns(w, u, c):
                return w[:, UK * u:UK * u + UK, :, bass.ds(c, 2 * P)]

            def ffn(w13, w2, n13, n2):
                w13 = w13.rearrange("o (k p) (s n) -> p (o k) s n", p=P, s=2)
                w2 = w2.rearrange("o (k p) n -> p (o k) n", p=P)
                for u in range(U1):
                    if n13 == F1A and u in X_AHEAD:
                        load_x(X_AHEAD.index(u))
                    load(n13 + u, two_columns(w13, u, 0))
                with sp.Fori(0, G1 - 1) as i:
                    for u in range(U1):
                        load(n13 + U1 + u, two_columns(w13, u, i * 256 + 256), U1, i)
                with sp.Fori(0, G2 // 2) as i:
                    for m in range(2):
                        for u in range(U2):
                            load(n2 + m * U2 + u, columns(w2, u, i * 1024 + m * 512), 2 * U2, i)

            ffn(a["ffn1_w13"], a["ffn1_w2"], F1A, F1B)

            w_in = a["w_in"].rearrange("o (k p) n -> p (o k) n", p=P)
            cx = 3 * D + H
            kinds = [(0, D), (2 * D, cx - 2 * D), (cx + D, D), (cx + 3 * D, D)]
            views = [w_in[:, :, c:c + 2 * step].rearrange("p k (s n) -> p k s n", s=2) for c, step in kinds]
            for j in range(UM):
                if j == 2 * U1:
                    for u in range(2):
                        load(MIX + 2 * U1 + u, w_in[:, 8 * u:8 * u + 8, 3 * D:3 * D + P])
                load(MIX + j + (2 if j >= 2 * U1 else 0), two_columns(views[j // U1], j % U1, 0))
            with sp.Fori(0, PAIRS - 1) as i:
                for j in range(UM):
                    load(MIX1 + j, two_columns(views[j // U1], j % U1, i * 256 + 256), UM, i)

            sp.wait_ge(w_used, MIX1)
            sp.dma_start(memr[:, :, :], a["mem"].rearrange("o (b p) n -> p (o b) n", p=P)).then_inc(mem_landed, 16)

            w_out = a["w_out"].rearrange("o (k p) n -> p (o k) n", p=P)
            w_mkv = a["w_mkv"].rearrange("o (k p) n -> p (o k) n", p=P)
            w_mq = a["w_mq"].rearrange("o (k p) n -> p (o k) n", p=P)
            w_mo = a["w_mo"].rearrange("o (k p) n -> p (o k) n", p=P)
            for j, (m, u) in enumerate(WO_ORDER):
                load(WO + j, columns(w_out, u, m * 512))
            for n0, w, c in ((MK, w_mkv, 0), (MQ, w_mq, 0), (MV, w_mkv, 512)):
                for u in range(U1):
                    load(n0 + u, columns(w, u, c))
            for u in range(G2 * UO):
                load(MO + u, columns(w_mo, u % UO, u // UO * 512))

            ffn(a["ffn2_w13"], a["ffn2_w2"], F2A, F2B)
            for c in range(0, 8, 2):
                sp.wait_ge(ot_ready, c + 1)
                sp.dma_start(out_chunk(c), ot[:, c, :]).then_inc(out_stored, 16)
            sp.wait_ge(out_stored, 8 * 16)

        @block.scalar
        def _(act):
            act.dma_start(prow[0:KD, 0, :], a["ffn1_pre_g"].rearrange("o (k p) -> (o k) p", p=P)).then_inc(gain_landed, 16)

            def unit(n0, per=0, i=None):
                s = slot_of(n0)
                act.wait_ge(landed[s], of(32 * (n0 // RING + 1), 32 * (per // RING), i))
                if n0 >= RING:
                    act.wait_ge(w_used, of(n0 - RING + 1, per, i))
                nc.scalar.copy(w_hi[:, s, :], raw[:, s, :]).then_inc(hi_done, 1)

            def units(n0, count):
                loops = count // RING
                if loops > 1:
                    with act.Fori(0, loops) as i:
                        for j in range(RING):
                            unit(n0 + j, RING, i)
                else:
                    loops = 0
                for j in range(loops * RING, count):
                    unit(n0 + j)

            def square_pair(norm, kp, src):
                if kp >= 3:
                    act.wait_ge(sq_added, added(norm, kp - 1))
                elif norm > 0:
                    act.wait_ge(sum_full, norm)
                to = sqsum[:, :] if kp == 0 else sq[:, kp % 2, :]
                nc.scalar.activation(to, src.rearrange("p k t -> p (k t)"), ACT.Square).then_inc(sq_ready, 1)

            def input_pair(base, norm, gain, kp):
                act.wait_ge(h_ready, base + kp + 1)
                if kp > 0 or norm == N_F1:
                    for k in (2 * kp, 2 * kp + 1):
                        ins = nc.scalar.activation(xs[:, k, 0, :], h[:, k, :], ACT.Copy, scale=par[:, gain + k:gain + k + 1])
                    ins.then_inc(xhi_ready, 1)
                square_pair(norm, kp, h[:, 2 * kp:2 * kp + 2, :])

            def input_and_units(base, norm, gain, n0, kp0=RING):
                for kp in range(HP):
                    if kp >= kp0:
                        unit(n0 + kp - kp0)
                    input_pair(base, norm, gain, kp)

            def branch_out(norm, grp, m):
                act.wait_ge(w_used, ENDS[grp])
                for c in range(2):
                    square_pair(norm, 2 * m + c, ps[:, grp % 2 * 2 + c, :].rearrange("p (k t) -> p k t", t=T))

            def next_and_branch_end(n0, norm, grp):
                unit(n0)
                unit(n0 + 1)
                unit(n0 + 2)
                branch_out(norm, grp, G2 - 1)
                unit(n0 + 3)

            def silu(ffn, grp0, per=0, i=None):
                n = ffn * G1 + grp0
                act.wait_ge(gate_in, of(n + 1, per, i))
                nc.scalar.activation(gt[:, :, :], gt[:, :, :], ACT.Silu).then_inc(silu_done, 1)

            def halves(grp, per=0, i=None):
                act.wait_ge(w_used, of(ENDS[grp], per * U1, i))
                act.wait_ge(grp_out, of(grp, per, i))
                nc.scalar.copy(half[:, :, :], wide_banks(grp)[:, :, T:2 * T]).then_inc(half_ready, 1)

            def ffn(k, base, norm, gain, n13, grp13, n2, grp2):
                if k == 0:
                    input_and_units(base, norm, gain, n13, 0)
                else:
                    input_and_units(base, norm, gain, n13 + RING)
                for grp in (1, 2):
                    for u in range(U1):
                        unit(n13 + U1 * grp + u)
                        if u == RING - 1:
                            silu(k, grp - 1)
                with act.Fori(0, (G1 - 4) // 2) as i:
                    for j in range(2 * U1):
                        unit(n13 + 3 * U1 + j, 2 * U1, i)
                        b = 2 + j // U1
                        if j % U1 == 3:
                            halves(grp13 + b, 2, i)
                        if j % U1 == 4:
                            silu(k, b, 2, i)
                for u in range(U1):
                    unit(n13 + (G1 - 1) * U1 + u)
                    if u == 3:
                        halves(grp13 + G1 - 2)
                    if u == 4:
                        silu(k, G1 - 2)
                for u in range(RING):
                    if u == RING - 1 and k == 1:
                        for c in range(8):
                            act.wait_ge(ht_full, c + 1)
                            nc.scalar.copy(ht[:, c, :], ps[:, 4 + c % 4, :]).then_inc(ht_ready, 1)
                    unit(n2 + u)
                halves(grp2 - 1)
                silu(k, G1 - 1)
                for m in range(0, G2, 2):
                    n = n2 + m * U2 + RING
                    units(n, U2)
                    halves(grp2 + m)
                    unit(n + U2)
                    act.wait_ge(grp_out, grp2 + m + 1)
                    for c in range(2):
                        square_pair(norm + 1, 2 * m + c, f[:, 4 * m + 2 * c:4 * m + 2 * c + 2, :])
                    if m + 2 < G2:
                        units(n + U2 + 1, U2 - 1)
                        branch_out(norm + 1, grp2 + m + 1, m + 1)
                    else:
                        units(n + U2 + 1, U2 - RING - 1)

            act.wait_ge(consts_set, 1)
            nc.scalar.copy(mst[:, 6:7], ones[:, 0:1])
            act.wait_ge(gain_ready, 1)
            ffn(0, 0, N_F1, C_F1PRE, F1A, F1A_G, F1B, F1B_G)

            act.wait_ge(par_ready, 1)
            next_and_branch_end(MIX, N_F1OUT, MIX_G - 1)

            def pair_starts(p):
                act.wait_ge(ncm_done, p + 1)
                nc.scalar.copy(cq[:, :, :], ctok[:, :, bass.ds(p * 2, 2)]).then_inc(cq_set, 1)
                act.dma_start(ncr[:, :, :], crow[:, bass.ds(p * 2, 2), :].broadcast_to([P, 2, T])).then_inc(ncr_landed, 16)

            def gates(p):
                act.wait_ge(grp_out, p * 4 + MIX1_G)
                act.wait_ge(prm_set, p + 1)
                for t in range(4):
                    ins = nc.scalar.activation(gat[:, t, :], gat[:, t, :], ACT.Exp,
                                               bias=prp[:, t % 2, 4 + t // 2:5 + t // 2], scale=-1.0)
                ins.then_inc(gat_exp, 1)

            def head_exp(p, hd):
                act.wait_ge(l_ready, p * 2 + hd + 1)
                nc.scalar.activation(lg[:, hd, 0:P], lg[:, hd, 0:P], ACT.Exp,
                                     bias=st[:, hd, 0:1], accum_out=st[:, hd, 2:3])
                nc.scalar.activation(lg[:, hd, P:3 * P], lg[:, hd, P:3 * P], ACT.Exp,
                                     bias=st[:, hd, 1:2], accum_out=st[:, hd, 3:4]).then_inc(e_done, 1)

            def pair_params(i):
                if not isinstance(i, int) or i > 0:
                    act.wait_ge(taps_done, i)
                nc.scalar.copy(prp[:, :, :], prm[:, bass.ds(i * 2, 2), :]).then_inc(prm_set, 1)

            input_and_units(HP, N_MIX, C_MIXPRE, MIX + RING)
            for j in range(U1, UM + 2):
                unit(MIX + j)
                if j == 22:
                    act.wait_ge(f_na, 1)
                    nc.scalar.activation(fz[:, 2, :], fz[:, 1, :], ACT.Exp).then_inc(f_e, 1)
                if j == 24:
                    act.wait_ge(f_y, 1)
                    nc.scalar.activation(fz[:, 4, :], fz[:, 3, :], ACT.Ln).then_inc(f_ln, 1)
                if j == 31:
                    act.wait_ge(f_c, 1)
                    act.dma_start(crow.rearrange("o h t -> (o h) t"), fz[:, 7, :]).then_inc(crow_stored, 16)
                if j == 22:
                    pair_params(0)

            def pair_body(i):
                for j in range(UM):
                    unit(MIX1 + j, UM, i)
                    if j == 0:
                        pair_starts(i)
                    if j == 4:
                        gates(i)
                    if j == 7:
                        head_exp(i, 0)
                    if j == 10:
                        head_exp(i, 1)
                    if j == 20:
                        pair_params(i + 1)

            act.wait_ge(crow_stored, 16)
            with act.Fori(0, PAIRS - 1) as i:
                pair_body(i)

            def memory_hi(j):
                if j in MEM_SPLIT:
                    kp = MEM_SPLIT.index(j)
                    act.wait_ge(memt_full, kp + 1)
                    for t in range(2):
                        k = 2 * kp + t
                        ins = nc.scalar.activation(mem[:, k, 0, :], ps[:, 5 + kp % 2, t * T:(t + 1) * T], ACT.Copy,
                                                   scale=par[:, C_MKV + k:C_MKV + k + 1])
                    ins.then_inc(memhi_ready, 1)

            for j in range(G2 * U1):
                unit(WO + j)
                if j == 0:
                    pair_starts(PAIRS - 1)
                if j == 4:
                    gates(PAIRS - 1)
                if j == 5:
                    head_exp(PAIRS - 1, 0)
                if j == 7:
                    head_exp(PAIRS - 1, 1)
                if j == 14:
                    act.wait_ge(m_ready, H + 1)
                    act.wait_ge(mem_landed, 16)
                    for b in range(2):
                        nc.scalar.activation(junk[:, b, :], memr[:, b, :], ACT.Square,
                                             accum_out=mst[:, b:b + 1]).then_inc(msq_done, 1)
                memory_hi(j)
                for m, after in enumerate((17, 19, 27)):
                    if j == after:
                        branch_out(N_MIXOUT, WO_G + m, m)

            next_and_branch_end(MK, N_MIXOUT, MK_G - 1)
            unit(MK + RING)
            for kp in range(HP):
                if kp + 1 < HP:
                    unit(MK + RING + kp + 1)
                input_pair(2 * HP, N_MQ, C_MQPRE, kp)
            for j in range(RING, U1):
                unit(MQ + j)

            def memory_exp(hd):
                act.wait_ge(mmax_ready, hd + 1)
                for b in range(2):
                    ins = nc.scalar.activation(ml[:, hd, b, :], ps[:, 4 + hd, b * T:(b + 1) * T], ACT.Exp,
                                               bias=mmx[:, hd, b:b + 1], scale=SCALE,
                                               accum_out=mmx[:, hd, 2 + b:3 + b])
                ins.then_inc(mexp_done, 1)

            for j in range(U1):
                unit(MV + j)
                if j >= 6:
                    memory_exp(2 * (j - 6))
                    memory_exp(2 * (j - 6) + 1)
            for j in range(RING):
                if j == RING - 1:
                    act.wait_ge(w_used, ENDS[MV_G])
                    nc.scalar.copy(mvtok[:, :, 0, :], memory_block(0)).then_inc(mv_out, 1)
                unit(MO + j)
            for hd in range(MH):
                act.wait_ge(mo_full, hd + 1)
                nc.scalar.copy(osp[:, hd, 0, :], ps[:, 4 + hd, 0:T]).then_inc(oshi_ready, 1)
            for j in range(RING, G2 * UO):
                unit(MO + j)
                if j % 2 == 1:
                    branch_out(N_MOUT, MO_G + (j - 5) // 2, (j - 5) // 2)
            branch_out(N_MOUT, MO_G + 2, 2)
            next_and_branch_end(F2A, N_MOUT, F2A_G - 1)
            ffn(1, 3 * HP, N_F2, C_F2PRE, F2A, F2A_G, F2B, F2B_G)
            branch_out(N_F2OUT, F2B_G + G2 - 1, G2 - 1)

            for c in range(1, 8, 2):
                act.wait_ge(ot_ready, c + 1)
                act.dma_start(out_chunk(c), ot[:, c, :]).then_inc(out_stored, 16)

        @block.vector
        def _(dve):
            own = Chain(dve, dve_own)

            def tile_tokens(r, n):
                return r[:, :].rearrange("p (o t) -> p o t", o=1).broadcast_to([P, n, T])

            def banks(grp, b=0, n=2):
                first = grp % 2 * 2 + b
                return ps[:, first:first + n, :].rearrange("p b (m t) -> p (b m) t", t=T)

            def unit(n0, per=0, i=None):
                s = slot_of(n0)
                dve.wait_ge(hi_done, of(n0 + 1, per, i))
                nc.vector.tensor_tensor(w_lo[:, s, :], raw[:, s, :], w_hi[:, s, :].bitcast(F32),
                                        ALU.subtract).then_inc(lo_done, 1)

            def units(n0, count):
                loops = count // RING
                if loops > 1:
                    with dve.Fori(0, loops) as i:
                        for j in range(RING):
                            unit(n0 + j, RING, i)
                else:
                    loops = 0
                for j in range(loops * RING, count):
                    unit(n0 + j)

            def group_done(grp, per=0, i=None):
                dve.wait_ge(w_used, of(ENDS[grp], per * U1, i))

            def mean(norm, weight=1.0):
                dve.wait_ge(sum_full, norm + 1)
                nc.vector.tensor_scalar(ms[:, :], ps[:, B_NORM, 0:2], 1.0 / (D * weight * weight),
                                        EPS / (weight * weight), ALU.mult, ALU.add).then_inc(ms_ready, 1)

            def spread(norm, meanwhile=None, first=None):
                dve.wait_ge(r_ready, norm + 1)
                for b in range(2):
                    ins = nc.vector.tensor_scalar(diag[:, b, :], ident[:, :], rtok[:, b:b + 1], None, ALU.mult)
                ins.then_inc(diag_ready, 1)
                if meanwhile is not None:
                    meanwhile()
                dve.wait_ge(r_full, norm + 1)
                if first is not None:
                    first()
                nc.vector.tensor_copy((r_out if norm % 2 else r_in)[:, :], ps[:, B_NORM, T:2 * T]).then_inc(r_set, 1)
                dve.wait_ge(r_set, norm + 1)

            def input_lo(base, gain, kp):
                dve.wait_ge(xhi_ready, base - base // HP + kp + 1)
                for k in (2 * kp, 2 * kp + 1):
                    ins = nc.vector.scalar_tensor_tensor(
                        out=xs[:, k, 1, :], in0=h[:, k, :], scalar=par[:, gain + k:gain + k + 1],
                        in1=xs[:, k, 0, :].bitcast(F32), op0=ALU.mult, op1=ALU.subtract)
                ins.then_inc(x_ready, 1)

            def branch_tiles(gain, norm, grp, m, tiles=range(GT)):
                dve.wait_ge(sq_ready, norm * HP + 2 * m + 2)
                for t in tiles:
                    k = 4 * m + t
                    ins = nc.vector.tensor_scalar(f[:, k, :], banks(grp)[:, t, :], par[:, gain + k:gain + k + 1], None, ALU.mult)
                if GT - 1 in tiles:
                    ins.then_inc(grp_out, 1)

            def branch_norm(kp):
                nc.vector.tensor_tensor(f[:, 2 * kp:2 * kp + 2, :], f[:, 2 * kp:2 * kp + 2, :],
                                        tile_tokens(r_out, 2), ALU.mult).then_inc(t_ready, 1)

            def branch_end(gain, norm, grp, weight=1.0):
                dve.wait_ge(sq_ready, (norm + 1) * HP)
                own.step(nc.vector.tensor_tensor(sq[:, 0, :], sq[:, 0, :], sq[:, 1, :], ALU.add))
                own.settle()
                nc.vector.tensor_tensor(sq[:, 0, 0:T], sq[:, 0, 0:T], sq[:, 0, T:2 * T], ALU.add).then_inc(sq_folded, 1)
                branch_tiles(gain, norm, grp, G2 - 1, range(2))
                mean(norm, weight)
                branch_tiles(gain, norm, grp, G2 - 1, range(2, GT))
                dve.wait_ge(grp_out, grp + 1)

            def first_pair(base, gain, between):
                for k in range(2):
                    if k == 1:
                        own.step(nc.vector.tensor_tensor(f[:, k, :], f[:, k, :], r_out[:, :], ALU.mult))
                    own.settle()
                    add = nc.vector.tensor_tensor(h[:, k, :], h[:, k, :], f[:, k, :], ALU.add)
                    if k == 0:
                        own.step(add)
                        own.settle()
                    else:
                        add.then_inc(h_ready, 1)
                        dve.wait_ge(h_ready, base + 1)
                    own.step(nc.vector.tensor_scalar(xs[:, k, 0, :], h[:, k, :], par[:, gain + k:gain + k + 1], None, ALU.mult))
                    own.settle()
                    nc.vector.scalar_tensor_tensor(
                        out=xs[:, k, 1, :], in0=h[:, k, :], scalar=par[:, gain + k:gain + k + 1],
                        in1=xs[:, k, 0, :].bitcast(F32), op0=ALU.mult, op1=ALU.subtract).then_inc(x_ready if k else x0_ready, 1)
                    if k == 0 and between is not None:
                        between()

            def next_input(norm, gain, n0, count=RING):
                base = (norm + 1) // 2 * HP
                if count == HP:
                    unit(n0)
                first_pair(base, gain, (lambda: unit(n0 + 1)) if count == HP else None)
                branch_norm(1)
                for kp in range(1, HP):
                    if kp < HP - 1:
                        branch_norm(kp + 1)
                    if count == HP and kp + 1 < HP:
                        unit(n0 + kp + 1)
                    elif count < HP and kp >= HP - count:
                        unit(n0 + kp - (HP - count))
                    input_lo(base, gain, kp)

            def gate_up_out(k, grp, par_grp, per=0, i=None):
                group_done(grp, per, i)
                nc.vector.tensor_tensor(gt[:, :, :], banks(par_grp, 0, 1), tile_tokens(r_in, 2), ALU.mult).then_inc(gate_in, 1)
                nc.vector.tensor_tensor(up[:, :, :], banks(par_grp, 1, 1), tile_tokens(r_in, 2), ALU.mult).then_inc(grp_out, 1)

            def add_halves(out, grp, b, n):
                return nc.vector.tensor_tensor(out, wide_banks(grp)[:, b:b + n, 0:T], half[:, b:b + n, :], ALU.add)

            def wide_gate_up_out(k, grp, n, per=0, i=None):
                dve.wait_ge(half_ready, of(k * WIDE + n + 1, per, i))
                own.step(add_halves(gt[:, :, :], grp, 0, 2))
                own.settle()
                nc.vector.tensor_tensor(gt[:, :, :], gt[:, :, :], tile_tokens(r_in, 2), ALU.mult).then_inc(gate_in, 1)
                add_halves(up[:, :, :], grp, 2, 2).then_inc(grp_out, 1)
                dve.wait_ge(grp_out, of(grp + 1, per, i))
                own.step(nc.vector.tensor_tensor(up[:, :, :], up[:, :, :], tile_tokens(r_in, 2), ALU.mult))
                own.settle()

            def gate_times_up(k, grp, n, per=0, i=None):
                dve.wait_ge(silu_done, of(k * G1 + n + 1, per, i))
                dve.wait_ge(grp_out, of(grp + 1, per, i))
                own.step(nc.vector.tensor_tensor(up[:, :, :], gt[:, :, :], up[:, :, :], ALU.mult))
                own.settle()
                where = bass.ds(2 * n if i is None else i * (2 * per) + 2 * n, 2)
                own.step(nc.vector.tensor_copy(g[:, where, 0, :], up[:, :, :]))
                own.settle()
                nc.vector.tensor_tensor(g[:, where, 1, :], up[:, :, :], g[:, where, 0, :].bitcast(F32),
                                        ALU.subtract).then_inc(g_ready, 1)

            def ffn(k, norm, post, n13, grp13, n2, grp2):
                for j in range(U1, 2 * U1):
                    unit(n13 + j)
                    if j == U1 + 3:
                        mean(norm)
                        spread(norm)
                        gate_up_out(k, grp13, grp13)
                    if j == U1 + 4:
                        gate_times_up(k, grp13, 0)
                    if j == 2 * U1 - 1 and k == 0:
                        parameters()
                for j in range(U1):
                    unit(n13 + 2 * U1 + j)
                    if j == 3:
                        gate_up_out(k, grp13 + 1, grp13 + 1)
                    if j == 4:
                        gate_times_up(k, grp13 + 1, 1)
                with dve.Fori(0, (G1 - 4) // 2) as i:
                    own.enter(i, 8)
                    for j in range(2 * U1):
                        unit(n13 + 3 * U1 + j, 2 * U1, i)
                        b = 2 + j // U1
                        if j % U1 == 3:
                            wide_gate_up_out(k, grp13 + b, b - 2, 2, i)
                        if j % U1 == 5:
                            gate_times_up(k, grp13 + b, b, 2, i)
                own.leave((G1 - 4) // 2)
                for j in range(U1):
                    unit(n13 + (G1 - 1) * U1 + j)
                    if j == 3:
                        wide_gate_up_out(k, grp2 - 2, G1 - 4)
                    if j == 5:
                        gate_times_up(k, grp2 - 2, G1 - 2)
                for j in range(RING):
                    unit(n2 + j)
                wide_gate_up_out(k, grp2 - 1, G1 - 3)
                gate_times_up(k, grp2 - 1, G1 - 1)
                for m in range(0, G2, 2):
                    n = n2 + m * U2 + RING
                    units(n, U2)
                    dve.wait_ge(half_ready, k * WIDE + G1 - 2 + m // 2 + 1)
                    add_halves(f[:, 4 * m:4 * m + 4, :], grp2 + m, 0, GT).then_inc(grp_out, 1)
                    unit(n + U2)
                    unit(n + U2 + 1)
                    dve.wait_ge(sq_ready, (norm + 1) * HP + 2 * m + 2)
                    dve.wait_ge(grp_out, grp2 + m + 1)
                    for t in range(GT):
                        tile = 4 * m + t
                        ins = nc.vector.tensor_scalar(f[:, tile, :], f[:, tile, :], par[:, post + tile:post + tile + 1], None, ALU.mult)
                    own.step(ins)
                    if m + 2 < G2:
                        units(n + U2 + 2, U2 - 2)
                        branch_tiles(post, norm + 1, grp2 + m + 1, m + 1)
                    else:
                        units(n + U2 + 2, U2 - RING - 2)
                own.settle()

            def next_and_branch_end(n0, gain, norm, grp, weight=1.0):
                unit(n0)
                unit(n0 + 1)
                unit(n0 + 2)
                branch_end(gain, norm, grp, weight)
                spread(norm, lambda: unit(n0 + 3), lambda: own.step(
                    nc.vector.tensor_tensor(f[:, 0, :], f[:, 0, :], ps[:, B_NORM, T:2 * T], ALU.mult)))

            nc.vector.memset(tri1[:, :], 1.0).then_inc(consts_set, 1)
            nc.vector.memset(mhalf[:, :], -0.5).then_inc(consts_set, 1)
            dve.sem_inc(ncm_done, 1)
            dve.sem_inc(m_ready, 1)
            dve.wait_ge(gain_t, 1)
            nc.vector.tensor_copy(par[:, 0:KD], ps[:, 2, 0:KD]).then_inc(gain_ready, 1)
            dve.wait_ge(gain_ready, 1)

            def parameters():
                dve.wait_ge(par_t, 1)
                nc.vector.tensor_copy(par[:, KD:P], ps[:, 5, KD:P])
                own.step(nc.vector.tensor_copy(par[:, P:NPAR], ps[:, 6, 0:NPAR - P]))
                own.settle()
                nc.vector.tensor_copy(prm[:, :, 0:4].rearrange("p k f -> p f k"),
                                      par[:, C_CW:NPAR].rearrange("p (f k) -> p f k", f=4))
                nc.vector.tensor_scalar(prm[:, :, 4:6].rearrange("p k f -> p f k"),
                                        par[:, C_GB:C_CW].rearrange("p (f k) -> p f k", f=2),
                                        -1.0, None, ALU.mult).then_inc(par_ready, 1)

            def x_pair(kp):
                dve.wait_ge(xt_full, kp + 1)
                nc.vector.tensor_copy(h[:, 2 * kp:2 * kp + 2, :].rearrange("p k t -> p (k t)"),
                                      ps[:, 4 + kp % 4, :]).then_inc(h_ready, 1)

            for kp in range(HP):
                x_pair(kp)
                unit(F1A + kp)
                input_lo(0, C_F1PRE, kp)
            ffn(0, N_F1, C_F1POST, F1A, F1A_G, F1B, F1B_G)

            next_and_branch_end(MIX, C_F1POST, N_F1OUT, MIX_G - 1, 0.5)
            next_input(N_F1OUT, C_MIXPRE, MIX + RING)

            def pair_qk(grp, par_grp, per=0, i=None):
                group_done(grp, per, i)
                nc.vector.tensor_tensor(qk[:, :, :], banks(par_grp), tile_tokens(r_in, 4), ALU.mult).then_inc(grp_out, 1)

            def pair_vc(grp, par_grp, per=0, i=None):
                group_done(grp, per, i)
                nc.vector.tensor_tensor(vc[:, :, :], banks(par_grp), tile_tokens(r_in, 4), ALU.mult).then_inc(grp_out, 1)

            def pair_vtok(p):
                dve.wait_ge(vt_full, p + 1)
                nc.vector.tensor_copy(vtok[:, :, :, :].rearrange("p a b d -> p (a b d)"), ps[:, B_Y, :]).then_inc(vtok_ready, 1)

            def pair_bc(p, grp, par_grp, per=0, i=None):
                group_done(grp, per, i)
                if i is not None:
                    dve.wait_ge(ycb_done, p)
                nc.vector.tensor_tensor(bc[:, :, :], banks(par_grp), tile_tokens(r_in, 4), ALU.mult).then_inc(grp_out, 1)

            def pair_taps(p):
                dve.wait_ge(z_ready, p + 1)
                dve.wait_ge(prm_set, p + 1)
                for t in range(2):
                    ins = nc.vector.tensor_scalar(yc[:, t, :], zp[:, t, 0:T], prp[:, t, 0:1], prp[:, t, 3:4], ALU.mult, ALU.add)
                own.step(ins)
                own.settle()
                for tap in (1, 2):
                    for t in range(2):
                        ins = nc.vector.scalar_tensor_tensor(out=yc[:, t, :], in0=zp[:, t, tap:tap + T], scalar=prp[:, t, tap:tap + 1],
                                                             in1=yc[:, t, :], op0=ALU.mult, op1=ALU.add)
                    if tap == 1:
                        own.step(ins)
                        own.settle()
                ins.then_inc(taps_done, 1)

            def pair_gates(grp, par_grp, per=0, i=None):
                group_done(grp, per, i)
                nc.vector.tensor_tensor(gat[:, :, :], banks(par_grp), tile_tokens(r_in, 4), ALU.mult).then_inc(grp_out, 1)

            def pair_sigmoid(p, t):
                dve.wait_ge(gat_exp, p + 1)
                own.step(nc.vector.tensor_scalar(gat[:, t, :], gat[:, t, :], 1.0, None, ALU.add))
                own.settle()
                nc.vector.reciprocal(gat[:, t, :], gat[:, t, :]).then_inc(sig_ready, 1)

            def pair_decay(p):
                dve.wait_ge(ncr_landed, p * 16 + 16)
                dve.wait_ge(cq_set, p + 1)
                for hd in range(2):
                    nc.vector.scalar_tensor_tensor(out=ncm[:, hd, 0:P], in0=ncr[:, hd, 0:P], scalar=cq[:, 0, hd:hd + 1],
                                                   in1=mask[:, :], op0=ALU.add, op1=ALU.add)
                    nc.vector.tensor_scalar(ncm[:, hd, P:2 * P], ncr[:, hd, 0:P], cq[:, 1, hd:hd + 1], None, ALU.add)
                    ins = nc.vector.scalar_tensor_tensor(out=ncm[:, hd, 2 * P:3 * P], in0=ncr[:, hd, P:T], scalar=cq[:, 1, hd:hd + 1],
                                                         in1=mask[:, :], op0=ALU.add, op1=ALU.add)
                ins.then_inc(ncm_done, 1)

            def head_logits(p, hd):
                dve.wait_ge(s_full, p * 2 + hd + 1)
                dve.wait_ge(ncm_done, p + 2)
                own.step(nc.vector.scalar_tensor_tensor(out=lg[:, hd, :], in0=ps[:, B_SCORE[hd], 0:3 * P], scalar=SCALE,
                                                        in1=ncm[:, hd, :], op0=ALU.mult, op1=ALU.add))
                own.settle()
                nc.vector.reduce_max(st[:, hd, 0:1], lg[:, hd, 0:P], AX_X)
                own.step(nc.vector.reduce_max(st[:, hd, 1:2], lg[:, hd, P:3 * P], AX_X))
                own.settle()
                nc.vector.tensor_scalar(st[:, hd, 0:2], st[:, hd, 0:2], -1.0, None, ALU.mult).then_inc(l_ready, 1)

            def head_probs(p, hd):
                dve.wait_ge(e_done, p * 2 + hd + 1)
                own.step(nc.vector.reciprocal(st[:, hd, 4:6], st[:, hd, 2:4]))
                own.settle()
                nc.vector.tensor_scalar(lg[:, hd, 0:P], lg[:, hd, 0:P], st[:, hd, 4:5], None, ALU.mult)
                nc.vector.tensor_scalar(lg[:, hd, P:3 * P], lg[:, hd, P:3 * P], st[:, hd, 5:6], None, ALU.mult).then_inc(p_ready, 1)

            def head_pt(p, hd):
                dve.wait_ge(pt_full, p * 2 + hd + 1)
                nc.vector.tensor_copy(pt[:, hd, :], ps[:, B_PT, 0:3 * P]).then_inc(pt_ready, 1)

            def head_merge(p, hd):
                dve.wait_ge(y_full, p * 2 + hd + 1)
                dve.wait_ge(sig_ready, p * 4 + 4)
                dve.wait_ge(m_ready, p * 2 + hd + 1)
                nc.vector.tensor_tensor(mg[:, :], ps[:, B_Y, 0:T], gat[:, hd, :], ALU.mult).then_inc(y_out, 1)
                dve.wait_ge(ymix_ready, p + 1)
                dve.wait_ge(y_out, p * 2 + hd + 1)
                own.step(nc.vector.tensor_tensor(mg[:, :], mg[:, :], yc[:, hd, :], ALU.add))
                own.settle()
                k = bass.ds(p * 2 + hd, 1)
                mgt = mg[:, :].rearrange("p (o t) -> p o t", o=1)
                own.step(nc.vector.tensor_copy(mrg[:, k, 0, :], mgt))
                own.settle()
                nc.vector.tensor_tensor(mrg[:, k, 1, :], mgt, mrg[:, k, 0, :].bitcast(F32), ALU.subtract).then_inc(m_ready, 1)

            for j in range(U1, UM + 2):
                unit(MIX + j)
                if j == 11:
                    mean(N_MIX)
                    spread(N_MIX)
                    pair_qk(MIX_G, MIX_G)
                if j == 21:
                    group_done(MIX_G + 2)
                    own.step(nc.vector.tensor_tensor(fz[:, 0, :], ps[0:H, (MIX_G + 2) % 2 * 2, 0:T], r_in[0:H, :], ALU.mult))
                    own.settle()
                    dve.wait_ge(par_landed, 12 * 16)
                    own.step(nc.vector.tensor_scalar(fz[:, 0, :], fz[:, 0, :], fbias[:, 0:1], None, ALU.add))
                    own.settle()
                    own.step(nc.vector.tensor_scalar(fz[:, 1, :], fz[:, 0, :], -1.0, None, ALU.mult))
                    own.settle()
                    nc.vector.tensor_tensor(fz[:, 1, :], fz[:, 0, :], fz[:, 1, :], ALU.min).then_inc(f_na, 1)
                    nc.vector.tensor_scalar(fz[:, 5, :], fz[:, 0, :], 0.0, None, ALU.min).then_inc(grp_out, 1)
                if j == 23:
                    dve.wait_ge(f_e, 1)
                    nc.vector.tensor_scalar(fz[:, 3, :], fz[:, 2, :], 1.0, None, ALU.add).then_inc(f_y, 1)
                    dve.wait_ge(f_y, 1)
                    nc.vector.scalar_tensor_tensor(out=fz[:, 6, :], in0=fz[:, 3, :], scalar=-1.0, in1=fz[:, 2, :],
                                                   op0=ALU.add, op1=ALU.subtract)
                    own.step(nc.vector.reciprocal(fz[:, 7, :], fz[:, 3, :]))
                    own.settle()
                if j == 25:
                    dve.wait_ge(f_ln, 1)
                    own.step(nc.vector.tensor_tensor(fz[:, 6, :], fz[:, 6, :], fz[:, 7, :], ALU.mult))
                    own.step(nc.vector.tensor_tensor(fz[:, 5, :], fz[:, 5, :], fz[:, 4, :], ALU.subtract))
                    own.settle()
                    nc.vector.tensor_tensor(fz[:, 5, :], fz[:, 5, :], fz[:, 6, :], ALU.add).then_inc(f_log, 1)
                if j == 27:
                    dve.wait_ge(f_tok, 1)
                    nc.vector.tensor_copy(ftok[:, :, :], ps[:, B_S, 0:2 * H].rearrange("p (b h) -> p b h", h=H)).then_inc(f_tokc, 1)
                if j == 19:
                    pair_vc(MIX_G + 1, MIX_G + 1)
                if j == 29:
                    dve.wait_ge(f_cum, 1)
                    nc.vector.tensor_copy(ctok[:, :, :], ps[:, B_PT, 0:2 * H].rearrange("p (b h) -> p b h", h=H))
                    nc.vector.tensor_scalar(fz[:, 7, :], ps[0:H, B_PT, T:2 * T], -1.0, None, ALU.mult).then_inc(f_c, 1)
                if j == 23:
                    pair_vtok(0)
                if j == 29:
                    pair_bc(0, MIX_G + 3, MIX_G + 3)
                if j == 31:
                    pair_taps(0)
            dve.wait_ge(taps_done, 1)

            with dve.Fori(0, PAIRS - 1) as i:
                own.enter(i, 16)
                for j in range(UM):
                    unit(MIX1 + j, UM, i)
                    if j == 3:
                        pair_gates(MIX1_G - 1, MIX1_G - 1, 4, i)
                    if j == 4:
                        pair_decay(i)
                    if j in SIGMOIDS:
                        pair_sigmoid(i, SIGMOIDS.index(j))
                    if j == 6:
                        head_logits(i, 0)
                    if j == 8:
                        head_probs(i, 0)
                    if j == 9:
                        head_logits(i, 1)
                    if j == 11:
                        head_pt(i, 0)
                        pair_qk(MIX1_G, MIX1_G, 4, i)
                    if j == 12:
                        head_probs(i, 1)
                    if j == 14:
                        head_merge(i, 0)
                    if j == 15:
                        head_pt(i, 1)
                    if j == 18:
                        head_merge(i, 1)
                    if j == 19:
                        pair_vc(MIX1_G + 1, MIX1_G + 1, 4, i)
                    if j == 23:
                        pair_vtok(i + 1)
                    if j == 27:
                        pair_bc(i + 1, MIX1_G + 2, MIX1_G + 2, 4, i)
                    if j == 29:
                        pair_taps(i + 1)
            own.leave(PAIRS - 1)

            def memory_lo(j):
                if j in MEM_SPLIT:
                    kp = MEM_SPLIT.index(j)
                    dve.wait_ge(memhi_ready, kp + 1)
                    for t in range(2):
                        k = 2 * kp + t
                        ins = nc.vector.scalar_tensor_tensor(
                            out=mem[:, k, 1, :], in0=ps[:, 5 + kp % 2, t * T:(t + 1) * T], scalar=par[:, C_MKV + k:C_MKV + k + 1],
                            in1=mem[:, k, 0, :].bitcast(F32), op0=ALU.mult, op1=ALU.subtract)
                    ins.then_inc(mem_ready, 1)

            last = PAIRS - 1
            for j in range(G2 * U1):
                unit(WO + j)
                if j == 3:
                    pair_gates(WO_G - 1, WO_G - 1)
                    pair_decay(last)
                if j == 4:
                    head_logits(last, 0)
                if j in SIGMOIDS:
                    pair_sigmoid(last, SIGMOIDS.index(j))
                if j == 6:
                    head_logits(last, 1)
                if j == 7:
                    head_probs(last, 0)
                if j == 8:
                    head_probs(last, 1)
                if j == 9:
                    head_pt(last, 0)
                if j == 11:
                    head_pt(last, 1)
                    head_merge(last, 0)
                if j == 13:
                    head_merge(last, 1)
                if j == 15:
                    dve.wait_ge(msq_done, 2)
                    nc.vector.tensor_scalar(mst[:, 2:4], mst[:, 0:2], 1.0 / D, EPS, ALU.mult, ALU.add).then_inc(mm_ready, 1)
                if j in (16, 18):
                    b = (j - 16) // 2
                    dve.wait_ge(mr_ready, 1)
                    nc.vector.tensor_scalar(memr[:, b, :], memr[:, b, :], mst[:, 4 + b:5 + b], None, ALU.mult).then_inc(memn_ready, 1)
                memory_lo(j)
                for m, after in enumerate((17, 19, 27)):
                    if j == after:
                        branch_tiles(C_MIXPOST, N_MIXOUT, WO_G + m, m)

            next_and_branch_end(MK, C_MIXPOST, N_MIXOUT, MK_G - 1)
            next_input(N_MIXOUT, C_MQPRE, MK + RING, HP)
            group_done(MK_G)
            nc.vector.tensor_copy(kt[:, :, :], banks(MK_G)).then_inc(grp_out, 1)
            for j in range(RING, U1):
                unit(MQ + j)

            def memory_max(hd):
                dve.wait_ge(ms_full, hd + 1)
                own.step(nc.vector.reduce_max(mmx[:, hd, 0:2], ps[:, 4 + hd, :].rearrange("p (b k) -> p b k", b=2), AX_X))
                own.settle()
                nc.vector.tensor_scalar(mmx[:, hd, 0:2], mmx[:, hd, 0:2], -SCALE, None, ALU.mult).then_inc(mmax_ready, 1)

            def memory_probs(hd):
                dve.wait_ge(mexp_done, hd + 1)
                own.step(nc.vector.reciprocal(mmx[:, hd, 4:6], mmx[:, hd, 2:4]))
                own.settle()
                for b in range(2):
                    ins = nc.vector.tensor_scalar(ml[:, hd, b, :], ml[:, hd, b, :], mmx[:, hd, 4 + b:5 + b], None, ALU.mult)
                ins.then_inc(mp_ready, 1)

            def memory_pt(hd):
                dve.wait_ge(mpt_full, hd + 1)
                nc.vector.tensor_copy(mpt[:, hd, :, :].rearrange("p b t -> p (b t)"), ps[:, 4 + hd, :]).then_inc(mpt_ready, 1)

            def split_output(hd):
                dve.wait_ge(oshi_ready, hd + 1)
                nc.vector.tensor_tensor(osp[:, hd, 1, :], ps[:, 4 + hd, 0:T], osp[:, hd, 0, :].bitcast(F32), ALU.subtract).then_inc(os_ready, 1)

            for j in range(U1 + RING):
                if j == U1 + RING - 1:
                    group_done(MV_G)
                    nc.vector.tensor_copy(mvtok[:, :, 1, :], memory_block(1)).then_inc(grp_out, 1)
                    split_output(0)
                    split_output(1)
                unit(MV + j)
                if j == 0:
                    mean(N_MQ)
                    spread(N_MQ)
                if j == 3:
                    group_done(MQ_G)
                    nc.vector.tensor_tensor(qt[:, :, :], banks(MQ_G), tile_tokens(r_in, MH), ALU.mult).then_inc(grp_out, 1)
                for step, first in ((memory_max, 5), (memory_probs, 7), (memory_pt, 8)):
                    if first <= j < first + 2:
                        step(2 * (j - first))
                        step(2 * (j - first) + 1)
            split_output(2)
            split_output(3)
            for j in range(RING, G2 * UO):
                unit(MO + j)
                if j % 2 == 1:
                    branch_tiles(C_MPOST, N_MOUT, MO_G + (j - 5) // 2, (j - 5) // 2)
            branch_tiles(C_MPOST, N_MOUT, MO_G + 2, 2)
            next_and_branch_end(F2A, C_MPOST, N_MOUT, F2A_G - 1)
            next_input(N_MOUT, C_F2PRE, F2A + RING)
            ffn(1, N_F2, C_F2POST, F2A, F2A_G, F2B, F2B_G)

            branch_end(C_F2POST, N_F2OUT, F2B_G + G2 - 1, 0.5)
            dve.wait_ge(r_ready, N_F2OUT + 1)
            dve.wait_ge(ht_ready, 8)
            for c in range(8):
                dve.wait_ge(ot_full, c + 1)
                nc.vector.scalar_tensor_tensor(out=ot[:, c, :], in0=ps[:, OUT_BANKS[c], :], scalar=rtok[:, c % 2:c % 2 + 1],
                                               in1=ht[:, c, :], op0=ALU.mult, op1=ALU.add).then_inc(ot_ready, 1)

        @block.gpsimd
        def _(pool):
            own = Chain(pool, pool_own)
            own.step(nc.gpsimd.memset(ident[:, :], 0.0))
            own.step(nc.gpsimd.memset(mask[:, :], 0.0))
            own.settle()
            nc.gpsimd.affine_select(out=ident[:, :], in_=ident[:, :], compare_op=ALU.not_equal, fill=1.0, base=0,
                                    pattern=[[-1, P]], channel_multiplier=1).then_inc(ident_set, 1)
            nc.gpsimd.affine_select(out=mask[:, :], in_=mask[:, :], compare_op=ALU.is_ge, fill=NEG, base=0,
                                    pattern=[[-1, P]], channel_multiplier=1)
            pool.wait_ge(consts_set, 2)
            nc.gpsimd.affine_select(out=tri1[:, 0:P], in_=tri1[:, 0:P], compare_op=ALU.is_ge, fill=0.0, base=0,
                                    pattern=[[1, P]], channel_multiplier=-1).then_inc(ident_set, 1)

            rows = [(n, "o (k p) -> (o k) p") for n in (
                "ffn1_post_g", "mix_pre_g", "mix_post_g", "mem_q_pre_g", "mem_kv_g",
                "mem_post_g", "ffn2_pre_g", "ffn2_post_g")]
            rows += [("gate_bias", "o b (k p) -> (o b k) p"), ("conv_w", "o b (k p) -> (o b k) p"),
                     ("conv_b", "o (k p) -> (o k) p")]
            r = KD
            for name, how in rows:
                src = a[name].rearrange(how, p=P)
                n = src.shape[0]
                pool.dma_start(prow[r % P:r % P + n, r // P, :], src).then_inc(par_landed, 16)
                r += n
            pool.dma_start(fbias[:, :], a["forget_bias"].rearrange("o h -> h o")).then_inc(par_landed, 16)

            def add_squares(norm, kp):
                pool.wait_ge(sq_ready, norm * HP + kp + 1)
                if kp > 1:
                    pool.wait_ge(sq_added, added(norm, kp))
                nc.gpsimd.tensor_tensor(sqsum[:, :], sqsum[:, :], sq[:, kp % 2, :], ALU.add).then_inc(sq_added, 1)

            def inverse_rms(norm):
                pool.wait_ge(ms_ready, norm + 1)
                nc.gpsimd.tensor_tensor(rtok[:, :], ms[:, :], mhalf[:, :], ALU.pow).then_inc(r_ready, 1)

            def update(n, kp):
                pool.wait_ge(t_ready, n * (HP - 1) + kp)
                if kp == 1:
                    pool.wait_ge(h_ready, (n + 1) * HP + 1)
                nc.gpsimd.tensor_tensor(h[:, 2 * kp:2 * kp + 2, :], h[:, 2 * kp:2 * kp + 2, :],
                                        f[:, 2 * kp:2 * kp + 2, :], ALU.add).then_inc(h_ready, 1)

            def branch_and_input(n, norm):
                for kp in range(1, HP - 2):
                    add_squares(norm, kp)
                inverse_rms(norm)
                if norm < N_F2OUT:
                    for kp in range(HP):
                        if kp + 1 < HP:
                            update(n, kp + 1)
                        if kp > 0:
                            add_squares(norm + 1, kp)
                    inverse_rms(norm + 1)

            for kp in range(1, HP):
                add_squares(N_F1, kp)
            inverse_rms(N_F1)
            branch_and_input(0, N_F1OUT)

            def pair_conv(p, grp_done):
                grp_done()
                if not isinstance(p, int):
                    pool.wait_ge(taps_done, p)
                nc.gpsimd.tensor_tensor(zp[:, :, 2:T + 2], bc[:, 2:4, :], vc[:, 2:4, :], ALU.mult).then_inc(z_ready, 1)
                pool.wait_ge(taps_done, p + 1)
                nc.gpsimd.tensor_tensor(yc[:, :, :], yc[:, :, :], bc[:, 0:2, :], ALU.mult).then_inc(ycb_done, 1)

            def pair_conv_gate(p):
                pool.wait_ge(sig_ready, p * 4 + 4)
                pool.wait_ge(ycb_done, p + 1)
                nc.gpsimd.tensor_tensor(yc[:, :, :], yc[:, :, :], gat[:, 2:4, :], ALU.mult).then_inc(ymix_ready, 1)

            own.step(nc.gpsimd.memset(zp[:, :, 0:2], 0.0))
            own.settle()
            pair_conv(0, lambda: pool.wait_ge(grp_out, MIX_G + 4))
            with pool.Fori(0, PAIRS - 1) as i:
                pair_conv_gate(i)
                pair_conv(i + 1, lambda: pool.wait_ge(grp_out, i * 4 + MIX1_G + 3))
            pair_conv_gate(PAIRS - 1)

            pool.wait_ge(mm_ready, 1)
            nc.gpsimd.tensor_tensor(mst[:, 4:6], mst[:, 2:4], mhalf[:, 0:2], ALU.pow).then_inc(mr_ready, 1)
            branch_and_input(1, N_MIXOUT)
            branch_and_input(2, N_MOUT)
            branch_and_input(3, N_F2OUT)

        @block.tensor
        def _(pe):
            def product(n0, grp, x, k0, first=False, last=False, ready=None, per=0, i=None, grp_per=0, ready0=None,
                        wide=False):
                s = slot_of(n0)
                pe.wait_ge(lo_done, of(n0 + 1, per, i))
                if ready is not None:
                    pe.wait_ge(*(ready0 or ready))
                if first and grp >= 2:
                    pe.wait_ge(grp_out, of(grp - 1, grp_per, i))
                for kk in range(UK):
                    if kk == 1 and ready0 is not None:
                        pe.wait_ge(*ready)
                    for m in range(GT):
                        c = (kk * GT + m) * P
                        hi, lo = w_hi[:, s, c:c + P], w_lo[:, s, c:c + P]
                        if wide:
                            o = wide_banks(grp)[:, m, :]
                            nc.tensor.matmul(o, hi, x[:, k0 + kk, :, :].rearrange("p s t -> p (s t)"),
                                             start=first and kk == 0, stop=False, skip_group_check=True)
                            ins = nc.tensor.matmul(o[:, 0:T], lo, x[:, k0 + kk, 0, :], start=False,
                                                   stop=last and kk == UK - 1, skip_group_check=True)
                            continue
                        o = ps[:, grp % 2 * 2 + m // 2, m % 2 * T:m % 2 * T + T]
                        nc.tensor.matmul(o, hi, x[:, k0 + kk, 0, :], start=first and kk == 0 and m % 2 == 0,
                                         stop=False, skip_group_check=True)
                        nc.tensor.matmul(o, hi, x[:, k0 + kk, 1, :], start=False, stop=False, skip_group_check=True)
                        ins = nc.tensor.matmul(o, lo, x[:, k0 + kk, 0, :], start=False,
                                               stop=last and kk == UK - 1, skip_group_check=True)
                return ins

            def unit(n0, grp, x, k0, units=U1, ready=None, per=0, i=None, grp_per=0, ready0=None, wide=False):
                last = k0 == UK * (units - 1)
                ins = product(n0, grp, x, k0, k0 == 0, last, ready, per, i, grp_per, ready0, wide)
                ins.then_inc(w_used, 1)

            def sums(norm):
                pe.wait_ge(sq_added, added(norm, HP))
                if norm > 0:
                    pe.wait_ge(r_set, norm)
                for t in range(2):
                    for b in range(2):
                        c = t * T + b * P
                        ins = nc.tensor.matmul(ps[:, B_NORM, b:b + 1], sqsum[:, c:c + P], ones[:, 0:1],
                                               start=t == 0 and b == 0, stop=t == 1, skip_group_check=True)
                ins.then_inc(sum_full, 1)

            def branch_sums(norm, between=None):
                pe.wait_ge(sq_added, added(norm, HP - 2))
                pe.wait_ge(r_set, norm)
                for t in range(2):
                    for b in range(2):
                        c = t * T + b * P
                        nc.tensor.matmul(ps[:, B_NORM, b:b + 1], sqsum[:, c:c + P], ones[:, 0:1],
                                         start=t == 0 and b == 0, stop=False, skip_group_check=True)
                if between is not None:
                    between()
                pe.wait_ge(sq_folded, (norm + 1) // 2)
                for b in range(2):
                    ins = nc.tensor.matmul(ps[:, B_NORM, b:b + 1], sq[:, 0, b * P:(b + 1) * P], ones[:, 0:1],
                                           start=False, stop=True, skip_group_check=True)
                ins.then_inc(sum_full, 1)

            def spread(norm):
                pe.wait_ge(diag_ready, norm + 1)
                for b in range(2):
                    ins = nc.tensor.matmul(ps[:, B_NORM, T + b * P:T + (b + 1) * P], ones, diag[:, b, :],
                                           start=True, stop=True)
                ins.then_inc(r_full, 1)

            def transpose_chunk(src, c, bank, done):
                b, q = c % 2, c // 2
                for t in range(4):
                    ins = nc.tensor.transpose(ps[:, bank, t * P:(t + 1) * P], src[:, 4 * q + t, b * P:(b + 1) * P], ident[:, :])
                ins.then_inc(done, 1)

            def transpose_x(kp):
                if kp % 2 == 0:
                    pe.wait_ge(x_landed[kp // 2], 16)
                if kp >= 4:
                    pe.wait_ge(h_ready, kp - 3)
                for t in range(2):
                    for b in range(2):
                        k = 2 * kp + t
                        ins = nc.tensor.transpose(ps[:, 4 + kp % 4, (t * 2 + b) * P:(t * 2 + b + 1) * P],
                                                  xr[:, b, k * P:(k + 1) * P], ident[:, :])
                ins.then_inc(xt_full, 1)

            def ffn(k, base, norm, n13, grp13, n2, grp2):
                for b in range(2):
                    for u in range(U1):
                        if k == 0 and b == 0 and u + 1 < HP:
                            transpose_x(u + 1)
                        unit(n13 + b * U1 + u, grp13 + b, xs, UK * u, ready=(x_ready, base + u + 1) if b == 0 else None,
                             ready0=(x0_ready, 3) if k == 1 and b + u == 0 else None)
                        if b == 1 and u == 0:
                            sums(norm)
                        if b == 1 and u == 1:
                            spread(norm)
                        if b == 1 and u == 3 and k == 0:
                            pe.wait_ge(par_landed, 12 * 16)
                            pe.wait_ge(h_ready, HP)
                            nc.tensor.transpose(ps[:, 5, 0:P], prow[:, 0, :], ident[:, :])
                            nc.tensor.transpose(ps[:, 6, 0:NPAR - P], prow[0:NPAR - P, 1, :],
                                                ident[0:NPAR - P, 0:NPAR - P]).then_inc(par_t, 1)
                with pe.Fori(0, (G1 - 2) // 2) as i:
                    for b in range(2):
                        for u in range(U1):
                            unit(n13 + (2 + b) * U1 + u, grp13 + 2 + b, xs, UK * u, per=2 * U1, i=i, grp_per=2,
                                 wide=True)
                if k == 1:
                    for c in range(8):
                        if c >= 4:
                            pe.wait_ge(ht_ready, c - 3)
                        transpose_chunk(h, c, 4 + c % 4, ht_full)
                    pe.wait_ge(ht_ready, 8)
                with pe.Fori(0, G2 // 2) as i:
                    for b in range(2):
                        for u in range(U2):
                            unit(n2 + b * U2 + u, grp2 + b, g, UK * u, U2, (g_ready, k * G1 + u + 1) if b == 0 else None,
                                 2 * U2, i, 2, wide=b == 0)

            pe.wait_ge(ident_set, 2)
            pe.wait_ge(gain_landed, 16)
            nc.tensor.transpose(ps[:, 2, 0:KD], prow[0:KD, 0, :], ident[0:KD, 0:KD]).then_inc(gain_t, 1)
            transpose_x(0)
            ffn(0, 0, N_F1, F1A, F1A_G, F1B, F1B_G)
            branch_sums(N_F1OUT)
            spread(N_F1OUT)

            def head_scores(hd):
                q, k = qk[:, hd, :], qk[:, 2 + hd, :]
                bank = B_SCORE[hd]
                nc.tensor.matmul(ps[:, bank, 0:P], q[:, 0:P], k[:, 0:P], start=True, stop=True)
                nc.tensor.matmul(ps[:, bank, P:3 * P], q[:, P:T], k, start=True, stop=True).then_inc(s_full, 1)

            def head_transpose(p, hd):
                pe.wait_ge(p_ready, p * 2 + hd + 1)
                if hd == 1:
                    pe.wait_ge(pt_ready, p * 2 + 1)
                for b in range(3):
                    ins = nc.tensor.transpose(ps[:, B_PT, b * P:(b + 1) * P], lg[:, hd, b * P:(b + 1) * P], ident[:, :])
                ins.then_inc(pt_full, 1)

            def head_values(p, hd):
                pe.wait_ge(pt_ready, p * 2 + hd + 1)
                if hd == 0:
                    pe.wait_ge(vtok_ready, p + 1)
                else:
                    pe.wait_ge(y_out, p * 2 + 1)
                nc.tensor.matmul(ps[:, B_Y, 0:T], vtok[:, hd, 0, :], pt[:, hd, 0:2 * P], start=True, stop=False, skip_group_check=True)
                nc.tensor.matmul(ps[:, B_Y, P:T], vtok[:, hd, 1, :], pt[:, hd, 2 * P:3 * P], start=False, stop=True,
                                 skip_group_check=True).then_inc(y_full, 1)

            def pair_values(grp_done):
                grp_done()
                for hd in range(2):
                    for b in range(2):
                        ins = nc.tensor.transpose(ps[:, B_Y, (hd * 2 + b) * P:(hd * 2 + b + 1) * P],
                                                  vc[:, hd, b * P:(b + 1) * P], ident[:, :])
                ins.then_inc(vt_full, 1)

            for j in range(UM + 2):
                if j < U1:
                    unit(MIX + j, MIX_G, xs, UK * j, ready=(x_ready, HP + j + 1), ready0=(x0_ready, 1) if j == 0 else None)
                elif 2 * U1 <= j < 2 * U1 + 2:
                    fu, s = j - 2 * U1, slot_of(MIX + j)
                    pe.wait_ge(lo_done, MIX + j + 1)
                    if fu == 0:
                        pe.wait_ge(grp_out, MIX_G + 1)
                    o = ps[:, (MIX_G + 2) % 2 * 2, 0:T]
                    for kk in range(8):
                        k = fu * 8 + kk
                        hi, lo = w_hi[:, s, kk * P:(kk + 1) * P], w_lo[:, s, kk * P:(kk + 1) * P]
                        nc.tensor.matmul(o, hi, xs[:, k, 0, :], start=k == 0, stop=False, skip_group_check=True)
                        nc.tensor.matmul(o, hi, xs[:, k, 1, :], start=False, stop=False, skip_group_check=True)
                        ins = nc.tensor.matmul(o, lo, xs[:, k, 0, :], start=False, stop=k == KD - 1, skip_group_check=True)
                    ins.then_inc(w_used, 1)
                else:
                    b = j // U1 if j < 2 * U1 else (j - 2) // U1 + 1
                    unit(MIX + j, MIX_G + b, xs, UK * ((j if b < 2 else j - 2) % U1))
                if j == 8:
                    sums(N_MIX)
                if j == 9:
                    spread(N_MIX)
                if j == 23:
                    pe.wait_ge(f_log, 1)
                    for b in range(2):
                        ins = nc.tensor.matmul(ps[:, B_S, b * H:(b + 1) * H], fz[:, 5, b * P:(b + 1) * P],
                                               ident[0:H, 0:H], start=True, stop=True)
                    ins.then_inc(f_tok, 1)
                if j == 25:
                    pe.wait_ge(f_tokc, 1)
                    nc.tensor.matmul(ps[:, B_PT, 0:H], tri1[:, 0:P], ftok[:, 0, :], start=True, stop=True)
                    nc.tensor.matmul(ps[:, B_PT, H:2 * H], ones, ftok[:, 0, :], start=True, stop=False)
                    nc.tensor.matmul(ps[:, B_PT, H:2 * H], tri1[:, 0:P], ftok[:, 1, :], start=False, stop=True)
                    nc.tensor.matmul(ps[0:H, B_PT, T:2 * T], ftok[:, 0, :], tri1[:, :], start=True, stop=False, skip_group_check=True)
                    nc.tensor.matmul(ps[0:H, B_PT, T + P:2 * T], ftok[:, 1, :], tri1[:, 0:P], start=False, stop=True,
                                     skip_group_check=True).then_inc(f_cum, 1)
                if j == 19:
                    pair_values(lambda: pe.wait_ge(grp_out, MIX_G + 2))

            with pe.Fori(0, PAIRS - 1) as i:
                for j in range(UM):
                    unit(MIX1 + j, MIX1_G + j // U1, xs, UK * (j % U1), per=UM, i=i, grp_per=4)
                    if j == 1:
                        head_scores(0)
                    if j == 3:
                        head_scores(1)
                    if j == 6:
                        head_transpose(i, 0)
                    if j == 9:
                        head_values(i, 0)
                    if j == 10:
                        head_transpose(i, 1)
                    if j == 13:
                        head_values(i, 1)
                    if j == 19:
                        pe.wait_ge(y_out, i * 2 + 2)
                        pair_values(lambda: pe.wait_ge(grp_out, i * 4 + MIX1_G + 2))

            last = PAIRS - 1
            for j, (m, u) in enumerate(WO_ORDER):
                unit(WO + j, WO_G + m, mrg, UK * u, ready=(m_ready, 2 * u + 3) if m == 0 else None)
                if j == 0:
                    head_scores(0)
                    head_scores(1)
                if j == 5:
                    head_transpose(last, 0)
                if j == 7:
                    head_values(last, 0)
                    head_transpose(last, 1)
                if j == 9:
                    head_values(last, 1)
                if j in MEM_T:
                    kp = MEM_T.index(j)
                    pe.wait_ge(memn_ready, 2)
                    if kp >= 2:
                        pe.wait_ge(mem_ready, kp - 1)
                    for t in range(2):
                        for b in range(2):
                            k = 2 * kp + t
                            ins = nc.tensor.transpose(ps[:, 5 + kp % 2, (t * 2 + b) * P:(t * 2 + b + 1) * P],
                                                      memr[:, b, k * P:(k + 1) * P], ident[:, :])
                    ins.then_inc(memt_full, 1)

            for u in range(U1):
                unit(MK + u, MK_G, mem, UK * u, ready=(mem_ready, u + 1))
                if u == 1:
                    branch_sums(N_MIXOUT)
                if u == 2:
                    spread(N_MIXOUT)
            for u in range(U1):
                unit(MQ + u, MQ_G, xs, UK * u, ready=(x_ready, 2 * HP + u + 1))
                if u == 4:
                    sums(N_MQ)
                if u == 5:
                    spread(N_MQ)

            def memory_transpose(hd):
                pe.wait_ge(mp_ready, hd + 1)
                for kb in range(2):
                    for b in range(2):
                        ins = nc.tensor.transpose(ps[:, 4 + hd, (kb * 2 + b) * P:(kb * 2 + b + 1) * P],
                                                  ml[:, hd, b, kb * P:(kb + 1) * P], ident[:, :])
                ins.then_inc(mpt_full, 1)

            def memory_values(hd):
                pe.wait_ge(mpt_ready, hd + 1)
                for kb in range(2):
                    ins = nc.tensor.matmul(ps[:, 4 + hd, 0:T], mvtok[:, hd, kb, :], mpt[:, hd, kb, :], start=kb == 0, stop=kb == 1)
                ins.then_inc(mo_full, 1)

            for u in range(U1):
                s = slot_of(MV + u)
                pe.wait_ge(lo_done, MV + u + 1)
                if u == 0:
                    pe.wait_ge(grp_out, MV_G - 1)
                for kk in range(UK):
                    k = UK * u + kk
                    hi, lo = (w[:, s, kk * 512:(kk + 1) * 512] for w in (w_hi, w_lo))
                    for b in range(2):
                        o = ps[:, MV_G % 2 * 2 + b, :]
                        m_hi, m_lo = (mem[:, k, part, b * P:(b + 1) * P] for part in range(2))
                        nc.tensor.matmul(o, m_hi, hi, start=k == 0, stop=False)
                        nc.tensor.matmul(o, m_hi, lo, start=False, stop=False)
                        ins = nc.tensor.matmul(o, m_lo, hi, start=False, stop=k == KD - 1)
                ins.then_inc(w_used, 1)
                if u == 1:
                    pe.wait_ge(grp_out, MQ_G + 1)
                    for hd in range(MH):
                        for b in range(2):
                            ins = nc.tensor.matmul(ps[:, 4 + hd, b * T:(b + 1) * T], qt[:, hd, b * P:(b + 1) * P], kt[:, hd, :],
                                                   start=True, stop=True)
                        ins.then_inc(ms_full, 1)
                if u in (4, 5):
                    memory_transpose(2 * (u - 4))
                    memory_transpose(2 * (u - 4) + 1)
            pe.wait_ge(grp_out, MV_G + 1)
            pe.wait_ge(mv_out, 1)
            for j in range(G2 * UO):
                u = j % UO
                if j < UO:
                    memory_values(2 * j)
                    memory_values(2 * j + 1)
                unit(MO + j, MO_G + j // UO, osp, UK * u, UO, ready=(os_ready, 2 * u + 2) if j < UO else None,
                     ready0=(os_ready, 2 * u + 1) if j < UO else None)
            branch_sums(N_MOUT)
            spread(N_MOUT)

            ffn(1, 3 * HP, N_F2, F2A, F2A_G, F2B, F2B_G)

            def out_block(c):
                transpose_chunk(f, c, OUT_BANKS[c], ot_full)

            pe.wait_ge(grp_out, F2B_G + G2 - 1)
            branch_sums(N_F2OUT, lambda: out_block(0))
            for c in range(1, 5):
                out_block(c)
            pe.wait_ge(ms_ready, N_F2OUT + 1)
            out_block(5)
            pe.wait_ge(grp_out, F2B_G + G2)
            out_block(6)
            out_block(7)


_INS = ["x", "mem", "ffn1_pre_g", "ffn1_w13", "ffn1_w2", "ffn1_post_g", "mix_pre_g", "w_in", "forget_bias",
        "gate_bias", "conv_w", "conv_b", "w_out", "mix_post_g", "mem_q_pre_g", "mem_kv_g", "w_mq", "w_mkv",
        "w_mo", "mem_post_g", "ffn2_pre_g", "ffn2_w13", "ffn2_w2", "ffn2_post_g"]


def kernel(**inputs):
    import numpy as np
    import concourse.bacc as bacc
    from concourse.bass_utils import run_bass_kernel_spmd

    nc = bacc.Bacc("TRN2", target_bir_lowering=False, num_devices=1)
    arrays, aps = {}, {}
    for name in _INS:
        arrays[f"in_{name}"] = np.ascontiguousarray(inputs[name])
        aps[name] = nc.dram_tensor(f"in_{name}", arrays[f"in_{name}"].shape, F32, kind="ExternalInput").ap()
    out = nc.dram_tensor("out", (1, T, D), F32, kind="ExternalOutput").ap()
    build(nc, aps, out)
    return run_bass_kernel_spmd(nc, [arrays], core_ids=[0]).results[0]["out"]
```
